# Optimizing a Trainium2 kernel written in Bass

```python
import math
import jax
import jax.numpy as jnp
from jax import lax
import numpy as np

D_MODEL = 1024
BATCH = 1
SEQ = 2048
DEPTH = 2
DEC_BATCH = 8
DEC_SEQ = 4
PAST_LEN = 4096
PAGE_SIZE = 128

HEAD_DIM = 128
H_A = 4
H_B = 4
H_C = 4
H_D = 4
W_A = H_A * HEAD_DIM
W_B = H_B * HEAD_DIM
W_C = H_C * HEAD_DIM
W_D = H_D * HEAD_DIM
CONV_W = 4
CHUNK = 64
Q_BLOCK = 128
D_BRANCHES = ((128, 1), (512, 4), (2048, 16))
D_WIN_MAX = 2048
RET_DECAY_EXP0 = 5.0
ALIBI_MAX_BIAS = 8.0
FORGET_BIAS_INIT = 3.0
EPS = 1e-6
N_EVEN = (DEPTH + 1) // 2
N_ODD = DEPTH // 2
EVEN_SPLITS = (W_A, W_A, W_A, W_A, H_A, H_A, W_B, W_B, W_B, W_B)
ODD_SPLITS = (W_C, W_C, W_C, W_C, H_C, W_D, W_D, W_D, W_D)
EVEN_IN = 4 * W_A + 2 * H_A + 4 * W_B
ODD_IN = 4 * W_C + H_C + 4 * W_D

kernel_name = 'hybrid_deltanet_retention_fox_dilated_step'

F32 = jnp.float32

def rms_norm(x, g):
    xf = x.astype(F32)
    y = xf * lax.rsqrt(jnp.mean(xf * xf, -1, keepdims=True) + EPS)
    return y.astype(x.dtype) * g

def l2_norm(x):
    xf = x.astype(F32)
    return (xf * lax.rsqrt(jnp.sum(xf * xf, -1, keepdims=True) + EPS)).astype(x.dtype)

def group_norm(o, g):
    b, l, h, d = o.shape
    of = o.astype(F32)
    mu = of.mean(-1, keepdims=True)
    var = jnp.mean(jnp.square(of - mu), -1, keepdims=True)
    return ((of - mu) * lax.rsqrt(var + EPS)).reshape(b, l, h * d).astype(o.dtype) * g

def split_cols(t, sizes):
    return jnp.split(t, np.cumsum(sizes)[:-1].tolist(), axis=-1)

def heads(t, n_heads):
    return t.reshape(t.shape[:-1] + (n_heads, HEAD_DIM))

def to_chunks(t, n, c):
    t = t.reshape((t.shape[0], n, c) + t.shape[2:])
    return jnp.moveaxis(t, (1, 3), (0, 2))

def from_chunks(t):
    t = jnp.moveaxis(t, (0, 2), (1, 3))
    return t.reshape((t.shape[0], t.shape[1] * t.shape[2]) + t.shape[3:])

def retention_log_decay():
    return jnp.log1p(-jnp.exp2(-RET_DECAY_EXP0 - jnp.arange(H_B, dtype=F32)))

def alibi_slopes():
    return jnp.exp2(-ALIBI_MAX_BIAS * jnp.arange(1, H_D + 1, dtype=F32) / H_D)

def causal_conv(x, buf, w):
    L = x.shape[1]
    xp = jnp.concatenate([buf.astype(x.dtype), x], axis=1)
    y = xp[:, 0:L] * w[0]
    for j in range(1, CONV_W):
        y = y + xp[:, j:j + L] * w[j]
    return y, xp[:, -(CONV_W - 1):]

def gated_delta_chunked(q, k, v, g, beta, s0):
    out_dtype = v.dtype
    b, L, h, dk = q.shape
    dv = v.shape[-1]
    c = math.gcd(CHUNK, L)
    n = L // c
    qc, kc, vc = (to_chunks(t.astype(F32), n, c) for t in (q, k, v))
    gc = to_chunks(g.astype(F32), n, c)
    bc = to_chunks(beta.astype(F32), n, c)
    G = jnp.cumsum(gc, axis=-1)
    idx = jnp.arange(c)
    incl = idx[:, None] >= idx[None, :]
    strict = idx[:, None] > idx[None, :]
    decay_mat = jnp.exp(jnp.where(incl, G[..., :, None] - G[..., None, :], -jnp.inf))
    kk = jnp.einsum('nbhid,nbhjd->nbhij', kc, kc)
    a_mat = jnp.where(strict, bc[..., :, None] * kk * decay_mat, 0.0)
    lhs = jnp.eye(c, dtype=F32) + a_mat
    rhs = jnp.concatenate([bc[..., None] * vc, (bc * jnp.exp(G))[..., None] * kc], axis=-1)
    sol = lax.linalg.triangular_solve(lhs, rhs, left_side=True, lower=True, unit_diagonal=True)
    w_v, w_k = sol[..., :dv], sol[..., dv:]
    qk = jnp.einsum('nbhid,nbhjd->nbhij', qc, kc) * decay_mat
    q_dec = qc * jnp.exp(G)[..., None]
    k_tail = kc * jnp.exp(G[..., -1:] - G)[..., None]
    g_last = jnp.exp(G[..., -1])

    def step(S, xs):
        w_v_i, w_k_i, qk_i, q_dec_i, k_tail_i, g_last_i = xs
        u = w_v_i - jnp.einsum('bhik,bhkv->bhiv', w_k_i, S)
        o = jnp.einsum('bhik,bhkv->bhiv', q_dec_i, S) + jnp.einsum('bhij,bhjv->bhiv', qk_i, u)
        S = g_last_i[..., None, None] * S + jnp.einsum('bhik,bhiv->bhkv', k_tail_i, u)
        return S, o

    s_fin, o = lax.scan(step, s0.astype(F32), (w_v, w_k, qk, q_dec, k_tail, g_last))
    return from_chunks(o).astype(out_dtype), s_fin.astype(s0.dtype)

def retention_chunked(q, k, v, r0):
    out_dtype = v.dtype
    b, L, h, d = q.shape
    c = math.gcd(CHUNK, L)
    n = L // c
    lg = retention_log_decay()
    qc, kc, vc = (to_chunks(t.astype(F32), n, c) for t in (q, k, v))
    pos = jnp.arange(c, dtype=F32)
    causal = pos[:, None] >= pos[None, :]
    dmat = jnp.exp(jnp.where(causal, (pos[:, None] - pos[None, :]) * lg[:, None, None], -jnp.inf))
    o_inner = jnp.einsum('nbhij,nbhjd->nbhid', jnp.einsum('nbhid,nbhjd->nbhij', qc, kc) * dmat, vc)
    qd = qc * jnp.exp((pos + 1.0)[None, :] * lg[:, None])[:, :, None]
    kd = kc * jnp.exp((c - 1.0 - pos)[None, :] * lg[:, None])[:, :, None]
    g_c = jnp.exp(c * lg)

    def step(R, xs):
        qd_i, kd_i, v_i = xs
        o = jnp.einsum('bhik,bhkv->bhiv', qd_i, R)
        R = g_c[:, None, None] * R + jnp.einsum('bhik,bhiv->bhkv', kd_i, v_i)
        return R, o

    r_fin, o_cross = lax.scan(step, r0.astype(F32), (qd, kd, vc))
    return from_chunks(o_inner + o_cross).astype(out_dtype), r_fin.astype(r0.dtype)

def fox_attend(q, Fq, qpos, k, v, Fk, kpos):
    b, nq, h, d = q.shape
    FkT = jnp.swapaxes(Fk, 1, 2)

    def block(args):
        qb, Fqb, qpb = args
        s = jnp.einsum('bqhd,bkhd->bhqk', qb, k).astype(F32)
        s = s + jnp.swapaxes(Fqb, 1, 2)[..., :, None] - FkT[..., None, :]
        s = jnp.where(kpos[None, :] <= qpb[:, None], s, -jnp.inf)
        p = jax.nn.softmax(s, axis=-1)
        return jnp.einsum('bhqk,bkhd->bqhd', p.astype(v.dtype), v)

    if nq <= Q_BLOCK:
        return block((q, Fq, qpos))
    nb = -(-nq // Q_BLOCK)
    pad = nb * Q_BLOCK - nq
    qp = jnp.pad(q, ((0, 0), (0, pad), (0, 0), (0, 0))).reshape(b, nb, Q_BLOCK, h, d)
    Fp = jnp.pad(Fq, ((0, 0), (0, pad), (0, 0))).reshape(b, nb, Q_BLOCK, h)
    pp = jnp.pad(qpos, (0, pad), mode='edge').reshape(nb, Q_BLOCK)
    o = lax.map(block, (jnp.swapaxes(qp, 0, 1), jnp.swapaxes(Fp, 0, 1), pp))
    return jnp.swapaxes(o, 0, 1).reshape(b, nb * Q_BLOCK, h, d)[:, :nq]

def band_branch(q, k, v, slopes, dil, span):
    b, S, h, d = q.shape
    Ls = S // dil
    nb = -(-Ls // span)
    Lp = nb * span
    bb = b * dil

    def sub(t):
        t = t.reshape(b, Ls, dil, h, d)
        t = jnp.swapaxes(t, 1, 2).reshape(bb, Ls, h, d)
        return jnp.pad(t, ((0, 0), (0, Lp - Ls), (0, 0), (0, 0))).reshape(bb, nb, span, h, d)

    qb, kb, vb = sub(q), sub(k), sub(v)
    shift = ((0, 0), (1, 0), (0, 0), (0, 0), (0, 0))
    kext = jnp.concatenate([jnp.pad(kb, shift)[:, :-1], kb], axis=2)
    vext = jnp.concatenate([jnp.pad(vb, shift)[:, :-1], vb], axis=2)
    r = jnp.arange(span)
    cidx = jnp.arange(2 * span)
    dist = span + r[:, None] - cidx[None, :]
    first = (jnp.arange(nb) == 0)[:, None, None]
    valid = (dist >= 0) & (dist <= span) & ~(first & (cidx < span)[None, None, :])
    s = jnp.einsum('bnqhd,bnkhd->bnhqk', qb, kext).astype(F32)
    s = s - slopes[:, None, None] * (dil * dist).astype(F32)
    s = jnp.where(valid[:, None], s, -jnp.inf)
    m = s.max(-1)
    e = jnp.exp(s - m[..., None])
    den = e.sum(-1)
    num = jnp.einsum('bnhqk,bnkhd->bnqhd', e, vext.astype(F32))

    def unsub(t):
        t = t.reshape((bb, Lp) + t.shape[3:])[:, :Ls]
        t = t.reshape((b, dil, Ls) + t.shape[2:])
        return jnp.swapaxes(t, 1, 2).reshape((b, S) + t.shape[3:])

    return unsub(jnp.swapaxes(m, 2, 3)), unsub(jnp.swapaxes(den, 2, 3)), unsub(num)

def gather_branch(q, kbuf, vbuf, q_loc, slopes, dil, span):
    j = jnp.arange(span + 1)
    idx = q_loc[:, None] - dil * j[None, :]
    valid = idx >= 0
    idx = jnp.maximum(idx, 0)
    kg = kbuf[:, idx]
    vg = vbuf[:, idx]
    s = jnp.einsum('bqhd,bqjhd->bhqj', q, kg).astype(F32)
    s = s - slopes[:, None, None] * (dil * j).astype(F32)[None, None, :]
    s = jnp.where(valid[None, None], s, -jnp.inf)
    m = s.max(-1)
    e = jnp.exp(s - m[..., None])
    den = e.sum(-1)
    num = jnp.einsum('bhqj,bqjhd->bqhd', e, vg.astype(F32))
    return jnp.swapaxes(m, 1, 2), jnp.swapaxes(den, 1, 2), num

def merge_branches(parts):
    m = jnp.stack([p[0] for p in parts])
    den = jnp.stack([p[1] for p in parts])
    num = jnp.stack([p[2] for p in parts])
    w = jnp.exp(m - m.max(0))
    return (w[..., None] * num).sum(0) / (w * den).sum(0)[..., None]

def even_layer(x, norm_g, w_in, conv_w, a_log, dt_bias, a_norm, b_norm, w_out, s_delta, conv_buf, s_ret):
    b, L, _ = x.shape
    h = rms_norm(x, norm_g)
    aq, ak, av, az, ab, aa, bq, bk, bv, bg = split_cols(h @ w_in, EVEN_SPLITS)
    qkv, conv_new = causal_conv(jnp.concatenate([aq, ak, av], -1), conv_buf, conv_w)
    aq, ak, av = split_cols(jax.nn.silu(qkv), (W_A, W_A, W_A))
    aq = l2_norm(heads(aq, H_A)) * HEAD_DIM ** -0.5
    ak = l2_norm(heads(ak, H_A))
    av = heads(av, H_A)
    beta = jax.nn.sigmoid(ab.astype(F32))
    g = -jnp.exp(a_log.astype(F32)) * jax.nn.softplus((aa + dt_bias).astype(F32))
    o_a, s_delta_new = gated_delta_chunked(aq, ak, av, g, beta, s_delta)
    o_a = rms_norm(o_a, a_norm).reshape(b, L, W_A) * jax.nn.silu(az)
    o_b, s_ret_new = retention_chunked(heads(bq, H_B), heads(bk, H_B) * HEAD_DIM ** -0.5, heads(bv, H_B), s_ret)
    o_b = group_norm(o_b, b_norm) * jax.nn.silu(bg)
    y = jnp.concatenate([o_a, o_b], -1) @ w_out
    return x + y.astype(x.dtype), s_delta_new, conv_new, s_ret_new

def odd_layer(x, norm_g, w_in, w_out, cq_g, ck_g, f_b, dq_g, dk_g, past):
    b, L, _ = x.shape
    h = rms_norm(x, norm_g)
    cq, ck, cv, cg, cf, dq, dk, dv, dg = split_cols(h @ w_in, ODD_SPLITS)
    scale = HEAD_DIM ** -0.5
    cq = rms_norm(heads(cq, H_C), cq_g) * scale
    ck = rms_norm(heads(ck, H_C), ck_g)
    cv = heads(cv, H_C)
    logf = jax.nn.log_sigmoid((cf + f_b).astype(F32))
    dq = rms_norm(heads(dq, H_D), dq_g) * scale
    dk = rms_norm(heads(dk, H_D), dk_g)
    dv = heads(dv, H_D)
    slopes = alibi_slopes()
    if past is None:
        F = jnp.cumsum(logf, axis=1)
        pos = jnp.arange(L)
        o_c = fox_attend(cq, F, pos, ck, cv, F, pos)
        parts = [band_branch(dq, dk, dv, slopes, dil, win // dil) for win, dil in D_BRANCHES]
        wb = min(D_WIN_MAX, L)
        kbuf_new, vbuf_new = dk[:, L - wb:], dv[:, L - wb:]
    else:
        kp, vp, lfp, kbuf, vbuf = past
        P = kp.shape[1]
        F = jnp.cumsum(jnp.concatenate([lfp.astype(F32), logf], axis=1), axis=1)
        kpos = jnp.arange(P + L)
        o_c = fox_attend(cq, F[:, P:], P + jnp.arange(L), jnp.concatenate([kp, ck], 1),
                         jnp.concatenate([vp, cv], 1), F, kpos)
        wb = kbuf.shape[1]
        kcat = jnp.concatenate([kbuf, dk], 1)
        vcat = jnp.concatenate([vbuf, dv], 1)
        q_loc = wb + jnp.arange(L)
        parts = [gather_branch(dq, kcat, vcat, q_loc, slopes, dil, win // dil) for win, dil in D_BRANCHES]
        kbuf_new, vbuf_new = kcat[:, -wb:], vcat[:, -wb:]
    o_d = merge_branches(parts).astype(x.dtype)
    o = jnp.concatenate([o_c.reshape(b, L, W_C) * jax.nn.silu(cg), o_d.reshape(b, L, W_D) * jax.nn.silu(dg)], -1)
    y = o @ w_out
    return x + y.astype(x.dtype), ck, cv, logf, kbuf_new, vbuf_new

def setup_inputs(seed: int = 0) -> dict:
    key = jax.random.key(seed)
    k = jax.random.split(key, 27)
    n_pages = PAST_LEN // PAGE_SIZE
    n_used = DEC_BATCH * n_pages
    n_phys = n_used + max(1, n_used // 4)
    wbuf = min(D_WIN_MAX, PAST_LEN)

    def nrm(kk, shape, s):
        return jax.random.normal(kk, shape, F32) * s

    dt = jnp.exp(jax.random.uniform(k[15], (N_EVEN, H_A), F32, math.log(1e-3), math.log(1e-1)))
    return {
        'x_prompt': nrm(k[0], (BATCH, SEQ, D_MODEL), 1.0),
        'x_sample': nrm(k[1], (DEC_BATCH, DEC_SEQ, D_MODEL), 1.0),
        'cache_fox_k': nrm(k[2], (n_phys, N_ODD, PAGE_SIZE, H_C, HEAD_DIM), 1.0),
        'cache_fox_v': nrm(k[3], (n_phys, N_ODD, PAGE_SIZE, H_C, HEAD_DIM), 1.0),
        'cache_fox_logf': jax.nn.log_sigmoid(FORGET_BIAS_INIT + nrm(k[4], (n_phys, N_ODD, PAGE_SIZE, H_C), 1.0)),
        'page_table': jax.random.permutation(k[5], n_phys)[:n_used].reshape(DEC_BATCH, n_pages).astype(jnp.int32),
        'cache_win_k': nrm(k[6], (N_ODD, DEC_BATCH, wbuf, H_D, HEAD_DIM), 1.0),
        'cache_win_v': nrm(k[7], (N_ODD, DEC_BATCH, wbuf, H_D, HEAD_DIM), 1.0),
        'state_delta': nrm(k[8], (N_EVEN, DEC_BATCH, H_A, HEAD_DIM, HEAD_DIM), 0.1),
        'state_delta_conv': nrm(k[9], (N_EVEN, DEC_BATCH, CONV_W - 1, 3 * W_A), 1.0),
        'state_ret': nrm(k[10], (N_EVEN, DEC_BATCH, H_B, HEAD_DIM, HEAD_DIM), 0.5),
        'norm_even': 1.0 + nrm(k[11], (N_EVEN, D_MODEL), 0.1),
        'w_in_even': nrm(k[12], (N_EVEN, D_MODEL, EVEN_IN), D_MODEL ** -0.5),
        'conv_w': nrm(k[13], (N_EVEN, CONV_W, 3 * W_A), CONV_W ** -0.5),
        'a_log': jnp.log(jax.random.uniform(k[14], (N_EVEN, H_A), F32, 1.0, 16.0)),
        'dt_bias': dt + jnp.log(-jnp.expm1(-dt)),
        'a_norm': 1.0 + nrm(k[16], (N_EVEN, HEAD_DIM), 0.1),
        'b_norm': 1.0 + nrm(k[17], (N_EVEN, W_B), 0.1),
        'w_out_even': nrm(k[18], (N_EVEN, W_A + W_B, D_MODEL), (W_A + W_B) ** -0.5),
        'norm_odd': 1.0 + nrm(k[19], (N_ODD, D_MODEL), 0.1),
        'w_in_odd': nrm(k[20], (N_ODD, D_MODEL, ODD_IN), D_MODEL ** -0.5),
        'c_q_norm': 1.0 + nrm(k[21], (N_ODD, HEAD_DIM), 0.1),
        'c_k_norm': 1.0 + nrm(k[22], (N_ODD, HEAD_DIM), 0.1),
        'f_bias': FORGET_BIAS_INIT + nrm(k[23], (N_ODD, H_C), 0.5),
        'd_q_norm': 1.0 + nrm(k[24], (N_ODD, HEAD_DIM), 0.1),
        'd_k_norm': 1.0 + nrm(k[25], (N_ODD, HEAD_DIM), 0.1),
        'w_out_odd': nrm(k[26], (N_ODD, W_C + W_D, D_MODEL), (W_C + W_D) ** -0.5),
    }

def reference(x_prompt, x_sample, cache_fox_k, cache_fox_v, cache_fox_logf, page_table, cache_win_k, cache_win_v,
              state_delta, state_delta_conv, state_ret, norm_even, w_in_even, conv_w, a_log, dt_bias, a_norm, b_norm,
              w_out_even, norm_odd, w_in_odd, c_q_norm, c_k_norm, f_bias, d_q_norm, d_k_norm, w_out_odd):
    n_pr = x_prompt.shape[0]
    n_dec = x_sample.shape[0]
    yp, ys = x_prompt, x_sample
    fk_p, fv_p, fl_p, fk_s, fv_s, fl_s = [], [], [], [], [], []
    wk_p, wv_p, wk_s, wv_s = [], [], [], []
    dl_p, dc_p, dl_s, dc_s, rt_p, rt_s = [], [], [], [], [], []
    for li in range(DEPTH):
        i = li // 2
        if li % 2 == 0:
            w = (norm_even[i], w_in_even[i], conv_w[i], a_log[i], dt_bias[i], a_norm[i], b_norm[i], w_out_even[i])
            s0 = jnp.zeros((n_pr, H_A, HEAD_DIM, HEAD_DIM), state_delta.dtype)
            c0 = jnp.zeros((n_pr, CONV_W - 1, 3 * W_A), state_delta_conv.dtype)
            r0 = jnp.zeros((n_pr, H_B, HEAD_DIM, HEAD_DIM), state_ret.dtype)
            yp, s_new, c_new, r_new = even_layer(yp, *w, s0, c0, r0)
            dl_p.append(s_new)
            dc_p.append(c_new)
            rt_p.append(r_new)
            ys, s_new, c_new, r_new = even_layer(ys, *w, state_delta[i], state_delta_conv[i], state_ret[i])
            dl_s.append(s_new)
            dc_s.append(c_new)
            rt_s.append(r_new)
        else:
            w = (norm_odd[i], w_in_odd[i], w_out_odd[i], c_q_norm[i], c_k_norm[i], f_bias[i], d_q_norm[i], d_k_norm[i])
            yp, k_new, v_new, lf_new, kb_new, vb_new = odd_layer(yp, *w, None)
            fk_p.append(k_new)
            fv_p.append(v_new)
            fl_p.append(lf_new)
            wk_p.append(kb_new)
            wv_p.append(vb_new)
            past = (cache_fox_k[page_table, i].reshape(n_dec, -1, H_C, HEAD_DIM),
                    cache_fox_v[page_table, i].reshape(n_dec, -1, H_C, HEAD_DIM),
                    cache_fox_logf[page_table, i].reshape(n_dec, -1, H_C),
                    cache_win_k[i], cache_win_v[i])
            ys, k_new, v_new, lf_new, kb_new, vb_new = odd_layer(ys, *w, past)
            fk_s.append(k_new)
            fv_s.append(v_new)
            fl_s.append(lf_new)
            wk_s.append(kb_new)
            wv_s.append(vb_new)
    return (yp, ys,
            jnp.stack(fk_p, 1), jnp.stack(fv_p, 1), jnp.stack(fl_p, 1),
            jnp.stack(fk_s, 1), jnp.stack(fv_s, 1), jnp.stack(fl_s, 1),
            jnp.stack(wk_p), jnp.stack(wv_p), jnp.stack(wk_s), jnp.stack(wv_s),
            jnp.stack(dl_p), jnp.stack(dc_p), jnp.stack(dl_s), jnp.stack(dc_s),
            jnp.stack(rt_p), jnp.stack(rt_s))


_drawn_inputs = setup_inputs


def setup_inputs(seed=0):
    import zlib

    import numpy as np

    out = dict(_drawn_inputs(seed))
    spreads = {}
    factors = {'cache_fox_logf': 3.88, 'c_q_norm': 6.367, 'd_q_norm': 6.624}
    for name, (base, spread) in spreads.items():
        noise = np.random.default_rng([zlib.crc32(name.encode()), seed]).standard_normal(out[name].shape)
        drawn = base * np.exp(spread * noise) if base else spread * noise
        out[name] = jnp.asarray(drawn.astype(out[name].dtype))
    for name, factor in factors.items():
        out[name] = (out[name] * factor).astype(out[name].dtype)
    return out
```

```python
from contextlib import ExitStack

import numpy as np
import concourse.bass as bass
from concourse import mybir
from concourse.alu_op_type import AluOpType as ALU

F32 = mybir.dt.float32
I32 = mybir.dt.int32
ACT = mybir.ActivationFunctionType
X = mybir.AxisListType.X

P = 128
D_MODEL = 1024
KT = D_MODEL // P
T = 2048
TILES = T // P
B = 8
L = 4
TS = B * L
NT = T + TS
CH = 416
NC = NT // CH
H = 4
HD = H * P
G = 4
PAGE = 128
NPG = 32
NPHYS = 320
WBUF = 2048
WT = 7
EPS = 1e-6
BIG = 1e30
SCALE = P ** -0.5
EVEN_OFF = {"A": (0, 512, 1024, 1536), "B": (2056, 2568, 3080, 3592)}
ODD_OFF = {"C": (0, 512, 1024, 1536), "D": (2052, 2564, 3076, 3588)}
EVEN_IN = 4104
ODD_IN = 4100
WMAX = 2048


def shape_constants():
    i = np.arange(P)
    f = np.float32
    lower = i[:, None] > i[None, :]
    c = {
        "ident": np.eye(P), "ones": np.ones((P, P)),
        "not_lower": np.where(lower, 0, BIG), "not_causal": np.where(lower, BIG, 0),
        "diag16": i[:, None] // 16 == i[None, :] // 16,
    }
    for s in (16, 32, 64):
        c[f"under{2 * s}"] = (i[:, None] // (2 * s) == i[None, :] // (2 * s)) & (i[:, None] // s > i[None, :] // s)
    c["causal_bias"] = np.where(i[None, :] > i[:, None], -BIG, 0)
    c["later"] = lower
    s = np.arange(TS)
    same = s[:, None] // L == s[None, :] // L
    pad = lambda a: np.pad(a, ((0, P - a.shape[0]), (0, 0)))
    c["s_not_lower"] = pad(np.where(same & (s[:, None] > s[None, :]), 0, BIG))
    c["s_not_causal"] = pad(np.where(same & (s[:, None] <= s[None, :]), 0, BIG))
    c["s_last"] = pad(same & (s[None, :] % L == L - 1))
    c["s_prefix"] = pad(same & (s[:, None] <= s[None, :]))
    c["s_bias"] = pad(np.where(same & (s[:, None] <= s[None, :]), 0, -BIG))
    c["s_cols"] = np.broadcast_to((s[None, :] // L == np.arange(B)[:, None]).reshape(1, -1), (P, B * TS))
    c["s_rows"] = pad(s[:, None] // L == np.arange(B)[None, :])
    r = np.arange(4 * H)
    c["head_cols"] = pad((r[:, None] // L == np.arange(HD)[None, :] // P))
    c["page_reset"] = np.broadcast_to((np.arange(H * NPG) % NPG != 0)[None, :], (P, H * NPG))
    slope = 2.0 ** (-8.0 * np.arange(1, H + 1) / H)

    def reach(d):
        n = ((d >= 0) & (d <= 128)).astype(int) + ((d >= 0) & (d <= 512) & (d % 4 == 0)) \
            + ((d >= 0) & (d <= 2048) & (d % 16 == 0))
        return n

    def bias(d, h):
        n = reach(d)
        return np.where(n > 0, np.log(np.maximum(n, 1)) - slope[h] * d, -BIG)

    new = np.stack([np.where(same, bias(s[None, :] - s[:, None], h), -BIG) for h in range(H)], 1)
    c["s_window"] = np.pad(new.reshape(TS, H * TS), ((0, P - TS), (0, 0)))
    rows = window_rows().reshape(WT, P)
    past = np.zeros((P, WT, H, L))
    for h in range(H):
        for q in range(L):
            past[:, :, h, q] = bias(WBUF + q - rows, h).T
    c["window_past"] = past.reshape(P, -1)
    names, cols, at = {}, [], 0
    for k, v in c.items():
        v = np.asarray(v, f)
        names[k] = (at, v.shape[1])
        at += v.shape[1]
        cols.append(v)
    pack = np.concatenate(cols, 1)
    m = np.arange(T)
    window = np.stack([bias(i[:, None] + (T - P) - m[None, :], h) for h in range(H)]).astype(f)
    lg = np.log1p(-np.exp2(-5.0 - np.arange(H, dtype=np.float64)))
    ret = np.zeros((H, P, RET), f)
    for h in range(H):
        d = i[None, :] - i[:, None]
        ret[h, :, 0:P] = np.where(d >= 0, np.exp(np.maximum(d, 0) * lg[h]) * SCALE, 0)
        ret[h, :, P:2 * P] = np.exp((i + 1.0) * lg[h])[None, :]
        ret[h, :, 256] = np.exp((P - 1.0 - i) * lg[h]) * SCALE
        ret[h, :, 257] = np.exp(P * lg[h])
        ds = s[None, :] - s[:, None]
        ret[h, :TS, 258:290] = np.where(same & (ds >= 0), np.exp(np.maximum(ds, 0) * lg[h]) * SCALE, 0)
        ret[h, :, 290:322] = np.exp((s % L + 1.0) * lg[h])[None, :]
        ret[h, :TS, 322] = np.exp((L - 1.0 - s % L) * lg[h]) * SCALE
        ret[h, :, 323] = np.exp(L * lg[h])
    reset = np.ones((1, NT), f)
    reset[0, 0:T:P] = 0
    reset[0, T::L] = 0
    return {"c_pack": pack, "c_window": window, "c_ret": ret, "c_reset": reset}, names


RET = 324


def window_rows():
    g = np.arange(96)[:, None] * 16 + np.arange(4)[None, :]
    return np.concatenate([g.reshape(-1), np.arange(1536, 2048)])


def repeat(ap, axis, n):
    ap = ap.unsqueeze(axis)
    shape = list(ap.shape)
    shape[axis] = n
    return ap.broadcast_to(shape)


def clear(nc, sems):
    with nc.Block() as block:
        @block.gpsimd
        def _(pool):
            for s in sems:
                pool.sem_clear(s)


class Chip:
    pass


def load_tokens(nc, k, io):
    with ExitStack() as c:
        sem = lambda n: c.enter_context(nc.semaphore(n))
        const_loaded, vec_loaded = sem("const_loaded"), sem("vec_loaded")
        x_loaded = [sem("x_loaded0"), sem("x_loaded1")]
        rows_loaded, rows_turned, rows_copied = sem("rows_loaded"), sem("rows_turned"), sem("rows_copied")
        x_turned, left_copied, right_copied = sem("x_turned"), sem("left_copied"), sem("right_copied")
        xrow = c.enter_context(nc.sbuf_tensor("xrow", [P, 2, D_MODEL], F32))
        conv_rows = c.enter_context(nc.sbuf_tensor("conv_rows", [28, 3 * HD], F32))
        block = c.enter_context(nc.Block())
        vectors = [(k.g_even, io.norm_even[0].rearrange("(k p) -> p k", p=P)),
                   (k.g_odd, io.norm_odd[0].rearrange("(k p) -> p k", p=P)),
                   (k.b_norm, io.b_norm[0].rearrange("(k p) -> p k", p=P)),
                   (k.vec[:, 0:1], io.a_norm[0].unsqueeze(1)), (k.vec[:, 1:2], io.c_q_norm[0].unsqueeze(1)),
                   (k.vec[:, 2:3], io.c_k_norm[0].unsqueeze(1)), (k.vec[:, 3:4], io.d_q_norm[0].unsqueeze(1)),
                   (k.vec[:, 4:5], io.d_k_norm[0].unsqueeze(1)),
                   (k.small[32:36, 0:1], io.a_log[0].unsqueeze(1)), (k.small[32:36, 1:2], io.dt_bias[0].unsqueeze(1)),
                   (k.small[0:4, 2:3], io.f_bias[0].unsqueeze(1)),
                   (k.pages, io.page_table.rearrange("b n -> (b n)").unsqueeze(0))]

        @block.sync
        def _(sp):
            sp.dma_start(k.pack, io.c_pack).then_inc(const_loaded, 16)
            sp.dma_start(conv_rows[0:24, :], io.state_delta_conv[0].rearrange("b r c -> (b r) c")).then_inc(rows_loaded, 16)
            sp.dma_start(conv_rows[24:28, :], io.conv_w[0]).then_inc(rows_loaded, 16)
            for t in range(TILES + 1):
                if t >= 2:
                    sp.wait_ge(x_turned, 2 * (t - 1))
                src = io.x_prompt[0, t * P:(t + 1) * P, :] if t < TILES else io.x_sample.rearrange("b l d -> (b l) d")
                n = P if t < TILES else TS
                sp.dma_start(xrow[0:n, t % 2, :], src).then_inc(x_loaded[t % 2], 16)
            for dst, src in vectors:
                sp.dma_start(dst, src).then_inc(vec_loaded, 16)
            sp.wait_ge(vec_loaded, 16 * len(vectors))

        @block.tensor
        def _(pe):
            pe.wait_ge(const_loaded, 16)
            pe.wait_ge(rows_loaded, 32)
            for j in range(12):
                last = pe.transpose(k.ps[2][:, j * 28:(j + 1) * 28], conv_rows[:, j * P:(j + 1) * P], k.c("ident")[0:28, 0:28])
            last.then_inc(rows_turned, 1)
            for t in range(TILES + 1):
                n = P if t < TILES else TS
                pe.wait_ge(x_loaded[t % 2], 16 * (t // 2 + 1))
                for half, copied in ((0, left_copied), (1, right_copied)):
                    if t >= 1:
                        pe.wait_ge(copied, t)
                    for j in range(4):
                        kk = 4 * half + j
                        last = pe.transpose(k.ps[half][:, j * P:j * P + n], xrow[0:n, t % 2, kk * P:(kk + 1) * P],
                                            k.c("ident")[0:n, 0:n])
                    last.then_inc(x_turned, 1)

        @block.vector
        def _(dve):
            dve.wait_ge(rows_turned, 1)
            dve.tensor_copy(k.conv_cols.rearrange("p a b -> p (a b)"), k.ps[2][:, 0:336]).then_inc(rows_copied, 1)
            for t in range(TILES + 1):
                n = P if t < TILES else TS
                dve.wait_ge(x_turned, 2 * t + 1)
                dve.tensor_copy(k.xT[:, 0:4, t * P:t * P + n],
                                k.ps[0].rearrange("p (j n) -> p j n", j=4)[:, :, 0:n]).then_inc(left_copied, 1)

        @block.scalar
        def _(act):
            for t in range(TILES + 1):
                n = P if t < TILES else TS
                act.wait_ge(x_turned, 2 * t + 2)
                act.copy(k.xT[:, 4:8, t * P:t * P + n],
                         k.ps[1].rearrange("p (j n) -> p j n", j=4)[:, :, 0:n]).then_inc(right_copied, 1)
    clear(nc, [const_loaded, vec_loaded, *x_loaded, rows_loaded, rows_turned, rows_copied, x_turned, left_copied, right_copied])


def token_norms(nc, k, layer):
    with ExitStack() as c:
        sem = lambda n: c.enter_context(nc.semaphore(f"{n}_{layer}"))
        squared, summed, logged, rooted = sem("squared"), sem("summed"), sem("logged"), sem("rooted")
        sq = c.enter_context(nc.sbuf_tensor(f"sq_{layer}", [P, 2, NT], F32))
        block = c.enter_context(nc.Block())

        @block.scalar
        def _(act):
            for j in range(KT):
                if j >= 2:
                    act.wait_ge(summed, j - 1)
                act.activation(sq[:, j % 2, :], k.xT[:, j, :], ACT.Square).then_inc(squared, 1)
            act.wait_ge(summed, KT)
            for n in range(NC):
                act.activation(sq[:, 0, n * CH:(n + 1) * CH], k.ps[n][:, 0:CH], ACT.Ln, bias=k.eps,
                               scale=1.0 / D_MODEL).then_inc(logged, 1)
            act.wait_ge(logged, NC)
            act.activation(k.rstd[:, :], sq[:, 0, :], ACT.Exp, scale=-0.5).then_inc(rooted, 1)

        @block.tensor
        def _(pe):
            for j in range(KT):
                pe.wait_ge(squared, j + 1)
                for n in range(NC):
                    last = pe.matmul(k.ps[n][:, 0:CH], k.c("ones"), sq[:, j % 2, n * CH:(n + 1) * CH],
                                     start=(j == 0), stop=(j == KT - 1))
                last.then_inc(summed, 1)
    clear(nc, [squared, summed, logged, rooted])


def row_gates_even(nc, k, io):
    with ExitStack() as c:
        sem = lambda n: c.enter_context(nc.semaphore(n))
        w_loaded, w_zero, w_scaled = sem("gw_loaded"), sem("gw_zero"), sem("gw_scaled")
        row_ready, row_taken = sem("row_ready"), sem("row_taken")
        a_step, d_step = sem("gate_act"), sem("gate_dve")
        turned, cols_ready, stored = sem("gates_turned"), sem("gate_cols"), sem("g_stored")
        w = c.enter_context(nc.sbuf_tensor("gw", [P, KT, 36], F32))
        rows = c.enter_context(nc.sbuf_tensor("rows", [36, NT], F32))
        tmp = c.enter_context(nc.sbuf_tensor("rtmp", [36, NT], F32))
        tmp2 = c.enter_context(nc.sbuf_tensor("rtmp2", [36, NT], F32))
        reset = c.enter_context(nc.sbuf_tensor("reset", [36, NT], F32))
        block = c.enter_context(nc.Block())
        HI = slice(32, 36)

        @block.sync
        def _(sp):
            sp.wait_ge(w_zero, 1)
            wv = io.w_in_even[0].rearrange("(k p) c -> p k c", p=P)
            sp.dma_start(w[:, :, 0:4], wv[:, :, 2048:2052]).then_inc(w_loaded, 16)
            sp.dma_start(w[:, :, 32:36], wv[:, :, 2052:2056]).then_inc(w_loaded, 16)
            sp.dma_start(reset[HI, :], io.c_reset.broadcast_to([4, NT])).then_inc(w_loaded, 16)
            sp.wait_ge(d_step, 6)
            sp.dma_start(io.scr_g, rows[HI, :]).then_inc(stored, 16)
            sp.wait_ge(stored, 16)

        @block.vector
        def _(dve):
            dve.memset(w[:, :, :], 0.0).then_inc(w_zero, 1)
            dve.wait_ge(w_loaded, 48)
            dve.tensor_tensor(w[:, :, :], w[:, :, :], repeat(k.g_even, 2, 36), ALU.mult).then_inc(w_scaled, 1)
            for n in range(NC):
                dve.wait_ge(row_ready, n + 1)
                dve.tensor_tensor(rows[:, n * CH:(n + 1) * CH], k.ps[n % 2][0:36, 0:CH], k.rstd[0:36, n * CH:(n + 1) * CH],
                                  ALU.mult).then_inc(row_taken, 1)
            dve.wait_ge(a_step, 1)
            dve.tensor_scalar(rows[0:4, :], tmp[0:4, :], 0.5, 0.5, ALU.mult, ALU.add).then_inc(d_step, 1)
            dve.tensor_scalar(tmp2[HI, :], rows[HI, :], k.small[HI, 1:2], 0.0, ALU.add, ALU.max).then_inc(d_step, 1)
            dve.wait_ge(a_step, 4)
            dve.wait_ge(d_step, 2)
            dve.tensor_tensor(tmp2[HI, :], tmp2[HI, :], tmp[HI, :], ALU.add).then_inc(d_step, 1)
            dve.wait_ge(a_step, 5)
            dve.tensor_scalar(k.small[HI, 3:4], k.small[HI, 3:4], -1.0, None, ALU.mult).then_inc(d_step, 1)
            dve.wait_ge(d_step, 4)
            dve.tensor_scalar(tmp2[HI, :], tmp2[HI, :], k.small[HI, 3:4], None, ALU.mult).then_inc(d_step, 1)
            dve.wait_ge(d_step, 5)
            dve.tensor_tensor_scan(rows[HI, :], reset[HI, :], tmp2[HI, :], 0.0, ALU.mult, ALU.add).then_inc(d_step, 1)
            for half in range(2):
                dve.wait_ge(turned, half + 1)
                n = 9 - half
                for what in range(2):
                    last = dve.tensor_copy(k.gate_cols[:, what, :, 9 * half:9 * half + n],
                                           k.ps[2 + half][:, 0:36 * n].rearrange("p (t r) -> p r t", r=36)[:, 32 * what:32 * what + H, :])
                last.then_inc(cols_ready, 1)

        @block.scalar
        def _(act):
            act.wait_ge(row_taken, NC)
            act.activation(tmp[0:4, :], rows[0:4, :], ACT.Tanh, scale=0.5).then_inc(a_step, 1)
            act.activation(tmp[HI, :], rows[HI, :], ACT.Abs, bias=k.small[HI, 1:2]).then_inc(a_step, 1)
            act.wait_ge(a_step, 2)
            act.activation(tmp[HI, :], tmp[HI, :], ACT.Exp, scale=-1.0).then_inc(a_step, 1)
            act.wait_ge(a_step, 3)
            act.activation(tmp[HI, :], tmp[HI, :], ACT.Ln, bias=k.one[HI, :]).then_inc(a_step, 1)
            act.activation(k.small[HI, 3:4], k.small[HI, 0:1], ACT.Exp).then_inc(a_step, 1)

        @block.tensor
        def _(pe):
            pe.wait_ge(w_scaled, 1)
            for n in range(NC):
                if n >= 2:
                    pe.wait_ge(row_taken, n - 1)
                for j in range(KT):
                    last = pe.matmul(k.ps[n % 2][0:36, 0:CH], w[:, j, :], k.xT[:, j, n * CH:(n + 1) * CH],
                                     start=(j == 0), stop=(j == KT - 1))
                last.then_inc(row_ready, 1)
            pe.wait_ge(d_step, 6)
            for half in range(2):
                pe.matmul(k.ps[2 + half][:, 0:324], k.c("ones"), k.zero[:, 0:324], start=True, stop=True)
                for t in range(9 * half, 17 if half else 9):
                    m = P if t < TILES else TS
                    a = 36 * (t - 9 * half)
                    last = pe.transpose(k.ps[2 + half][0:m, a:a + 36], rows[:, t * P:t * P + m], k.c("ident")[0:36, 0:36])
                last.then_inc(turned, 1)
    clear(nc, [w_loaded, w_zero, w_scaled, row_ready, row_taken, a_step, d_step, turned, cols_ready, stored])


def project_head(nc, k, io, c, layer, branch, h, dst):
    sem = lambda n: c.enter_context(nc.semaphore(f"{n}_{branch}"))
    w_loaded, w_scaled, proj_ready, proj_taken = sem("w_loaded"), sem("w_scaled"), sem("proj_ready"), sem("proj_taken")
    w_all = io.w_in_even[0] if layer == 0 else io.w_in_odd[0]
    offs = (EVEN_OFF if layer == 0 else ODD_OFF)[branch]
    gain = k.g_even if layer == 0 else k.g_odd
    wv = w_all.rearrange("(k p) c -> p k c", p=P)

    def sync(sp):
        for m in range(4):
            sp.dma_start(k.w[:, :, m * P:(m + 1) * P], wv[:, :, bass.ds(h * P + offs[m], P)]).then_inc(w_loaded, 16)

    def gpsimd(pool):
        pool.wait_ge(w_loaded, 64)
        pool.tensor_tensor(k.w[:, :, :], k.w[:, :, :], repeat(gain, 2, 4 * P), ALU.mult).then_inc(w_scaled, 1)

    def tensor(pe):
        pe.wait_ge(w_scaled, 1)
        for m in range(4):
            for n in range(NC):
                at = m * NC + n
                if at >= 2:
                    pe.wait_ge(proj_taken, at - 1)
                for j in range(KT):
                    last = pe.matmul(k.ps[at % 2][:, 0:CH], k.w[:, j, m * P:(m + 1) * P],
                                     k.xT[:, j, n * CH:(n + 1) * CH], start=(j == 0), stop=(j == KT - 1))
                last.then_inc(proj_ready, 1)

    def vector(dve):
        for m in range(4):
            for n in range(NC):
                at = m * NC + n
                dve.wait_ge(proj_ready, at + 1)
                for out, a, b in dst(m, n):
                    r = k.rstd[:, n * CH + a:n * CH + b]
                    src = k.ps[at % 2][:, a:b]
                    if len(out.shape) == 3:
                        r = r.rearrange("p (x y) -> p x y", y=L)
                        src = src.rearrange("p (x y) -> p x y", y=L)
                    last = dve.tensor_tensor(out, src, r, ALU.mult)
                last.then_inc(proj_taken, 1)

    return [w_loaded, w_scaled, proj_ready, proj_taken], sync, gpsimd, tensor, vector


def feature_sums(pe, k, src, banks=(0, 1, 2, 3, 4)):
    for n in range(NC):
        last = pe.matmul(k.ps[banks[n]][:, 0:CH], k.c("ones"), src[:, n * CH:(n + 1) * CH], start=True, stop=True)
    return last


class Order:

    def __init__(self, eng, sem):
        self.eng, self.sem, self.n = eng, sem, 0

    def after(self, ins):
        ins.then_inc(self.sem, 1)
        self.n += 1
        self.eng.wait_ge(self.sem, self.n)


def head_A(nc, k, io, h):
    with ExitStack() as c:
        sbuf = lambda n, s: c.enter_context(nc.sbuf_tensor(n, s, F32))[:]
        sem = lambda n: c.enter_context(nc.semaphore(n))
        raw = sbuf("raw", [P, 3, 3 + T + B * 7])
        g_row, g_exp = sbuf("g_row", [P, NT]), sbuf("g_exp", [P, NT])
        grp, more = k.w, sbuf("grp", [P, 6, G * P])
        Kb, Kt, Vb, DT, A, N, NTr, N2 = [grp[:, i, :] for i in range(8)]
        N2T, N4, N4T, X0, X1, QK = [more[:, i, :] for i in range(6)]
        hcol = sbuf("hcol", [P, 4, 17])
        S = sbuf("S", [P, 2, P])
        S0 = raw[:, 2, 0:B * P].rearrange("p (b v) -> p b v", b=B)
        u = sbuf("u", [P, P])
        tail = sbuf("tailbuf", [TS, 1])
        convo = sbuf("convo", [P, 27])
        convr = sbuf("convr", [27, 3 * P])
        sq = raw[:, 1, 0:NT]
        O = raw[:, 0, 0:NT]
        Q = k.qkvz
        w_sems, p_sync, p_pool, p_tensor, p_vector = project_head(
            nc, k, io, c, 0, "A", h,
            lambda m, n: [(Q[:, 3, n * CH:(n + 1) * CH], 0, CH)] if m == 3 else
            ([(raw[:, m, 3 + n * CH:3 + (n + 1) * CH], 0, CH)] if n < NC - 1 else
             [(raw[:, m, 3 + n * CH:3 + T], 0, T - n * CH),
              (raw[:, m, 3 + T:].rearrange("p (b r) -> p b r", r=7)[:, :, 3:7], T - n * CH, CH)]))
        names = ["g_loaded", "s_loaded", "conv_set", "conv_done", "conv_kept", "conv_turned", "conv_out",
                 "silu_done", "sq_done", "ss_done", "ln_done", "root_done", "normed",
                 "dve_order", "act_order", "grams", "exp_in", "exp_out", "product", "operand", "u_made", "u_kept",
                 "s_made", "s_kept", "o_kept", "um_ready", "sn_made", "sn_kept", "out_stored", "post_sq", "post_ss",
                 "post_root", "post_ready", "gate_done", "cols_done"]
        s = {n: sem(n) for n in names}
        block = c.enter_context(nc.Block())

        groups = [(g * G * P, G, P) for g in range(TILES // G)] + [(T, 1, TS)]

        @block.sync
        def _(sp):
            p_sync(sp)
            sp.dma_start(g_row, io.scr_g[bass.ds(h, 1), :].broadcast_to([P, NT])).then_inc(s["g_loaded"], 16)
            sp.wait_ge(s["conv_out"], 1)
            for m in range(3):
                col = bass.ds(h * P + m * HD, P)
                sp.dma_start(io.out_delta_conv_prompt[0, 0, :, col], convr[0:3, m * P:(m + 1) * P]).then_inc(s["out_stored"], 16)
                sp.dma_start(io.out_delta_conv_sample[0, :, :, col].rearrange("b r c -> (b r) c"),
                             convr[3:27, m * P:(m + 1) * P]).then_inc(s["out_stored"], 16)
            sp.wait_ge(s["normed"], 3)
            sp.dma_start(S0, io.state_delta[0, :, bass.ds(h, 1), :, :].rearrange("b o k v -> k (b o) v")).then_inc(s["s_loaded"], 16)
            sp.wait_ge(s["s_kept"], TILES)
            sp.dma_start(io.out_delta_prompt[0, 0, bass.ds(h, 1)].rearrange("o k v -> (o k) v"), S[:, TILES % 2, :]).then_inc(s["out_stored"], 16)
            sp.wait_ge(s["sn_kept"], 1)
            sp.dma_start(io.out_delta_sample[0, :, bass.ds(h, 1), :, :].rearrange("b o k v -> k (b o) v"), S0).then_inc(s["out_stored"], 16)
            sp.wait_ge(s["post_ready"], 1)
            sp.dma_start(io.scr_o[bass.ds(h, 1)].rearrange("o p n -> (o p) n"), O).then_inc(s["out_stored"], 16)
            sp.wait_ge(s["out_stored"], 16 * 9)

        @block.gpsimd
        def _(pool):
            p_pool(pool)

        @block.tensor
        def _(pe):
            p_tensor(pe)
            for m in range(3):
                pe.wait_ge(s["conv_kept"], m + 1)
                if m:
                    pe.wait_ge(s["cols_done"], m)
                pe.transpose(k.ps[2][0:27, 0:P], convo, k.c("ident")).then_inc(s["conv_turned"], 1)
            for m in range(2):
                pe.wait_ge(s["sq_done"], m + 1)
                if m:
                    pe.wait_ge(s["ln_done"], NC)
                feature_sums(pe, k, sq).then_inc(s["ss_done"], 1)
            pe.wait_ge(s["normed"], 3)
            used = 0
            tile = 0
            for gi, (t0, ng, w) in enumerate(groups):
                sample = w != P
                idn = k.c("ident")[0:w, 0:w]
                sl = [slice(i * w, (i + 1) * w) for i in range(ng)]
                hs = [slice(i * P, (i + 1) * P) for i in range(ng)]
                tok = [slice(t0 + i * w, t0 + (i + 1) * w) for i in range(ng)]
                if gi:
                    pe.wait_ge(s["o_kept"], tile)
                    pe.wait_ge(s["s_kept"], tile)
                for i in range(ng):
                    pe.transpose(k.ps[0][0:w, hs[i]], Q[:, 1, tok[i]], k.c("ident"))
                    pe.transpose(k.ps[1][0:w, hs[i]], Q[:, 2, tok[i]], k.c("ident"))
                    pe.matmul(k.ps[2][0:w, sl[i]], Q[:, 1, tok[i]], Q[:, 1, tok[i]], start=True, stop=True)
                    last = pe.matmul(k.ps[3][0:w, sl[i]], Q[:, 1, tok[i]], Q[:, 0, tok[i]], start=True, stop=True)
                last.then_inc(s["grams"], 1)

                def products(todo):
                    nonlocal used
                    used += 1
                    pe.wait_ge(s["operand"], used)
                    for bank, lhs, rhs in todo:
                        for i in range(ng):
                            if rhs is None:
                                last = pe.transpose(k.ps[bank][0:w, sl[i]], lhs[0:w, sl[i]], idn)
                            else:
                                last = pe.matmul(k.ps[bank][0:w, sl[i]], lhs[0:w, sl[i]], rhs[0:w, sl[i]], start=True, stop=True)
                    last.then_inc(s["product"], 1)

                products([(4, N, None)])
                if sample:
                    products([(5, NTr, N)])
                    products([(4, N2, X0)])
                    XT = X1
                else:
                    products([(5, NTr, N), (6, N, NTr)])
                    products([(5, N2T, N2), (6, N2, N2T), (4, N2, X0)])
                    products([(5, N4T, N4), (4, N4, X1)])
                    products([(4, N, X0)])
                    cur, nxt = X1, X0
                    for _l in range(3):
                        products([(5, cur, None), (6, N, cur)])
                        products([(4, NTr, N2)])
                        cur, nxt = nxt, cur
                    XT = cur
                pe.wait_ge(s["operand"], used + 1)
                for i in range(ng):
                    last = pe.matmul(k.ps[5][:, sl[i]], Kb[0:w, hs[i]], XT[0:w, sl[i]], start=True, stop=True)
                last.then_inc(s["product"], 1)
                pe.wait_ge(s["operand"], used + 2)
                used += 2
                if not sample:
                    for i in range(ng):
                        if tile:
                            pe.wait_ge(s["s_kept"], tile)
                        pe.matmul(k.ps[0][:, 0:P], XT[:, sl[i]], Vb[:, hs[i]], start=True, stop=False)
                        pe.matmul(k.ps[0][:, 0:P], N4[:, sl[i]], S[:, tile % 2, :], start=False, stop=True).then_inc(s["u_made"], 1)
                        if tile:
                            pe.wait_ge(s["o_kept"], tile)
                        pe.matmul(k.ps[7][:, 0:P], S[:, tile % 2, :], k.qd[:, tok[i]], start=True, stop=False)
                        pe.wait_ge(s["u_kept"], tile + 1)
                        pe.matmul(k.ps[7][:, 0:P], u, QK[:, sl[i]], start=False, stop=True)
                        pe.matmul(k.ps[1][:, 0:P], Kt[:, hs[i]], u, start=True, stop=True).then_inc(s["s_made"], 1)
                        tile += 1
                else:
                    pe.wait_ge(s["s_loaded"], 16)
                    pe.matmul(k.ps[0][0:TS, 0:P], XT[0:TS, 0:TS], Vb[0:TS, 0:P], start=True, stop=False)
                    for b in range(B):
                        last = pe.matmul(k.ps[0][0:TS, 0:P], N4[:, b * TS:(b + 1) * TS], S0[:, b, :], start=False, stop=(b == B - 1))
                    last.then_inc(s["u_made"], 1)
                    pe.wait_ge(s["u_kept"], tile + 1)
                    pe.matmul(k.ps[7][:, 0:TS], u[0:TS, :], QK[0:TS, 0:TS], start=True, stop=False)
                    for b in range(B):
                        last = pe.matmul(k.ps[7][:, b * L:(b + 1) * L], S0[:, b, :], k.qd[:, T + b * L:T + (b + 1) * L],
                                         start=False, stop=(b == B - 1))
                    last.then_inc(s["s_made"], 1)
                    pe.wait_ge(s["um_ready"], 1)
                    for half in range(2):
                        last = pe.matmul(k.ps[1 + half][:, 0:512], Kt[0:TS, 0:P],
                                         grp[0:TS, 5 + half, :], start=True, stop=True)
                    last.then_inc(s["sn_made"], 1)
            pe.wait_ge(s["post_sq"], 1)
            feature_sums(pe, k, sq).then_inc(s["post_ss"], 1)

        @block.vector
        def _(dve):
            d = Order(dve, s["dve_order"])
            for m in range(3):
                dve.memset(raw[:, m, 0:3], 0.0)
                last = dve.tensor_copy(raw[:, m, 3 + T:].rearrange("p (b r) -> p b r", r=7)[:, :, 0:3],
                                       k.conv_cols[:, bass.ds(h + m * H, 1), 0:24].rearrange("p o (b r) -> p (o b) r", r=3))
            d.after(last)
            cw = k.cw_head
            for m in range(3):
                last = dve.tensor_copy(cw[:, m, :], k.conv_cols[:, bass.ds(h + m * H, 1), 24:28].rearrange("p o r -> p (o r)"))
            d.after(last)
            d.after(dve.tensor_copy(hcol[:, 0:2, :], k.gate_cols[:, :, bass.ds(h, 1), :].rearrange("p u o t -> p u (o t)")))
            p_vector(dve)
            dve.wait_ge(w_sems[3], 4 * NC)
            for m in range(3):
                if m:
                    dve.wait_ge(s["conv_turned"], m)
                dve.tensor_copy(convo[:, 0:3], raw[:, m, T:T + 3])
                dve.tensor_copy(convo[:, 3:27].rearrange("p (b r) -> p b r", r=3),
                                raw[:, m, 3 + T:].rearrange("p (b r) -> p b r", r=7)[:, :, 4:7]).then_inc(s["conv_kept"], 1)
                for out, src in ((Q[:, m, 0:T], lambda j: raw[:, m, j:j + T]),
                                 (Q[:, m, T:NT].rearrange("p (b l) -> p b l", l=L),
                                  lambda j: raw[:, m, 3 + T:].rearrange("p (b r) -> p b r", r=7)[:, :, j:j + L])):
                    d.after(dve.tensor_scalar(out, src(0), cw[:, m, 0:1], None, ALU.mult))
                    for j in range(1, 4):
                        last = dve.scalar_tensor_tensor(out, src(j), cw[:, m, j:j + 1], out, ALU.mult, ALU.add)
                        d.after(last)
                dve.engine_nop().then_inc(s["conv_done"], 1)
                dve.wait_ge(s["conv_turned"], m + 1)
                dve.tensor_copy(convr[:, m * P:(m + 1) * P], k.ps[2][0:27, 0:P]).then_inc(s["cols_done"], 1)
            dve.wait_ge(s["cols_done"], 3)
            dve.engine_nop().then_inc(s["conv_out"], 1)
            dve.wait_ge(s["exp_out"], 1)
            d.after(dve.tensor_tensor(hcol[:, 2, :], hcol[:, 2, :], hcol[:, 0, :], ALU.mult))
            d.after(dve.tensor_scalar(hcol[:, 3, :], hcol[:, 0, :], -1.0, None, ALU.mult))
            for m in range(2):
                dve.wait_ge(s["root_done"], m + 1)
                dve.scalar_tensor_tensor(Q[:, m, :], Q[:, m, :], SCALE if m == 0 else 1.0, sq, ALU.mult, ALU.mult).then_inc(s["normed"], 1)
            dve.wait_ge(s["normed"], 2)
            dve.tensor_tensor(k.qd[:, :], Q[:, 0, :], g_exp, ALU.mult).then_inc(s["normed"], 1)
            dve.memset(S[:, 0, :], 0.0)
            seen = 0
            tile = 0
            exps = 1
            for gi, (t0, ng, w) in enumerate(groups):
                sample = w != P
                v3 = lambda ap, n=w: ap[0:w, 0:ng * n].rearrange("p (g n) -> p g n", g=ng)
                ti = t0 // P
                gcol = repeat(hcol[0:w, 1, ti:ti + ng], 2, w)
                mask = lambda n: repeat(k.c(n)[0:w, 0:w], 1, ng)
                row = g_row[0:w, t0:t0 + ng * w].rearrange("p (g n) -> p g n", g=ng)
                pre = "s_" if sample else ""
                if gi:
                    dve.wait_ge(s["s_made"], tile)
                d.after(dve.tensor_tensor(v3(X0), row, gcol, ALU.subtract))
                dve.tensor_tensor(v3(X1), v3(X0), mask(pre + "not_lower"), ALU.add).then_inc(s["exp_in"], 1)
                dve.tensor_tensor(v3(DT), v3(X0), mask(pre + "not_causal"), ALU.subtract).then_inc(s["exp_in"], 1)
                exps += 2
                dve.wait_ge(s["exp_out"], exps)
                dve.wait_ge(s["grams"], gi + 1)
                d.after(dve.tensor_tensor(v3(A), v3(X1), repeat(hcol[0:w, 3, ti:ti + ng], 2, w), ALU.mult))
                d.after(dve.tensor_tensor(v3(A), v3(k.ps[2]), v3(A), ALU.mult))
                if sample:
                    dve.tensor_copy(v3(N), v3(A)).then_inc(s["operand"], 1)
                else:
                    dve.tensor_tensor(v3(N), v3(A), mask("diag16"), ALU.mult).then_inc(s["operand"], 1)
                dve.tensor_tensor(v3(QK), v3(k.ps[3]), v3(DT), ALU.mult)
                kt = lambda ap: v3(ap, P)
                dve.tensor_tensor(kt(Kb), kt(k.ps[0]), repeat(hcol[0:w, 2, ti:ti + ng], 2, P), ALU.mult)
                dve.tensor_tensor(kt(Vb), kt(k.ps[1]), repeat(hcol[0:w, 0, ti:ti + ng], 2, P), ALU.mult)
                if sample:
                    d.after(dve.tensor_tensor(X0[0:w, 0:w], DT[0:w, 0:w], k.c("s_last")[0:w, :], ALU.mult))
                    d.after(dve.tensor_reduce(tail, X0[0:w, 0:w], X, ALU.add))
                    d.after(dve.tensor_scalar(Kt[0:w, 0:P], k.ps[0][0:w, 0:P], tail, None, ALU.mult))
                else:
                    d.after(dve.tensor_tensor(kt(Kt), kt(k.ps[0]), repeat(DT.rearrange("p (g n) -> p g n", g=ng)[:, :, P - 1], 2, P), ALU.mult))

                def take(todo):
                    nonlocal seen
                    dve.wait_ge(s["product"], seen + 1)
                    seen += 1
                    for fn in todo:
                        last = fn()
                    last.then_inc(s["operand"], 1)

                cp = lambda dst, bank: (lambda: dve.tensor_copy(v3(dst), v3(k.ps[bank])))
                plus = lambda dst, src, bank: (lambda: dve.tensor_tensor(v3(dst), v3(src), v3(k.ps[bank]), ALU.add))
                take([cp(NTr, 4), lambda: dve.tensor_tensor(v3(X0), v3(k.ps[4]), mask("ident"), ALU.add)])
                if sample:
                    take([cp(N2, 5)])
                    take([plus(X1, X0, 4)])
                else:
                    take([cp(N2, 5), cp(N2T, 6)])
                    take([cp(N4, 5), cp(N4T, 6), plus(X1, X0, 4)])
                    take([cp(N, 5), plus(X0, X1, 4)])
                    dve.wait_ge(s["product"], seen + 1)
                    seen += 1
                    dve.tensor_tensor(v3(X1), v3(X0), v3(k.ps[4]), ALU.add)
                    dve.tensor_tensor(v3(N), v3(A), mask("under32"), ALU.mult).then_inc(s["operand"], 1)
                    cur, nxt = X1, X0
                    for lvl in (32, 64, 128):
                        take([cp(NTr, 5), cp(N2, 6)])
                        if lvl < 128:
                            take([plus(nxt, cur, 4), lambda: dve.tensor_tensor(v3(N), v3(A), mask(f"under{2 * lvl}"), ALU.mult)])
                        else:
                            take([plus(nxt, cur, 4)])
                        cur, nxt = nxt, cur
                dve.wait_ge(s["product"], seen + 1)
                seen += 1
                if not sample:
                    dve.tensor_scalar(N4, k.ps[5], -1.0, None, ALU.mult).then_inc(s["operand"], 1)
                    for i in range(ng):
                        dve.wait_ge(s["s_made"], tile + 1)
                        dve.wait_ge(s["s_kept"], tile) if tile else None
                        dve.scalar_tensor_tensor(S[:, (tile + 1) % 2, :], S[:, tile % 2, :], g_exp[:, t0 + (i + 1) * P - 1:t0 + (i + 1) * P],
                                                 k.ps[1][:, 0:P], ALU.mult, ALU.add).then_inc(s["s_kept"], 1)
                        tile += 1
                else:
                    dve.scalar_tensor_tensor(N4[:, 0:B * TS].rearrange("p (b t) -> p b t", b=B), repeat(k.ps[5][:, 0:TS], 1, B), -1.0,
                                             k.c("s_cols").rearrange("p (b t) -> p b t", b=B), ALU.mult, ALU.mult).then_inc(s["operand"], 1)
                    dve.wait_ge(s["u_kept"], tile + 1)
                    for half in range(2):
                        last = dve.tensor_tensor(grp[0:TS, 5 + half, :].rearrange("p (b v) -> p b v", b=4), repeat(u[0:TS, :], 1, 4),
                                                 repeat(k.c("s_rows")[0:TS, 4 * half:4 * half + 4], 2, P), ALU.mult)
                    last.then_inc(s["um_ready"], 1)
                    dve.wait_ge(s["s_made"], tile + 1)
                    d.after(dve.tensor_tensor(S0, S0, repeat(g_exp[:, T + L - 1::L], 2, P), ALU.mult))
                    dve.wait_ge(s["sn_made"], 1)
                    for half in range(2):
                        last = dve.tensor_tensor(S0[:, 4 * half:4 * half + 4, :], S0[:, 4 * half:4 * half + 4, :],
                                                 k.ps[1 + half].rearrange("p (b v) -> p b v", b=4), ALU.add)
                    last.then_inc(s["sn_kept"], 1)
            dve.wait_ge(s["o_kept"], TILES + 1)
            dve.tensor_tensor(sq, O, O, ALU.mult).then_inc(s["post_sq"], 1)
            dve.wait_ge(s["post_root"], 1)
            d.after(dve.scalar_tensor_tensor(O, O, k.vec[:, 0:1], sq, ALU.mult, ALU.mult))
            dve.wait_ge(s["gate_done"], 1)
            dve.tensor_tensor(O, O, Q[:, 3, :], ALU.mult).then_inc(s["post_ready"], 1)

        @block.scalar
        def _(act):
            a = Order(act, s["act_order"])
            act.wait_ge(w_sems[3], 4 * NC)
            act.activation(Q[:, 3, :], Q[:, 3, :], ACT.Silu).then_inc(s["gate_done"], 1)
            for m in range(3):
                act.wait_ge(s["conv_done"], m + 1)
                act.activation(Q[:, m, :], Q[:, m, :], ACT.Silu).then_inc(s["silu_done"], 1)
            act.wait_ge(s["silu_done"], 3)
            for m in range(2):
                if m:
                    act.wait_ge(s["normed"], 1)
                else:
                    act.wait_ge(s["conv_out"], 1)
                act.activation(sq, Q[:, m, :], ACT.Square).then_inc(s["sq_done"], 1)
                act.wait_ge(s["ss_done"], m + 1)
                for n in range(NC):
                    last = act.activation(sq[:, n * CH:(n + 1) * CH], k.ps[n][:, 0:CH], ACT.Ln, bias=k.eps)
                    last.then_inc(s["ln_done"], 1)
                act.wait_ge(s["ln_done"], (m + 1) * NC)
                if m == 0:
                    act.wait_ge(s["g_loaded"], 16)
                    act.activation(g_exp, g_row, ACT.Exp)
                    act.activation(hcol[:, 2, :], hcol[:, 1, :], ACT.Exp).then_inc(s["exp_out"], 1)
                act.activation(sq, sq, ACT.Exp, scale=-0.5).then_inc(s["root_done"], 1)
            tile = 0
            for gi, (t0, ng, w) in enumerate(groups):
                act.wait_ge(s["exp_in"], 2 * gi + 1)
                act.activation(X1[0:w, 0:ng * w], X1[0:w, 0:ng * w], ACT.Exp, scale=-1.0).then_inc(s["exp_out"], 1)
                act.wait_ge(s["exp_in"], 2 * gi + 2)
                act.activation(DT[0:w, 0:ng * w], DT[0:w, 0:ng * w], ACT.Exp).then_inc(s["exp_out"], 1)
                for i in range(ng):
                    act.wait_ge(s["u_made"], tile + 1)
                    if tile:
                        act.wait_ge(s["s_made"], tile)
                    act.copy(u[0:w, :], k.ps[0][0:w, 0:P]).then_inc(s["u_kept"], 1)
                    act.wait_ge(s["s_made"], tile + 1)
                    act.copy(O[:, t0 + i * w:t0 + (i + 1) * w], k.ps[7][:, 0:w]).then_inc(s["o_kept"], 1)
                    tile += 1
            act.wait_ge(s["post_ss"], 1)
            for n in range(NC):
                last = act.activation(sq[:, n * CH:(n + 1) * CH], k.ps[n][:, 0:CH], ACT.Ln, bias=k.eps, scale=1.0 / P)
            a.after(last)
            act.activation(sq, sq, ACT.Exp, scale=-0.5).then_inc(s["post_root"], 1)
    clear(nc, w_sems + list(s.values()))


def head_B(nc, k, io, h):
    with ExitStack() as c:
        sbuf = lambda n, s: c.enter_context(nc.sbuf_tensor(n, s, F32))[:]
        sem = lambda n: c.enter_context(nc.semaphore(n))
        ret = sbuf("ret", [P, RET])
        buf = sbuf("retbuf", [P, 2, 3, G * P])
        R = sbuf("R", [P, 2, P])
        R0 = sbuf("R0", [P, B, P])
        vm = sbuf("vm", [TS, B, P])
        sq, O, mean = sbuf("sqB", [P, NT]), sbuf("OB", [P, NT]), k.qd
        bn = sbuf("bn", [P, 1])
        Q = k.qkvz
        qd = k.qd
        w_sems, p_sync, p_pool, p_tensor, p_vector = project_head(
            nc, k, io, c, 0, "B", h, lambda m, n: [(Q[:, m, n * CH:(n + 1) * CH], 0, CH)])
        names = ["ret_loaded", "r0_loaded", "qd_ready", "turned_b", "tiles_b", "o_made", "r_made", "r_kept", "o_kept_b",
                 "so_made", "rn_made", "rn_kept", "gate_b", "mean_in", "mean_out", "var_in", "var_out", "root_b", "post_b",
                 "stored_b", "order_b", "act_b"]
        s = {n: sem(n) for n in names}
        block = c.enter_context(nc.Block())
        groups = [(g * G * P, G, P) for g in range(TILES // G)] + [(T, 1, TS)]

        @block.sync
        def _(sp):
            p_sync(sp)
            sp.dma_start(ret, io.c_ret[bass.ds(h, 1)].rearrange("o p n -> (o p) n")).then_inc(s["ret_loaded"], 16)
            sp.dma_start(R0, io.state_ret[0, :, bass.ds(h, 1), :, :].rearrange("b o k v -> k (b o) v")).then_inc(s["r0_loaded"], 16)
            sp.wait_ge(s["r_kept"], TILES)
            sp.dma_start(io.out_ret_prompt[0, 0, bass.ds(h, 1)].rearrange("o k v -> (o k) v"), R[:, TILES % 2, :]).then_inc(s["stored_b"], 16)
            sp.wait_ge(s["rn_kept"], 1)
            sp.dma_start(io.out_ret_sample[0, :, bass.ds(h, 1), :, :].rearrange("b o k v -> k (b o) v"), R0).then_inc(s["stored_b"], 16)
            sp.wait_ge(s["post_b"], 1)
            sp.dma_start(io.scr_o[bass.ds(h + H, 1)].rearrange("o p n -> (o p) n"), O).then_inc(s["stored_b"], 16)
            sp.wait_ge(s["stored_b"], 16 * 3)

        @block.gpsimd
        def _(pool):
            p_pool(pool)

        @block.tensor
        def _(pe):
            p_tensor(pe)
            tile = 0
            for gi, (t0, ng, w) in enumerate(groups):
                hs = [slice(i * P, (i + 1) * P) for i in range(ng)]
                sl = [slice(i * w, (i + 1) * w) for i in range(ng)]
                tok = [slice(t0 + i * w, t0 + (i + 1) * w) for i in range(ng)]
                Ktl, V, PT = [buf[:, gi % 2, i, :] for i in range(3)]
                pe.wait_ge(s["qd_ready"], 1)
                if gi:
                    pe.wait_ge(s["tiles_b"], gi)
                for i in range(ng):
                    pe.transpose(k.ps[2][0:w, hs[i]], Q[:, 1, tok[i]], k.c("ident"))
                    pe.transpose(k.ps[3][0:w, hs[i]], Q[:, 2, tok[i]], k.c("ident"))
                    last = pe.matmul(k.ps[4][0:w, sl[i]], Q[:, 1, tok[i]], Q[:, 0, tok[i]], start=True, stop=True)
                last.then_inc(s["turned_b"], 1)
                pe.wait_ge(s["tiles_b"], gi + 1)
                if w == P:
                    for i in range(ng):
                        if tile >= 2:
                            pe.wait_ge(s["r_kept"], tile - 1)
                        pe.matmul(k.ps[tile % 2][:, 0:P], Ktl[:, hs[i]], V[:, hs[i]], start=True, stop=True).then_inc(s["r_made"], 1)
                        if tile >= 2:
                            pe.wait_ge(s["o_kept_b"], tile - 1)
                        pe.matmul(k.ps[6 + tile % 2][:, 0:P], V[:, hs[i]], PT[:, sl[i]], start=True, stop=False)
                        pe.wait_ge(s["r_kept"], tile) if tile else None
                        pe.matmul(k.ps[6 + tile % 2][:, 0:P], R[:, tile % 2, :], qd[:, tok[i]], start=False, stop=True).then_inc(s["o_made"], 1)
                        tile += 1
                else:
                    pe.wait_ge(s["r0_loaded"], 16)
                    pe.wait_ge(s["o_kept_b"], tile)
                    pe.wait_ge(s["r_kept"], tile)
                    pe.matmul(k.ps[6][:, 0:TS], V[0:TS, 0:P], PT[0:TS, 0:TS], start=True, stop=False)
                    for b in range(B):
                        last = pe.matmul(k.ps[6][:, b * L:(b + 1) * L], R0[:, b, :], qd[:, T + b * L:T + (b + 1) * L],
                                         start=False, stop=(b == B - 1))
                    last.then_inc(s["o_made"], 1)
                    for half in range(2):
                        last = pe.matmul(k.ps[half], Ktl[0:TS, 0:P], vm[:, 4 * half:4 * half + 4, :].rearrange("p b v -> p (b v)"),
                                         start=True, stop=True)
                    last.then_inc(s["rn_made"], 1)
            pe.wait_ge(s["rn_kept"], 1)
            pe.wait_ge(s["o_kept_b"], TILES + 1)
            feature_sums(pe, k, O).then_inc(s["mean_in"], 1)
            pe.wait_ge(s["var_in"], 1)
            feature_sums(pe, k, sq).then_inc(s["var_out"], 1)

        @block.vector
        def _(dve):
            d = Order(dve, s["order_b"])
            dve.memset(R[:, 0, :], 0.0)
            dve.tensor_copy(bn, k.b_norm[:, bass.ds(h, 1)])
            p_vector(dve)
            dve.wait_ge(w_sems[3], 4 * NC)
            dve.wait_ge(s["ret_loaded"], 16)
            dve.tensor_tensor(qd[:, 0:T].rearrange("p (t n) -> p t n", n=P), Q[:, 0, 0:T].rearrange("p (t n) -> p t n", n=P),
                              repeat(ret[:, P:2 * P], 1, TILES), ALU.mult)
            dve.tensor_tensor(qd[:, T:NT], Q[:, 0, T:NT], ret[:, 290:322], ALU.mult).then_inc(s["qd_ready"], 1)
            tile = 0
            for gi, (t0, ng, w) in enumerate(groups):
                Ktl, V, PT = [buf[:, gi % 2, i, :] for i in range(3)]
                dve.wait_ge(s["turned_b"], gi + 1)
                if w == P:
                    if gi >= 2:
                        dve.wait_ge(s["o_made"], (gi - 1) * G)
                    dve.tensor_copy(V, k.ps[3])
                    dve.tensor_scalar(Ktl, k.ps[2], ret[:, 256:257], None, ALU.mult)
                    dve.tensor_tensor(PT.rearrange("p (g n) -> p g n", g=G), k.ps[4].rearrange("p (g n) -> p g n", g=G),
                                      repeat(ret[:, 0:P], 1, G), ALU.mult).then_inc(s["tiles_b"], 1)
                    for i in range(ng):
                        dve.wait_ge(s["r_made"], tile + 1)
                        if tile >= 1:
                            dve.wait_ge(s["o_made"], tile)
                            dve.wait_ge(s["r_kept"], tile)
                        dve.scalar_tensor_tensor(R[:, (tile + 1) % 2, :], R[:, tile % 2, :], ret[:, 257:258], k.ps[tile % 2][:, 0:P],
                                                 ALU.mult, ALU.add).then_inc(s["r_kept"], 1)
                        tile += 1
                else:
                    d.after(dve.tensor_copy(V[0:TS, 0:P], k.ps[3][0:TS, 0:P]))
                    dve.tensor_tensor(vm, repeat(V[0:TS, 0:P], 1, B), repeat(k.c("s_rows")[0:TS, :], 2, P), ALU.mult)
                    dve.tensor_scalar(Ktl[0:TS, 0:P], k.ps[2][0:TS, 0:P], ret[0:TS, 322:323], None, ALU.mult)
                    dve.tensor_tensor(PT[0:TS, 0:TS], k.ps[4][0:TS, 0:TS], ret[0:TS, 258:290], ALU.mult).then_inc(s["tiles_b"], 1)
                    dve.wait_ge(s["rn_made"], 1)
                    for half in range(2):
                        last = dve.scalar_tensor_tensor(R0[:, 4 * half:4 * half + 4, :], R0[:, 4 * half:4 * half + 4, :], ret[:, 323:324],
                                                        k.ps[half].rearrange("p (b v) -> p b v", b=4), ALU.mult, ALU.add)
                    last.then_inc(s["rn_kept"], 1)
            dve.wait_ge(s["mean_in"], 1)
            for n in range(NC):
                a, b = n * CH, (n + 1) * CH
                last = dve.scalar_tensor_tensor(O[:, a:b], k.ps[n][:, 0:CH], -1.0 / P, O[:, a:b], ALU.mult, ALU.add)
            d.after(last)
            dve.tensor_tensor(sq, O, O, ALU.mult).then_inc(s["var_in"], 1)
            dve.wait_ge(s["root_b"], 1)
            d.after(dve.scalar_tensor_tensor(O, O, bn, sq, ALU.mult, ALU.mult))
            dve.wait_ge(s["gate_b"], 1)
            dve.tensor_tensor(O, O, Q[:, 3, :], ALU.mult).then_inc(s["post_b"], 1)

        @block.scalar
        def _(act):
            a = Order(act, s["act_b"])
            act.wait_ge(w_sems[3], 4 * NC)
            act.activation(Q[:, 3, :], Q[:, 3, :], ACT.Silu).then_inc(s["gate_b"], 1)
            tile = 0
            for gi, (t0, ng, w) in enumerate(groups):
                for i in range(ng):
                    act.wait_ge(s["o_made"], tile + 1)
                    act.copy(O[:, t0 + i * w:t0 + (i + 1) * w], k.ps[6 + tile % 2][:, 0:w]).then_inc(s["o_kept_b"], 1)
                    tile += 1
            act.wait_ge(s["var_out"], 1)
            for n in range(NC):
                last = act.activation(sq[:, n * CH:(n + 1) * CH], k.ps[n][:, 0:CH], ACT.Ln, bias=k.eps, scale=1.0 / P)
            a.after(last)
            act.activation(sq, sq, ACT.Exp, scale=-0.5).then_inc(s["root_b"], 1)
    clear(nc, w_sems + list(s.values()))


def output_projection(nc, k, io, layer):
    with ExitStack() as c:
        sem = lambda n: c.enter_context(nc.semaphore(f"{n}_{layer}"))
        wout = c.enter_context(nc.sbuf_tensor(f"wout{layer}", [P, KT, D_MODEL], F32))[:]
        o = k.big[:, 0:2 * KT * CH].rearrange("p (s k n) -> p s k n", s=2, k=KT)
        wo_loaded, o_loaded = sem("wo_loaded"), [sem("o_loaded0"), sem("o_loaded1")]
        y_made, y_added = sem("y_made"), sem("y_added")
        block = c.enter_context(nc.Block())
        w = io.w_out_even[0] if layer == 0 else io.w_out_odd[0]

        @block.sync
        def _(sp):
            sp.dma_start(wout, w.rearrange("(k p) n -> p k n", p=P)).then_inc(wo_loaded, 16)
            for n in range(NC):
                if n >= 2:
                    sp.wait_ge(y_made, (n - 1) * KT)
                sp.dma_start(o[:, n % 2], io.scr_o[:, :, n * CH:(n + 1) * CH].rearrange("k p n -> p k n")).then_inc(o_loaded[n % 2], 16)

        @block.tensor
        def _(pe):
            pe.wait_ge(wo_loaded, 16)
            for n in range(NC):
                pe.wait_ge(o_loaded[n % 2], 16 * (n // 2 + 1))
                for m in range(KT):
                    at = n * KT + m
                    if at >= 4:
                        pe.wait_ge(y_added, at - 3)
                    for j in range(KT):
                        last = pe.matmul(k.ps[at % 4][:, 0:CH], wout[:, j, m * P:(m + 1) * P], o[:, n % 2, j, :],
                                         start=(j == 0), stop=(j == KT - 1))
                    last.then_inc(y_made, 1)

        @block.vector
        def _(dve):
            for n in range(NC):
                for m in range(KT):
                    at = n * KT + m
                    dve.wait_ge(y_made, at + 1)
                    x = k.xT[:, m, n * CH:(n + 1) * CH]
                    dve.tensor_tensor(x, x, k.ps[at % 4][:, 0:CH], ALU.add).then_inc(y_added, 1)
    clear(nc, [wo_loaded, *o_loaded, y_made, y_added])


def row_gates_odd(nc, k, io):
    with ExitStack() as c:
        sem = lambda n: c.enter_context(nc.semaphore(n))
        w_loaded, w_scaled = sem("fw_loaded"), sem("fw_scaled")
        row_ready, row_taken = sem("f_row_ready"), sem("f_row_taken")
        a_step, d_step = sem("f_act"), sem("f_dve")
        turned, cols_ready, stored = sem("f_turned"), sem("f_cols"), sem("f_stored")
        w = c.enter_context(nc.sbuf_tensor("fw", [P, KT, 4], F32))
        rows = c.enter_context(nc.sbuf_tensor("frows", [4, NT], F32))
        tmp = c.enter_context(nc.sbuf_tensor("ftmp", [4, NT], F32))
        one = c.enter_context(nc.sbuf_tensor("fones", [4, T], F32))
        block = c.enter_context(nc.Block())

        @block.sync
        def _(sp):
            sp.dma_start(w[:, :, :], io.w_in_odd[0].rearrange("(k p) c -> p k c", p=P)[:, :, 2048:2052]).then_inc(w_loaded, 16)
            sp.wait_ge(d_step, 4)
            sp.dma_start(io.scr_f, tmp[:, 0:T]).then_inc(stored, 16)
            sp.wait_ge(cols_ready, 1)
            sp.dma_start(io.out_fox_logf_prompt[0, 0].rearrange("(t p) h -> p t h", p=P), k.logf_cols[:, 0:TILES, :]).then_inc(stored, 16)
            sp.dma_start(io.out_fox_logf_sample.rearrange("b o l h -> (b o l) h"), k.logf_cols[0:TS, TILES, :]).then_inc(stored, 16)
            sp.wait_ge(stored, 48)

        @block.vector
        def _(dve):
            dve.memset(one[:, :], 1.0)
            dve.wait_ge(w_loaded, 16)
            dve.tensor_tensor(w[:, :, :], w[:, :, :], repeat(k.g_odd, 2, 4), ALU.mult).then_inc(w_scaled, 1)
            for n in range(NC):
                dve.wait_ge(row_ready, n + 1)
                dve.tensor_tensor(rows[:, n * CH:(n + 1) * CH], k.ps[n % 2][0:4, 0:CH], k.rstd[0:4, n * CH:(n + 1) * CH],
                                  ALU.mult).then_inc(row_taken, 1)
            dve.wait_ge(a_step, 3)
            dve.tensor_scalar(rows[:, :], rows[:, :], k.small[0:4, 2:3], 0.0, ALU.add, ALU.min).then_inc(d_step, 1)
            dve.wait_ge(d_step, 1)
            dve.tensor_tensor(rows[:, :], rows[:, :], tmp[:, :], ALU.subtract).then_inc(d_step, 1)
            dve.wait_ge(d_step, 2)
            dve.tensor_tensor_scan(tmp[:, 0:T], one[:, :], rows[:, 0:T], 0.0, ALU.mult, ALU.add).then_inc(d_step, 1)
            dve.wait_ge(d_step, 3)
            dve.tensor_scalar(tmp[:, 0:T], tmp[:, 0:T], -1.0, None, ALU.mult).then_inc(d_step, 1)
            dve.wait_ge(turned, 1)
            dve.tensor_copy(k.logf_cols.rearrange("p t h -> p (t h)"), k.ps[2][:, 0:68]).then_inc(cols_ready, 1)

        @block.scalar
        def _(act):
            act.wait_ge(row_taken, NC)
            act.activation(tmp[:, :], rows[:, :], ACT.Abs, bias=k.small[0:4, 2:3]).then_inc(a_step, 1)
            act.wait_ge(a_step, 1)
            act.activation(tmp[:, :], tmp[:, :], ACT.Exp, scale=-1.0).then_inc(a_step, 1)
            act.wait_ge(a_step, 2)
            act.activation(tmp[:, :], tmp[:, :], ACT.Ln, bias=k.one[0:4, :]).then_inc(a_step, 1)

        @block.tensor
        def _(pe):
            pe.wait_ge(w_scaled, 1)
            for n in range(NC):
                if n >= 2:
                    pe.wait_ge(row_taken, n - 1)
                for j in range(KT):
                    last = pe.matmul(k.ps[n % 2][0:4, 0:CH], w[:, j, :], k.xT[:, j, n * CH:(n + 1) * CH],
                                     start=(j == 0), stop=(j == KT - 1))
                last.then_inc(row_ready, 1)
            pe.wait_ge(d_step, 2)
            pe.matmul(k.ps[2][:, 0:68], k.c("ones"), k.zero[:, 0:68], start=True, stop=True)
            for t in range(TILES + 1):
                m = P if t < TILES else TS
                last = pe.transpose(k.ps[2][0:m, 4 * t:4 * t + 4], rows[:, t * P:t * P + m], k.c("ident")[0:4, 0:4])
            last.then_inc(turned, 1)
    clear(nc, [w_loaded, w_scaled, row_ready, row_taken, a_step, d_step, turned, cols_ready, stored])


def head_attention(nc, k, io, h, branch):
    with ExitStack() as c:
        sbuf = lambda n, s: c.enter_context(nc.sbuf_tensor(f"{n}{branch}", s, F32))[:]
        sem = lambda n: c.enter_context(nc.semaphore(f"{n}_{branch}"))
        fox = branch == "C"
        ktok, vtok = sbuf("ktok", [P, TILES + 1, P]), sbuf("vtok", [P, TILES + 1, P])
        bias = sbuf("bias", [P, T])
        sc = sbuf("sc", [P, 2, T])
        wt = sbuf("wt", [P, 2, G * P])
        otok = sbuf("otok", [P, P])
        stat = sbuf("stat", [P, 2, 4])
        sq = sc[:, 0:2, :].rearrange("p a n -> p (a n)")[:, 0:NT]
        O = k.qd
        Q = k.qkvz
        keep = k.foxs if fox else k.wins
        gq, gk = (k.vec[:, 1:2], k.vec[:, 2:3]) if fox else (k.vec[:, 3:4], k.vec[:, 4:5])
        w_sems, p_sync, p_pool, p_tensor, p_vector = project_head(
            nc, k, io, c, 1, branch, h, lambda m, n: [(Q[:, m, n * CH:(n + 1) * CH], 0, CH)])
        names = ["bias_loaded", "sq_done", "ss_done", "ln_done", "root_done", "normed", "gate_done", "kv_turned", "kv_kept",
                 "scores_made", "scores_kept", "max_ready", "exp_done", "wt_made", "wt_kept", "o_made", "recip_ready",
                 "otok_ready", "o_turned", "o_done", "kept", "stored", "order", "neg_order"]
        s = {n: sem(n) for n in names}
        block = c.enter_context(nc.Block())
        kout, vout, ks, vs = ((io.out_fox_k_prompt[0, 0], io.out_fox_v_prompt[0, 0],
                               io.out_fox_k_sample.rearrange("b o l h d -> (b o l) h d"), io.out_fox_v_sample.rearrange("b o l h d -> (b o l) h d"))
                              if fox else (io.out_win_k_prompt[0, 0], io.out_win_v_prompt[0, 0], None, None))
        chunks = [(i, j, min(G, i + 1 - j)) for i in range(TILES) for j in range(0, i + 1, G)]

        @block.sync
        def _(sp):
            p_sync(sp)
            src = io.scr_f[bass.ds(h, 1), :].broadcast_to([P, T]) if fox else io.c_window[bass.ds(h, 1)].rearrange("o p n -> (o p) n")
            sp.dma_start(bias, src).then_inc(s["bias_loaded"], 16)
            sp.wait_ge(s["kv_kept"], 10)
            n = 2
            for dst, ap in ((kout, ktok), (vout, vtok)):
                sp.dma_start(dst[:, bass.ds(h, 1), :].rearrange("(t p) o d -> p t (o d)", p=P), ap[:, 0:TILES, :]).then_inc(s["stored"], 16)
            if fox:
                for dst, ap in ((ks, ktok), (vs, vtok)):
                    sp.dma_start(dst[:, bass.ds(h, 1), :].rearrange("t o d -> t (o d)"), ap[0:TS, TILES, :]).then_inc(s["stored"], 16)
            else:
                for dst, ap in ((io.out_win_k_sample, ktok), (io.out_win_v_sample, vtok)):
                    for b in range(B):
                        sp.dma_start(dst[0, b, WBUF - L:WBUF, bass.ds(h, 1), :].rearrange("l o d -> l (o d)"), ap[b * L:(b + 1) * L, TILES, :]).then_inc(s["stored"], 16)
            sp.wait_ge(s["o_done"], TILES)
            sp.dma_start(io.scr_o[bass.ds(h + (0 if fox else H), 1)].rearrange("o p n -> (o p) n")[:, 0:T], O[:, 0:T]).then_inc(s["stored"], 16)
            sp.wait_ge(s["stored"], 16 * (2 + (2 if fox else 2 * B) + 1))

        @block.gpsimd
        def _(pool):
            p_pool(pool)

        @block.tensor
        def _(pe):
            p_tensor(pe)
            for m in range(2):
                pe.wait_ge(s["sq_done"], m + 1)
                if m:
                    pe.wait_ge(s["ln_done"], NC)
                feature_sums(pe, k, sq).then_inc(s["ss_done"], 1)
            pe.wait_ge(s["normed"], 2)
            for g in range(5):
                ts = range(4 * g, min(4 * g + 4, TILES + 1))
                for which in range(2):
                    at = 2 * g + which
                    if at >= 2:
                        pe.wait_ge(s["kv_kept"], at - 1)
                    for t in ts:
                        w = P if t < TILES else TS
                        last = pe.transpose(k.ps[5 + which][0:w, (t % 4) * P:(t % 4 + 1) * P], Q[:, 1 + which, t * P:t * P + w], k.c("ident"))
                    last.then_inc(s["kv_turned"], 1)
            pe.wait_ge(s["kv_kept"], 10)

            def scores(i):
                if i:
                    pe.wait_ge(s["scores_kept"], i)
                qt = Q[:, 0, i * P:(i + 1) * P]
                for j in range(0, i + 1, G):
                    n = min(G, i + 1 - j) * P
                    diag = fox and j + G > i
                    last = pe.matmul(k.ps4[:, j * P:j * P + n], qt, Q[:, 1, j * P:j * P + n], start=True, stop=not diag)
                    if diag:
                        last = pe.matmul(k.ps4[:, i * P:(i + 1) * P], k.c("ident"), k.c("causal_bias"), start=False, stop=True)
                last.then_inc(s["scores_made"], 1)

            scores(0)
            at = 0
            for i in range(TILES):
                if i + 1 < TILES:
                    scores(i + 1)
                pe.wait_ge(s["exp_done"], i + 1)
                if i:
                    pe.wait_ge(s["otok_ready"], i)
                mine = [x for x in chunks if x[0] == i]
                for step in range(len(mine) + 1):
                    if step < len(mine):
                        _, j, n = mine[step]
                        if at >= 2:
                            pe.wait_ge(s["wt_kept"], at - 1)
                        for jj in range(n):
                            last = pe.transpose(k.ps[4 + at % 2][:, jj * P:(jj + 1) * P], sc[:, i % 2, (j + jj) * P:(j + jj + 1) * P], k.c("ident"))
                        last.then_inc(s["wt_made"], 1)
                        at += 1
                    if step:
                        _, j, n = mine[step - 1]
                        prev = at - (1 if step == len(mine) else 2)
                        pe.wait_ge(s["wt_kept"], prev + 1)
                        for jj in range(n):
                            last = pe.matmul(k.ps[6][:, 0:P], wt[:, prev % 2, jj * P:(jj + 1) * P], vtok[:, j + jj, :],
                                             start=(j + jj == 0), stop=(j + jj == i))
                last.then_inc(s["o_made"], 1)
                pe.wait_ge(s["otok_ready"], i + 1)
                if i:
                    pe.wait_ge(s["o_done"], i)
                pe.transpose(k.ps[7][:, 0:P], otok, k.c("ident")).then_inc(s["o_turned"], 1)

        @block.vector
        def _(dve):
            d = Order(dve, s["order"])
            p_vector(dve)
            dve.wait_ge(w_sems[3], 4 * NC)
            for m in range(2):
                dve.wait_ge(s["root_done"], m + 1)
                if m == 0:
                    dve.tensor_scalar(stat[:, 0, 0:1], gq, SCALE, None, ALU.mult).then_inc(s["neg_order"], 1)
                    dve.wait_ge(s["neg_order"], 1)
                dve.scalar_tensor_tensor(Q[:, m, :], Q[:, m, :], stat[:, 0, 0:1] if m == 0 else gk, sq, ALU.mult, ALU.mult).then_inc(s["normed"], 1)
            for g in range(5):
                n = 4 if g < 4 else 1
                w = P if g < 4 else TS
                for which, dst in ((0, ktok), (1, vtok)):
                    dve.wait_ge(s["kv_turned"], 2 * g + which + 1)
                    dve.tensor_copy(dst[0:w, 4 * g:4 * g + n, :], k.ps[5 + which][0:w, 0:n * P].rearrange("p (t d) -> p t d", t=n)).then_inc(s["kv_kept"], 1)
            dve.wait_ge(s["normed"], 2)
            dve.wait_ge(s["gate_done"], 1)
            dve.wait_ge(s["kv_kept"], 10)
            for which, src in ((0, Q[:, 0, T:NT]), (1, Q[:, 1, T:NT]), (2, Q[:, 3, T:NT])):
                dve.tensor_copy(keep[:, which, bass.ds(h, 1), :].rearrange("p o t -> p (o t)"), src)
            dve.tensor_copy((k.foxv if fox else k.winv)[:, bass.ds(h, 1), :].rearrange("t o d -> t (o d)"), vtok[0:TS, TILES, :])
            dve.wait_ge(s["bias_loaded"], 16)

            def soften(i):
                n = (i + 1) * P
                dve.wait_ge(s["scores_made"], i + 1)
                if i >= 2:
                    dve.wait_ge(s["o_made"], i - 1)
                b = bias[:, 0:n] if fox else bias[:, T - n:T]
                dve.tensor_tensor(sc[:, i % 2, 0:n], k.ps4[:, 0:n], b, ALU.add).then_inc(s["scores_kept"], 1)
                dve.wait_ge(s["scores_kept"], i + 1)
                d.after(dve.tensor_reduce(stat[:, i % 2, 0:1], sc[:, i % 2, 0:n], X, ALU.max))
                dve.tensor_scalar(stat[:, i % 2, 1:2], stat[:, i % 2, 0:1], -1.0, None, ALU.mult).then_inc(s["max_ready"], 1)

            soften(0)
            at = 0
            for i in range(TILES):
                if i + 1 < TILES:
                    soften(i + 1)
                for _, j, n in [x for x in chunks if x[0] == i]:
                    dve.wait_ge(s["wt_made"], at + 1)
                    dve.tensor_copy(wt[:, at % 2, 0:n * P], k.ps[4 + at % 2][:, 0:n * P]).then_inc(s["wt_kept"], 1)
                    at += 1
                dve.wait_ge(s["exp_done"], i + 1)
                dve.reciprocal(stat[:, i % 2, 3:4], stat[:, i % 2, 2:3]).then_inc(s["recip_ready"], 1)
                dve.wait_ge(s["recip_ready"], i + 1)
                dve.wait_ge(s["o_made"], i + 1)
                dve.tensor_scalar(otok, k.ps[6][:, 0:P], stat[:, i % 2, 3:4], None, ALU.mult).then_inc(s["otok_ready"], 1)
                dve.wait_ge(s["o_turned"], i + 1)
                dve.tensor_tensor(O[:, i * P:(i + 1) * P], k.ps[7][:, 0:P], Q[:, 3, i * P:(i + 1) * P], ALU.mult).then_inc(s["o_done"], 1)

        @block.scalar
        def _(act):
            act.wait_ge(w_sems[3], 4 * NC)
            act.activation(Q[:, 3, :], Q[:, 3, :], ACT.Silu).then_inc(s["gate_done"], 1)
            for m in range(2):
                if m:
                    act.wait_ge(s["normed"], 1)
                act.activation(sq, Q[:, m, :], ACT.Square).then_inc(s["sq_done"], 1)
                act.wait_ge(s["ss_done"], m + 1)
                for n in range(NC):
                    act.activation(sq[:, n * CH:(n + 1) * CH], k.ps[n][:, 0:CH], ACT.Ln, bias=k.eps, scale=1.0 / P).then_inc(s["ln_done"], 1)
                act.wait_ge(s["ln_done"], (m + 1) * NC)
                act.activation(sq, sq, ACT.Exp, scale=-0.5).then_inc(s["root_done"], 1)
            for i in range(TILES):
                n = (i + 1) * P
                act.wait_ge(s["max_ready"], i + 1)
                act.activation(sc[:, i % 2, 0:n], sc[:, i % 2, 0:n], ACT.Exp, bias=stat[:, i % 2, 1:2],
                               accum_out=stat[:, i % 2, 2:3]).then_inc(s["exp_done"], 1)
    clear(nc, w_sems + list(s.values()))


def sample_new_scores(nc, k, io):
    with ExitStack() as c:
        sem = lambda n: c.enter_context(nc.semaphore(n))
        prefix, dot, negated, centred = sem("new_prefix"), sem("new_dot"), sem("new_negated"), sem("new_centred")
        col = c.enter_context(nc.sbuf_tensor("newcol", [TS, H], F32))[:]
        block = c.enter_context(nc.Block())

        @block.tensor
        def _(pe):
            pe.matmul(k.ps[0][0:TS, 0:H], k.c("s_prefix")[0:TS, :], k.logf_cols[0:TS, TILES, :], start=True, stop=True).then_inc(prefix, 1)
            for f, keep in enumerate((k.foxs, k.wins)):
                for hh in range(H):
                    last = pe.matmul(k.ps[1 + f][0:TS, hh * TS:(hh + 1) * TS], keep[:, 1, hh, :], keep[:, 0, hh, :], start=True, stop=True)
                last.then_inc(dot, 1)

        @block.vector
        def _(dve):
            dve.memset(k.sc_all[:, :, :], -BIG)
            dve.wait_ge(prefix, 1)
            dve.tensor_scalar(col, k.ps[0][0:TS, 0:H], -1.0, None, ALU.mult).then_inc(negated, 1)
            dve.wait_ge(dot, 2)
            dve.wait_ge(negated, 1)
            dve.tensor_tensor(k.snew[:, 0], k.ps[1][0:TS, 0:P].rearrange("p (h t) -> p h t", h=H), repeat(col, 2, TS), ALU.add).then_inc(centred, 1)
            dve.wait_ge(centred, 1)
            dve.tensor_tensor(k.snew[:, 0], k.snew[:, 0], repeat(k.c("s_bias")[0:TS, :], 1, H), ALU.add)
            dve.tensor_tensor(k.snew[:, 1], k.ps[2][0:TS, 0:P].rearrange("p (h t) -> p h t", h=H),
                              k.c("s_window")[0:TS, :].rearrange("p (h t) -> p h t", h=H), ALU.add)
    clear(nc, [prefix, dot, negated, centred])


def sample_attention(nc, k, io, b):
    with ExitStack() as c:
        sbuf = lambda n, s: c.enter_context(nc.sbuf_tensor(n, s, F32))[:]
        sem = lambda n: c.enter_context(nc.semaphore(n))
        RING = 4
        ITEMS = NPG + WT
        GR = 4 * H
        kring, kt = sbuf("kring", [P, RING, HD]), sbuf("kt", [P, 2, HD])
        vextra = sbuf("vextra", [P, 4 + WT, HD])
        vslot = [k.big[:, i * HD:(i + 1) * HD] for i in range(28)] + [vextra[:, i, :] for i in range(4)]
        vwin = [vextra[:, 4 + i, :] for i in range(WT)]
        pr = sbuf("pr", [P, NPG + 1 + WT + 1, GR])
        qb = sbuf("qb", [P, 2, GR])
        lfp = sbuf("lfp", [NPG, PAGE * H])
        lft, pre, later, fbias = sbuf("lft", [P, H * NPG]), sbuf("pre", [P, H * NPG]), sbuf("later", [P, H * NPG]), sbuf("fbias", [P, H * NPG])
        mx, mrow, mdiag, rs = sbuf("mx", [P, 2 * GR]), sbuf("mrow", [2 * GR, 1]), sbuf("mdiag", [2 * GR, 2 * GR]), sbuf("rs", [P, 2 * GR])
        ov, res = sbuf("ov", [GR, 2, HD]), sbuf("res", [P, 2, GR])
        k_loaded = [sem(f"k_loaded{i}") for i in range(RING)]
        names = ["v_loaded", "vw_loaded", "lf_loaded", "k_turned", "kt_kept_v", "kt_kept_s", "scored", "q_ready",
                 "lf_turned", "lf_kept", "later_ready", "fbias_made", "max_cols", "max_turned", "max_diag", "max_made",
                 "shifted", "exp_done", "sums_ready", "sums_made", "pv_made", "ov_ready", "ot_made", "done", "order"]
        s = {n: sem(n) for n in names}
        block = c.enter_context(nc.Block())
        sc = k.sc_all
        kf, vf = io.cache_fox_k.rearrange("n o t h d -> n t (o h d)"), io.cache_fox_v.rearrange("n o t h d -> n t (o h d)")
        lf = io.cache_fox_logf.rearrange("n o t h -> n (o t h)")
        kw, vw = (a[0].rearrange("b r h d -> b r (h d)") for a in (io.cache_win_k, io.cache_win_v))

        def window_tile(src, i):
            if i < 3:
                return src[bass.ds(b, 1), 512 * i:512 * (i + 1), :].rearrange("o (g r) c -> (o g) r c", r=16)[:, 0:4, :]
            return src[bass.ds(b, 1), 1536 + P * (i - 3):1536 + P * (i - 2), :].rearrange("o r c -> (o r) c")

        @block.sync
        def _(sp):
            for p in range(ITEMS):
                if p >= RING:
                    sp.wait_ge(s["k_turned"], p - RING + 1)
                if p < NPG:
                    page = sp.value_load(k.pages[0:1, bass.ds(b * NPG + p, 1)], min_val=0, max_val=NPHYS - 1)
                    sp.dma_start(kring[:, p % RING, :], kf[bass.ds(page, 1)].rearrange("o t c -> (o t) c")).then_inc(k_loaded[p % RING], 16)
                    sp.dma_start(lfp[p:p + 1, :], lf[bass.ds(page, 1), :]).then_inc(s["lf_loaded"], 16)
                else:
                    sp.dma_start(kring[:, p % RING, :], window_tile(kw, p - NPG)).then_inc(k_loaded[p % RING], 16)

        @block.tensor
        def _(pe):
            def kept(p):
                pe.wait_ge(s["kt_kept_s"] if p % 2 else s["kt_kept_v"], p // 2 + 1)

            def score(p):
                kept(p)
                if p == 0:
                    pe.wait_ge(s["q_ready"], 1)
                f = int(p >= NPG)
                at = GR * (p - NPG * f)
                for hh in range(H):
                    last = pe.matmul(k.ps[2 + f][:, at + 4 * hh:at + 4 * hh + 4], kt[:, p % 2, hh * P:(hh + 1) * P],
                                     qb[:, f, 4 * hh:4 * hh + 4], start=True, stop=True)
                last.then_inc(s["scored"], 1)

            for p in range(ITEMS):
                pe.wait_ge(k_loaded[p % RING], 16 * (p // RING + 1))
                if p >= 2:
                    kept(p - 2)
                for hh in range(H):
                    last = pe.transpose(k.ps[p % 2][:, hh * P:(hh + 1) * P], kring[:, p % RING, hh * P:(hh + 1) * P], k.c("ident"))
                last.then_inc(s["k_turned"], 1)
                if p:
                    score(p - 1)
            score(ITEMS - 1)
            pe.wait_ge(s["lf_loaded"], 16 * NPG)
            for hh in range(H):
                last = pe.transpose(k.ps[4][:, hh * NPG:(hh + 1) * NPG], lfp.rearrange("p (t h) -> p h t", h=H)[:, hh, :], k.c("ident")[0:NPG, 0:NPG])
            last.then_inc(s["lf_turned"], 1)
            pe.wait_ge(s["later_ready"], 1)
            pe.matmul(k.ps[5][:, 0:P], k.c("later"), lft, start=True, stop=False)
            pe.matmul(k.ps[5][:, 0:P], k.c("ones"), later, start=False, stop=True).then_inc(s["fbias_made"], 1)
            pe.wait_ge(s["max_cols"], 2)
            pe.transpose(k.ps[6][0:2 * GR, 0:P], mx, k.c("ident")).then_inc(s["max_turned"], 1)
            pe.wait_ge(s["max_diag"], 1)
            pe.matmul(k.ps[7][:, 0:2 * GR], k.c("ones")[0:2 * GR, :], mdiag, start=True, stop=True).then_inc(s["max_made"], 1)
            pe.wait_ge(s["exp_done"], 1)
            pe.wait_ge(s["v_loaded"], 16 * NPG)
            for p in range(NPG):
                pe.matmul(k.ps[0][0:GR, :], pr[:, p, :], vslot[p], start=(p == 0), stop=False)
            pe.matmul(k.ps[0][0:GR, :], pr[0:TS, NPG, :], k.foxv.rearrange("t h d -> t (h d)"), start=False, stop=True).then_inc(s["pv_made"], 1)
            pe.wait_ge(s["vw_loaded"], 16 * WT)
            for i in range(WT):
                pe.matmul(k.ps[1][0:GR, :], pr[:, NPG + 1 + i, :], vwin[i], start=(i == 0), stop=False)
            pe.matmul(k.ps[1][0:GR, :], pr[0:TS, NPG + 1 + WT, :], k.winv.rearrange("t h d -> t (h d)"), start=False, stop=True).then_inc(s["pv_made"], 1)
            pe.wait_ge(s["sums_ready"], 1)
            pe.matmul(k.ps[6][:, 0:2 * GR], k.c("ones"), mx, start=True, stop=True).then_inc(s["sums_made"], 1)
            for f in range(2):
                pe.wait_ge(s["ov_ready"], f + 1)
                for hh in range(H):
                    last = pe.matmul(k.ps[4 + f][:, 0:GR], ov[:, f, hh * P:(hh + 1) * P], k.c("ident")[0:GR, 0:GR],
                                     start=(hh == 0), stop=(hh == H - 1))
                last.then_inc(s["ot_made"], 1)

        @block.vector
        def _(dve):
            d = Order(dve, s["order"])
            for f, keep in enumerate((k.foxs, k.wins)):
                last = dve.tensor_copy(qb[:, f, :].rearrange("p (h q) -> p h q", h=H), keep[:, 0, :, bass.ds(b * L, L)])
            last.then_inc(s["q_ready"], 1)
            for f, blk in ((0, NPG), (1, NPG + 1 + WT)):
                dve.tensor_copy(sc[0:TS, blk, :].rearrange("p (h q) -> p h q", h=H), k.snew[:, f, :, bass.ds(b * L, L)])
            for p in range(0, ITEMS, 2):
                dve.wait_ge(s["k_turned"], p + 1)
                if p >= 2:
                    dve.wait_ge(s["scored"], p - 1)
                dve.tensor_copy(kt[:, 0, :], k.ps[0][:, :]).then_inc(s["kt_kept_v"], 1)
            dve.wait_ge(s["lf_turned"], 1)
            d.after(dve.tensor_copy(lft, k.ps[4][:, 0:P]))
            d.after(dve.tensor_tensor_scan(pre, k.c("page_reset"), lft, 0.0, ALU.mult, ALU.add))
            p3 = pre.rearrange("p (h n) -> p h n", h=H)
            dve.tensor_tensor(later.rearrange("p (h n) -> p h n", h=H), repeat(p3[:, :, NPG - 1], 2, NPG), p3, ALU.subtract).then_inc(s["later_ready"], 1)
            dve.wait_ge(s["fbias_made"], 1)
            d.after(dve.tensor_copy(fbias, k.ps[5][:, 0:P]))
            dve.wait_ge(s["scored"], ITEMS)
            dve.tensor_tensor(sc[:, 0:NPG, :].rearrange("p n (h q) -> p n h q", h=H), k.ps[2].rearrange("p (n h q) -> p n h q", n=NPG, h=H),
                              repeat(fbias.rearrange("p (h n) -> p n h", h=H), 3, L), ALU.add)
            d.after(dve.tensor_tensor(sc[:, NPG + 1:NPG + 1 + WT, :], k.ps[3][:, 0:WT * GR].rearrange("p (n g) -> p n g", n=WT),
                                      k.c("window_past").rearrange("p (n g) -> p n g", n=WT), ALU.add))
            parts = (slice(0, NPG + 1), slice(NPG + 1, NPG + 2 + WT))
            for f in range(2):
                dve.tensor_reduce(mx[:, f * GR:(f + 1) * GR], sc[:, parts[f], :].rearrange("p n g -> p g n"), X, ALU.max).then_inc(s["max_cols"], 1)
            dve.wait_ge(s["max_turned"], 1)
            d.after(dve.tensor_reduce(mrow, k.ps[6][0:2 * GR, 0:P], X, ALU.max))
            dve.tensor_scalar(mdiag, k.c("ident")[0:2 * GR, 0:2 * GR], mrow, None, ALU.mult).then_inc(s["max_diag"], 1)
            dve.wait_ge(s["max_made"], 1)
            for f in range(2):
                n = parts[f].stop - parts[f].start
                last = dve.tensor_tensor(pr[:, parts[f], :], sc[:, parts[f], :], repeat(k.ps[7][:, f * GR:(f + 1) * GR], 1, n), ALU.subtract)
            last.then_inc(s["shifted"], 1)
            dve.wait_ge(s["exp_done"], 1)
            for f in range(2):
                last = dve.tensor_reduce(mx[:, f * GR:(f + 1) * GR], pr[:, parts[f], :].rearrange("p n g -> p g n"), X, ALU.add)
            last.then_inc(s["sums_ready"], 1)
            for f in range(2):
                dve.wait_ge(s["pv_made"], f + 1)
                dve.tensor_tensor(ov[:, f, :], k.ps[f][0:GR, :], k.c("head_cols")[0:GR, :], ALU.mult).then_inc(s["ov_ready"], 1)
            dve.wait_ge(s["sums_made"], 1)
            d.after(dve.reciprocal(rs, k.ps[6][:, 0:2 * GR]))
            for f, keep in enumerate((k.foxs, k.wins)):
                dve.wait_ge(s["ot_made"], f + 1)
                d.after(dve.tensor_tensor(res[:, f, :], k.ps[4 + f][:, 0:GR], rs[:, f * GR:(f + 1) * GR], ALU.mult))
                dve.tensor_tensor(k.osample[:, f * H:(f + 1) * H, bass.ds(b * L, L)], res[:, f, :].rearrange("p (h q) -> p h q", h=H),
                                  keep[:, 2, :, bass.ds(b * L, L)], ALU.mult)

        @block.scalar
        def _(act):
            for p in range(NPG):
                page = act.value_load(k.pages[0:1, bass.ds(b * NPG + p, 1)], min_val=0, max_val=NPHYS - 1)
                act.dma_start(vslot[p], vf[bass.ds(page, 1)].rearrange("o t c -> (o t) c")).then_inc(s["v_loaded"], 16)
            for i in range(WT):
                act.dma_start(vwin[i], window_tile(vw, i)).then_inc(s["vw_loaded"], 16)
            for p in range(1, ITEMS, 2):
                act.wait_ge(s["k_turned"], p + 1)
                if p >= 2:
                    act.wait_ge(s["scored"], p - 1)
                act.copy(kt[:, 1, :], k.ps[1][:, :]).then_inc(s["kt_kept_s"], 1)
            act.wait_ge(s["shifted"], 1)
            act.activation(pr.rearrange("p n g -> p (n g)"), pr.rearrange("p n g -> p (n g)"), ACT.Exp).then_inc(s["exp_done"], 1)
    clear(nc, k_loaded + list(s.values()))


def store_sample_heads(nc, k, io):
    with nc.semaphore("sample_stored") as stored:
        with nc.Block() as block:
            @block.sync
            def _(sp):
                sp.dma_start(io.scr_o[:, :, T:NT].rearrange("k p n -> p k n"), k.osample).then_inc(stored, 16)
                sp.wait_ge(stored, 16)
        clear(nc, [stored])


def write_tokens(nc, k, io):
    with ExitStack() as c:
        sem = lambda n: c.enter_context(nc.semaphore(n))
        turned, left, right, stored = sem("y_turned"), sem("y_left"), sem("y_right"), [sem("y_stored0"), sem("y_stored1")]
        row = c.enter_context(nc.sbuf_tensor("yrow", [P, 2, D_MODEL], F32))
        block = c.enter_context(nc.Block())

        @block.tensor
        def _(pe):
            for t in range(TILES + 1):
                n = P if t < TILES else TS
                for half, taken in ((0, left), (1, right)):
                    if t >= 2:
                        pe.wait_ge(taken, t - 1)
                    for j in range(4):
                        last = pe.transpose(k.ps[half + 2 * (t % 2)][0:n, j * P:(j + 1) * P], k.xT[:, 4 * half + j, t * P:t * P + n], k.c("ident"))
                    last.then_inc(turned, 1)

        @block.vector
        def _(dve):
            for t in range(TILES + 1):
                n = P if t < TILES else TS
                dve.wait_ge(turned, 2 * t + 1)
                if t >= 2:
                    dve.wait_ge(stored[t % 2], 16 * (t // 2))
                dve.tensor_copy(row[0:n, t % 2, 0:512], k.ps[2 * (t % 2)][0:n, :]).then_inc(left, 1)

        @block.scalar
        def _(act):
            for t in range(TILES + 1):
                n = P if t < TILES else TS
                act.wait_ge(turned, 2 * t + 2)
                if t >= 2:
                    act.wait_ge(stored[t % 2], 16 * (t // 2))
                act.copy(row[0:n, t % 2, 512:1024], k.ps[1 + 2 * (t % 2)][0:n, :]).then_inc(right, 1)

        @block.sync
        def _(sp):
            for t in range(TILES + 1):
                n = P if t < TILES else TS
                sp.wait_ge(left, t + 1)
                sp.wait_ge(right, t + 1)
                dst = io.out_y_prompt[0, t * P:t * P + n, :] if t < TILES else io.out_y_sample.rearrange("b l d -> (b l) d")
                sp.dma_start(dst, row[0:n, t % 2, :]).then_inc(stored[t % 2], 16)
            sp.wait_ge(stored[0], 16 * 9)
            sp.wait_ge(stored[1], 16 * 8)


def build(nc, io, const_names, stop=99):
    with ExitStack() as c:
        sb = lambda n, s, dt=F32: c.enter_context(nc.sbuf_tensor(n, s, dt))[:]
        k = Chip()
        width = io.c_pack.shape[1]
        k.xT, k.rstd = sb("xT", [P, KT, NT]), sb("rstd", [P, NT])
        k.pack = sb("pack", [P, width])
        k.c = lambda n: k.pack[:, const_names[n][0]:const_names[n][0] + const_names[n][1]]
        k.big = sb("big", [P, 4 * NT + KT * 4 * P + NT])
        k.qkvz = k.big[:, 0:4 * NT].rearrange("p (m n) -> p m n", m=4)
        k.w = k.big[:, 4 * NT:4 * NT + KT * 4 * P].rearrange("p (k n) -> p k n", k=KT)
        k.qd = k.big[:, 4 * NT + KT * 4 * P:]
        k.conv_cols, k.cw_head = sb("conv_cols", [P, 12, 28]), sb("cw_head", [P, 3, 4])
        k.gate_cols, k.logf_cols = sb("gate_cols", [P, 2, H, TILES + 1]), sb("logf_cols", [P, TILES + 1, H])
        k.g_even, k.g_odd, k.b_norm = sb("g_even", [P, KT]), sb("g_odd", [P, KT]), sb("b_norm", [P, H])
        k.vec, k.small, k.pages = sb("vec", [P, 5]), sb("small", [36, 4]), sb("pages", [1, B * NPG], I32)
        k.eps, k.one, k.zero = sb("eps", [P, 1]), sb("one", [P, 1]), sb("zero", [P, 324])
        k.ps4 = c.enter_context(nc.psum_tensor("ps0123", [P, 4 * 512], F32))[:]
        k.ps = [k.ps4[:, i * 512:(i + 1) * 512] for i in range(4)]
        k.ps += [c.enter_context(nc.psum_tensor(f"ps{i}", [P, 512], F32))[:] for i in range(4, 8)]
        with nc.semaphore("windows_shifted") as windows_shifted:
            with nc.Block() as block:
                @block.vector
                def _(dve):
                    dve.memset(k.eps, EPS)
                    dve.memset(k.one, 1.0)
                    dve.memset(k.zero, 0.0)
                    dve.memset(k.small, 0.0)

                @block.sync
                def _(sp):
                    for b in range(B):
                        for dst, src in ((io.out_win_k_sample, io.cache_win_k), (io.out_win_v_sample, io.cache_win_v)):
                            sp.dma_start(dst[0, b, 0:WBUF - L].rearrange("(g r) h d -> g (r h d)", g=28),
                                         src[0, b, L:WBUF].rearrange("(g r) h d -> g (r h d)", g=28)).then_inc(windows_shifted, 16)
            with nc.allow_non_contiguous_dma(reason="a few thousand single words, once"):
                load_tokens(nc, k, io)
            token_norms(nc, k, 0)
            row_gates_even(nc, k, io)
            if stop > 1:
                with nc.Fori(0, H) as h:
                    head_A(nc, k, io, h)
            if stop > 2:
                with nc.Fori(0, H) as h:
                    head_B(nc, k, io, h)
            if stop > 3:
                output_projection(nc, k, io, 0)
                token_norms(nc, k, 1)
                row_gates_odd(nc, k, io)
                k.foxs, k.wins = sb("foxs", [P, 3, H, TS]), sb("wins", [P, 3, H, TS])
                k.foxv, k.winv = sb("foxv", [TS, H, P]), sb("winv", [TS, H, P])
                k.snew, k.osample = sb("snew", [TS, 2, H, TS]), sb("osample", [P, 2 * H, TS])
            if stop > 4:
                with nc.Fori(0, H) as h:
                    head_attention(nc, k, io, h, "C")
            if stop > 5:
                with nc.Fori(0, H) as h:
                    head_attention(nc, k, io, h, "D")
            if stop > 6:
                k.sc_all = sb("sc_all", [P, NPG + 1 + WT + 1, 4 * H])
                sample_new_scores(nc, k, io)
                with nc.Fori(0, B) as b:
                    sample_attention(nc, k, io, b)
                store_sample_heads(nc, k, io)
                output_projection(nc, k, io, 1)
            if stop > 3:
                write_tokens(nc, k, io)
            with nc.Block() as block:
                @block.sync
                def _(sp):
                    sp.wait_ge(windows_shifted, 16 * 2 * B)


_INS = ["x_prompt", "x_sample", "cache_fox_k", "cache_fox_v", "cache_fox_logf", "page_table", "cache_win_k", "cache_win_v",
        "state_delta", "state_delta_conv", "state_ret", "norm_even", "w_in_even", "conv_w", "a_log", "dt_bias", "a_norm",
        "b_norm", "w_out_even", "norm_odd", "w_in_odd", "c_q_norm", "c_k_norm", "f_bias", "d_q_norm", "d_k_norm", "w_out_odd"]
_OUTS = [("y_prompt", (1, T, D_MODEL)), ("y_sample", (B, L, D_MODEL)),
         ("fox_k_prompt", (1, 1, T, H, P)), ("fox_v_prompt", (1, 1, T, H, P)), ("fox_logf_prompt", (1, 1, T, H)),
         ("fox_k_sample", (B, 1, L, H, P)), ("fox_v_sample", (B, 1, L, H, P)), ("fox_logf_sample", (B, 1, L, H)),
         ("win_k_prompt", (1, 1, T, H, P)), ("win_v_prompt", (1, 1, T, H, P)),
         ("win_k_sample", (1, B, WBUF, H, P)), ("win_v_sample", (1, B, WBUF, H, P)),
         ("delta_prompt", (1, 1, H, P, P)), ("delta_conv_prompt", (1, 1, 3, 3 * HD)),
         ("delta_sample", (1, B, H, P, P)), ("delta_conv_sample", (1, B, 3, 3 * HD)),
         ("ret_prompt", (1, 1, H, P, P)), ("ret_sample", (1, B, H, P, P))]


class Dram:

    def __init__(self, t):
        self.a_log = t["a_log"]
        self.a_norm = t["a_norm"]
        self.b_norm = t["b_norm"]
        self.c_k_norm = t["c_k_norm"]
        self.c_pack = t["c_pack"]
        self.c_q_norm = t["c_q_norm"]
        self.c_reset = t["c_reset"]
        self.c_ret = t["c_ret"]
        self.c_window = t["c_window"]
        self.cache_fox_k = t["cache_fox_k"]
        self.cache_fox_logf = t["cache_fox_logf"]
        self.cache_fox_v = t["cache_fox_v"]
        self.cache_win_k = t["cache_win_k"]
        self.cache_win_v = t["cache_win_v"]
        self.conv_w = t["conv_w"]
        self.d_k_norm = t["d_k_norm"]
        self.d_q_norm = t["d_q_norm"]
        self.dt_bias = t["dt_bias"]
        self.f_bias = t["f_bias"]
        self.norm_even = t["norm_even"]
        self.norm_odd = t["norm_odd"]
        self.out_delta_conv_prompt = t["out_delta_conv_prompt"]
        self.out_delta_conv_sample = t["out_delta_conv_sample"]
        self.out_delta_prompt = t["out_delta_prompt"]
        self.out_delta_sample = t["out_delta_sample"]
        self.out_fox_k_prompt = t["out_fox_k_prompt"]
        self.out_fox_k_sample = t["out_fox_k_sample"]
        self.out_fox_logf_prompt = t["out_fox_logf_prompt"]
        self.out_fox_logf_sample = t["out_fox_logf_sample"]
        self.out_fox_v_prompt = t["out_fox_v_prompt"]
        self.out_fox_v_sample = t["out_fox_v_sample"]
        self.out_ret_prompt = t["out_ret_prompt"]
        self.out_ret_sample = t["out_ret_sample"]
        self.out_win_k_prompt = t["out_win_k_prompt"]
        self.out_win_k_sample = t["out_win_k_sample"]
        self.out_win_v_prompt = t["out_win_v_prompt"]
        self.out_win_v_sample = t["out_win_v_sample"]
        self.out_y_prompt = t["out_y_prompt"]
        self.out_y_sample = t["out_y_sample"]
        self.page_table = t["page_table"]
        self.scr_f = t["scr_f"]
        self.scr_g = t["scr_g"]
        self.scr_o = t["scr_o"]
        self.state_delta = t["state_delta"]
        self.state_delta_conv = t["state_delta_conv"]
        self.state_ret = t["state_ret"]
        self.w_in_even = t["w_in_even"]
        self.w_in_odd = t["w_in_odd"]
        self.w_out_even = t["w_out_even"]
        self.w_out_odd = t["w_out_odd"]
        self.x_prompt = t["x_prompt"]
        self.x_sample = t["x_sample"]


def declare(nc, inputs):
    tensors, arrays = {}, {}
    consts, names = shape_constants()
    given = {n: np.ascontiguousarray(inputs[n]) for n in _INS}
    given.update(consts)
    for n, a in given.items():
        arrays[f"in_{n}"] = a
        tensors[n] = nc.dram_tensor(f"in_{n}", a.shape, mybir.dt.from_np(a.dtype), kind="ExternalInput").ap()
    for n, shape in _OUTS:
        tensors[f"out_{n}"] = nc.dram_tensor(f"out_{n}", shape, F32, kind="ExternalOutput").ap()
    tensors["scr_g"] = nc.dram_tensor("scr_g", (H, NT), F32).ap()
    tensors["scr_f"] = nc.dram_tensor("scr_f", (H, T), F32).ap()
    tensors["scr_o"] = nc.dram_tensor("scr_o", (2 * H, P, NT), F32).ap()
    return Dram(tensors), arrays, names


def kernel(**inputs):
    import concourse.bacc as _bacc
    from concourse.bass_utils import run_bass_kernel_spmd as _run

    nc = _bacc.Bacc("TRN2", target_bir_lowering=False, num_devices=1)
    io, arrays, names = declare(nc, inputs)
    build(nc, io, names)
    r = _run(nc, [arrays], core_ids=[0])
    return tuple(r.results[0][f"out_{n}"] for n, _ in _OUTS)
```

```python
from contextlib import ExitStack

import numpy as np
import concourse.bass as bass
from concourse import mybir
from concourse.alu_op_type import AluOpType as ALU

F32 = mybir.dt.float32
I32 = mybir.dt.int32
ACT = mybir.ActivationFunctionType
X = mybir.AxisListType.X

P = 128
D_MODEL = 1024
KT = D_MODEL // P
T = 2048
TILES = T // P
B = 8
L = 4
TS = B * L
NT = T + TS
CH = 416
NC = NT // CH
H = 4
HD = H * P
G = 4
PAGE = 128
NPG = 32
NPHYS = 320
WBUF = 2048
WT = 7
EPS = 1e-6
BIG = 1e30
SCALE = P ** -0.5
EVEN_OFF = {"A": (0, 512, 1024, 1536), "B": (2056, 2568, 3080, 3592)}
ODD_OFF = {"C": (0, 512, 1024, 1536), "D": (2052, 2564, 3076, 3588)}
EVEN_IN = 4104
ODD_IN = 4100
WMAX = 2048


def shape_constants():
    i = np.arange(P)
    f = np.float32
    lower = i[:, None] > i[None, :]
    c = {
        "ident": np.eye(P), "ones": np.ones((P, P)),
        "not_lower": np.where(lower, 0, BIG), "not_causal": np.where(lower, BIG, 0),
        "diag16": i[:, None] // 16 == i[None, :] // 16,
    }
    for s in (16, 32, 64):
        c[f"under{2 * s}"] = (i[:, None] // (2 * s) == i[None, :] // (2 * s)) & (i[:, None] // s > i[None, :] // s)
    c["causal_bias"] = np.where(i[None, :] > i[:, None], -BIG, 0)
    c["later"] = lower
    s = np.arange(TS)
    same = s[:, None] // L == s[None, :] // L
    pad = lambda a: np.pad(a, ((0, P - a.shape[0]), (0, 0)))
    c["s_not_lower"] = pad(np.where(same & (s[:, None] > s[None, :]), 0, BIG))
    c["s_not_causal"] = pad(np.where(same & (s[:, None] <= s[None, :]), 0, BIG))
    c["s_last"] = pad(same & (s[None, :] % L == L - 1))
    c["s_prefix"] = pad(same & (s[:, None] <= s[None, :]))
    c["s_bias"] = pad(np.where(same & (s[:, None] <= s[None, :]), 0, -BIG))
    c["s_cols"] = np.broadcast_to((s[None, :] // L == np.arange(B)[:, None]).reshape(1, -1), (P, B * TS))
    c["s_rows"] = pad(s[:, None] // L == np.arange(B)[None, :])
    r = np.arange(4 * H)
    c["head_cols"] = pad((r[:, None] // L == np.arange(HD)[None, :] // P))
    c["page_reset"] = np.broadcast_to((np.arange(H * NPG) % NPG != 0)[None, :], (P, H * NPG))
    slope = 2.0 ** (-8.0 * np.arange(1, H + 1) / H)

    def reach(d):
        n = ((d >= 0) & (d <= 128)).astype(int) + ((d >= 0) & (d <= 512) & (d % 4 == 0)) \
            + ((d >= 0) & (d <= 2048) & (d % 16 == 0))
        return n

    def bias(d, h):
        n = reach(d)
        return np.where(n > 0, np.log(np.maximum(n, 1)) - slope[h] * d, -BIG)

    new = np.stack([np.where(same, bias(s[None, :] - s[:, None], h), -BIG) for h in range(H)], 1)
    c["s_window"] = np.pad(new.reshape(TS, H * TS), ((0, P - TS), (0, 0)))
    rows = window_rows().reshape(WT, P)
    past = np.zeros((P, WT, H, L))
    for h in range(H):
        for q in range(L):
            past[:, :, h, q] = bias(WBUF + q - rows, h).T
    c["window_past"] = past.reshape(P, -1)
    names, cols, at = {}, [], 0
    for k, v in c.items():
        v = np.asarray(v, f)
        names[k] = (at, v.shape[1])
        at += v.shape[1]
        cols.append(v)
    pack = np.concatenate(cols, 1)
    m = np.arange(T)
    window = np.stack([bias(i[:, None] + (T - P) - m[None, :], h) for h in range(H)]).astype(f)
    lg = np.log1p(-np.exp2(-5.0 - np.arange(H, dtype=np.float64)))
    ret = np.zeros((H, P, RET), f)
    for h in range(H):
        d = i[None, :] - i[:, None]
        ret[h, :, 0:P] = np.where(d >= 0, np.exp(np.maximum(d, 0) * lg[h]) * SCALE, 0)
        ret[h, :, P:2 * P] = np.exp((i + 1.0) * lg[h])[None, :]
        ret[h, :, 256] = np.exp((P - 1.0 - i) * lg[h]) * SCALE
        ret[h, :, 257] = np.exp(P * lg[h])
        ds = s[None, :] - s[:, None]
        ret[h, :TS, 258:290] = np.where(same & (ds >= 0), np.exp(np.maximum(ds, 0) * lg[h]) * SCALE, 0)
        ret[h, :, 290:322] = np.exp((s % L + 1.0) * lg[h])[None, :]
        ret[h, :TS, 322] = np.exp((L - 1.0 - s % L) * lg[h]) * SCALE
        ret[h, :, 323] = np.exp(L * lg[h])
    reset = np.ones((1, NT), f)
    reset[0, 0:T:P] = 0
    reset[0, T::L] = 0
    return {"c_pack": pack, "c_window": window, "c_ret": ret, "c_reset": reset}, names


RET = 324


def window_rows():
    g = np.arange(96)[:, None] * 16 + np.arange(4)[None, :]
    return np.concatenate([g.reshape(-1), np.arange(1536, 2048)])


def repeat(ap, axis, n):
    ap = ap.unsqueeze(axis)
    shape = list(ap.shape)
    shape[axis] = n
    return ap.broadcast_to(shape)


def clear(nc, sems):
    with nc.Block() as block:
        @block.gpsimd
        def _(pool):
            for s in sems[0::5]:
                pool.sem_clear(s)

        @block.vector
        def _(dve):
            for s in sems[1::5]:
                dve.sem_clear(s)

        @block.scalar
        def _(act):
            for s in sems[2::5]:
                act.sem_clear(s)

        @block.sync
        def _(sp):
            for s in sems[3::5]:
                sp.sem_clear(s)

        @block.tensor
        def _(pe):
            for s in sems[4::5]:
                pe.sem_clear(s)


class Chip:
    pass


def load_tokens(nc, k, io):
    with ExitStack() as c:
        sem = lambda n: c.enter_context(nc.semaphore(n))
        const_loaded, vec_loaded = sem("const_loaded"), sem("vec_loaded")
        x_loaded = [sem("x_loaded0"), sem("x_loaded1")]
        rows_loaded, rows_turned, rows_copied = sem("rows_loaded"), sem("rows_turned"), sem("rows_copied")
        x_turned, left_copied, right_copied = sem("x_turned"), sem("left_copied"), sem("right_copied")
        xrow = c.enter_context(nc.sbuf_tensor("xrow", [P, 2, D_MODEL], F32))
        conv_rows = c.enter_context(nc.sbuf_tensor("conv_rows", [28, 3 * HD], F32))
        block = c.enter_context(nc.Block())
        vectors = [(k.g_even, io.norm_even[0].rearrange("(k p) -> p k", p=P)),
                   (k.g_odd, io.norm_odd[0].rearrange("(k p) -> p k", p=P)),
                   (k.b_norm, io.b_norm[0].rearrange("(k p) -> p k", p=P)),
                   (k.vec[:, 0:1], io.a_norm[0].unsqueeze(1)), (k.vec[:, 1:2], io.c_q_norm[0].unsqueeze(1)),
                   (k.vec[:, 2:3], io.c_k_norm[0].unsqueeze(1)), (k.vec[:, 3:4], io.d_q_norm[0].unsqueeze(1)),
                   (k.vec[:, 4:5], io.d_k_norm[0].unsqueeze(1)),
                   (k.small[32:36, 0:1], io.a_log[0].unsqueeze(1)), (k.small[32:36, 1:2], io.dt_bias[0].unsqueeze(1)),
                   (k.small[0:4, 2:3], io.f_bias[0].unsqueeze(1)),
                   (k.pages, io.page_table.rearrange("b n -> (b n)").unsqueeze(0))]

        @block.sync
        def _(sp):
            sp.dma_start(k.pack, io.c_pack).then_inc(const_loaded, 16)
            sp.dma_start(conv_rows[0:24, :], io.state_delta_conv[0].rearrange("b r c -> (b r) c")).then_inc(rows_loaded, 16)
            sp.dma_start(conv_rows[24:28, :], io.conv_w[0]).then_inc(rows_loaded, 16)
            for t in range(TILES + 1):
                if t >= 2:
                    sp.wait_ge(x_turned, 2 * (t - 1))
                src = io.x_prompt[0, t * P:(t + 1) * P, :] if t < TILES else io.x_sample.rearrange("b l d -> (b l) d")
                n = P if t < TILES else TS
                sp.dma_start(xrow[0:n, t % 2, :], src).then_inc(x_loaded[t % 2], 16)
            for dst, src in vectors:
                sp.dma_start(dst, src).then_inc(vec_loaded, 16)
            sp.wait_ge(vec_loaded, 16 * len(vectors))

        @block.tensor
        def _(pe):
            pe.wait_ge(const_loaded, 16)
            pe.wait_ge(rows_loaded, 32)
            for j in range(12):
                last = pe.transpose(k.ps[2][:, j * 28:(j + 1) * 28], conv_rows[:, j * P:(j + 1) * P], k.c("ident")[0:28, 0:28])
            last.then_inc(rows_turned, 1)
            for t in range(TILES + 1):
                n = P if t < TILES else TS
                pe.wait_ge(x_loaded[t % 2], 16 * (t // 2 + 1))
                for half, copied in ((0, left_copied), (1, right_copied)):
                    if t >= 1:
                        pe.wait_ge(copied, t)
                    for j in range(4):
                        kk = 4 * half + j
                        last = pe.transpose(k.ps[half][:, j * P:j * P + n], xrow[0:n, t % 2, kk * P:(kk + 1) * P],
                                            k.c("ident")[0:n, 0:n])
                    last.then_inc(x_turned, 1)

        @block.vector
        def _(dve):
            dve.wait_ge(rows_turned, 1)
            dve.tensor_copy(k.conv_cols.rearrange("p a b -> p (a b)"), k.ps[2][:, 0:336]).then_inc(rows_copied, 1)
            for t in range(TILES + 1):
                n = P if t < TILES else TS
                dve.wait_ge(x_turned, 2 * t + 1)
                dve.tensor_copy(k.xT[:, 0:4, t * P:t * P + n],
                                k.ps[0].rearrange("p (j n) -> p j n", j=4)[:, :, 0:n]).then_inc(left_copied, 1)

        @block.scalar
        def _(act):
            for t in range(TILES + 1):
                n = P if t < TILES else TS
                act.wait_ge(x_turned, 2 * t + 2)
                act.copy(k.xT[:, 4:8, t * P:t * P + n],
                         k.ps[1].rearrange("p (j n) -> p j n", j=4)[:, :, 0:n]).then_inc(right_copied, 1)
    clear(nc, [const_loaded, vec_loaded, *x_loaded, rows_loaded, rows_turned, rows_copied, x_turned, left_copied, right_copied])


def token_norms(nc, k, layer):
    with ExitStack() as c:
        sem = lambda n: c.enter_context(nc.semaphore(f"{n}_{layer}"))
        squared, summed, logged, rooted = sem("squared"), sem("summed"), sem("logged"), sem("rooted")
        sq = c.enter_context(nc.sbuf_tensor(f"sq_{layer}", [P, 2, NT], F32))
        block = c.enter_context(nc.Block())

        @block.scalar
        def _(act):
            for j in range(KT):
                if j >= 2:
                    act.wait_ge(summed, j - 1)
                act.activation(sq[:, j % 2, :], k.xT[:, j, :], ACT.Square).then_inc(squared, 1)
            act.wait_ge(summed, KT)
            for n in range(NC):
                act.activation(sq[:, 0, n * CH:(n + 1) * CH], k.ps[n][:, 0:CH], ACT.Ln, bias=k.eps,
                               scale=1.0 / D_MODEL).then_inc(logged, 1)
            act.wait_ge(logged, NC)
            act.activation(k.rstd[:, :], sq[:, 0, :], ACT.Exp, scale=-0.5).then_inc(rooted, 1)

        @block.tensor
        def _(pe):
            for j in range(KT):
                pe.wait_ge(squared, j + 1)
                for n in range(NC):
                    last = pe.matmul(k.ps[n][:, 0:CH], k.c("ones"), sq[:, j % 2, n * CH:(n + 1) * CH],
                                     start=(j == 0), stop=(j == KT - 1))
                last.then_inc(summed, 1)
    clear(nc, [squared, summed, logged, rooted])


def row_gates_even(nc, k, io):
    with ExitStack() as c:
        sem = lambda n: c.enter_context(nc.semaphore(n))
        w_loaded, w_zero, w_scaled = sem("gw_loaded"), sem("gw_zero"), sem("gw_scaled")
        row_ready, row_taken = sem("row_ready"), sem("row_taken")
        a_step, d_step = sem("gate_act"), sem("gate_dve")
        turned, cols_ready, stored = sem("gates_turned"), sem("gate_cols"), sem("g_stored")
        w = c.enter_context(nc.sbuf_tensor("gw", [P, KT, 36], F32))
        rows = c.enter_context(nc.sbuf_tensor("rows", [36, NT], F32))
        tmp = c.enter_context(nc.sbuf_tensor("rtmp", [36, NT], F32))
        tmp2 = c.enter_context(nc.sbuf_tensor("rtmp2", [36, NT], F32))
        reset = c.enter_context(nc.sbuf_tensor("reset", [36, NT], F32))
        block = c.enter_context(nc.Block())
        HI = slice(32, 36)

        @block.sync
        def _(sp):
            sp.wait_ge(w_zero, 1)
            wv = io.w_in_even[0].rearrange("(k p) c -> p k c", p=P)
            sp.dma_start(w[:, :, 0:4], wv[:, :, 2048:2052]).then_inc(w_loaded, 16)
            sp.dma_start(w[:, :, 32:36], wv[:, :, 2052:2056]).then_inc(w_loaded, 16)
            sp.dma_start(reset[HI, :], io.c_reset.broadcast_to([4, NT])).then_inc(w_loaded, 16)
            sp.wait_ge(d_step, 6)
            sp.dma_start(io.scr_g, rows[HI, :]).then_inc(stored, 16)
            sp.wait_ge(stored, 16)

        @block.vector
        def _(dve):
            dve.memset(w[:, :, :], 0.0).then_inc(w_zero, 1)
            dve.wait_ge(w_loaded, 48)
            dve.tensor_tensor(w[:, :, :], w[:, :, :], repeat(k.g_even, 2, 36), ALU.mult).then_inc(w_scaled, 1)
            for n in range(NC):
                dve.wait_ge(row_ready, n + 1)
                dve.tensor_tensor(rows[:, n * CH:(n + 1) * CH], k.ps[n % 2][0:36, 0:CH], k.rstd[0:36, n * CH:(n + 1) * CH],
                                  ALU.mult).then_inc(row_taken, 1)
            dve.wait_ge(a_step, 1)
            dve.tensor_scalar(rows[0:4, :], tmp[0:4, :], 0.5, 0.5, ALU.mult, ALU.add).then_inc(d_step, 1)
            dve.tensor_scalar(tmp2[HI, :], rows[HI, :], k.small[HI, 1:2], 0.0, ALU.add, ALU.max).then_inc(d_step, 1)
            dve.wait_ge(a_step, 4)
            dve.wait_ge(d_step, 2)
            dve.tensor_tensor(tmp2[HI, :], tmp2[HI, :], tmp[HI, :], ALU.add).then_inc(d_step, 1)
            dve.wait_ge(a_step, 5)
            dve.tensor_scalar(k.small[HI, 3:4], k.small[HI, 3:4], -1.0, None, ALU.mult).then_inc(d_step, 1)
            dve.wait_ge(d_step, 4)
            dve.tensor_scalar(tmp2[HI, :], tmp2[HI, :], k.small[HI, 3:4], None, ALU.mult).then_inc(d_step, 1)
            dve.wait_ge(d_step, 5)
            dve.tensor_tensor_scan(rows[HI, :], reset[HI, :], tmp2[HI, :], 0.0, ALU.mult, ALU.add).then_inc(d_step, 1)
            for half in range(2):
                dve.wait_ge(turned, half + 1)
                n = 9 - half
                for what in range(2):
                    last = dve.tensor_copy(k.gate_cols[:, what, :, 9 * half:9 * half + n],
                                           k.ps[2 + half][:, 0:36 * n].rearrange("p (t r) -> p r t", r=36)[:, 32 * what:32 * what + H, :])
                last.then_inc(cols_ready, 1)

        @block.scalar
        def _(act):
            act.wait_ge(row_taken, NC)
            act.activation(tmp[0:4, :], rows[0:4, :], ACT.Tanh, scale=0.5).then_inc(a_step, 1)
            act.activation(tmp[HI, :], rows[HI, :], ACT.Abs, bias=k.small[HI, 1:2]).then_inc(a_step, 1)
            act.wait_ge(a_step, 2)
            act.activation(tmp[HI, :], tmp[HI, :], ACT.Exp, scale=-1.0).then_inc(a_step, 1)
            act.wait_ge(a_step, 3)
            act.activation(tmp[HI, :], tmp[HI, :], ACT.Ln, bias=k.one[HI, :]).then_inc(a_step, 1)
            act.activation(k.small[HI, 3:4], k.small[HI, 0:1], ACT.Exp).then_inc(a_step, 1)

        @block.tensor
        def _(pe):
            pe.wait_ge(w_scaled, 1)
            for n in range(NC):
                if n >= 2:
                    pe.wait_ge(row_taken, n - 1)
                for j in range(KT):
                    last = pe.matmul(k.ps[n % 2][0:36, 0:CH], w[:, j, :], k.xT[:, j, n * CH:(n + 1) * CH],
                                     start=(j == 0), stop=(j == KT - 1))
                last.then_inc(row_ready, 1)
            pe.wait_ge(d_step, 6)
            for half in range(2):
                pe.matmul(k.ps[2 + half][:, 0:324], k.c("ones"), k.zero[:, 0:324], start=True, stop=True)
                for t in range(9 * half, 17 if half else 9):
                    m = P if t < TILES else TS
                    a = 36 * (t - 9 * half)
                    last = pe.transpose(k.ps[2 + half][0:m, a:a + 36], rows[:, t * P:t * P + m], k.c("ident")[0:36, 0:36])
                last.then_inc(turned, 1)
    clear(nc, [w_loaded, w_zero, w_scaled, row_ready, row_taken, a_step, d_step, turned, cols_ready, stored])


def head_weights(k, io, branch, h, w_loaded, w_scaled):
    layer = 0 if branch in EVEN_OFF else 1
    wv = (io.w_in_even if layer == 0 else io.w_in_odd)[0].rearrange("(k p) c -> p k c", p=P)
    offs = (EVEN_OFF if layer == 0 else ODD_OFF)[branch]
    gain = k.g_even if layer == 0 else k.g_odd

    def sync(sp):
        for m in range(4):
            sp.dma_start(k.w[:, :, m * P:(m + 1) * P], wv[:, :, bass.ds(h * P + offs[m], P)]).then_inc(w_loaded, 16)

    def gpsimd(pool):
        pool.wait_ge(w_loaded, 64)
        pool.tensor_tensor(k.w[:, :, :], k.w[:, :, :], repeat(gain, 2, 4 * P), ALU.mult).then_inc(w_scaled, 1)
        pool.wait_ge(w_scaled, 1)

    return sync, gpsimd


def first_weights(nc, k, io, branch):
    with nc.semaphore(f"w_loaded_{branch}0") as w_loaded, nc.semaphore(f"w_scaled_{branch}0") as w_scaled:
        load, scale = head_weights(k, io, branch, 0, w_loaded, w_scaled)
        with nc.Block() as block:
            @block.sync
            def _(sp):
                load(sp)

            @block.gpsimd
            def _(pool):
                scale(pool)
        clear(nc, [w_loaded, w_scaled])


def project_head(nc, k, io, c, branch, h, dst):
    sem = lambda n: c.enter_context(nc.semaphore(f"{n}_{branch}"))
    w_loaded, w_scaled, proj_ready, proj_taken = sem("w_loaded"), sem("w_scaled"), sem("proj_ready"), sem("proj_taken")
    next_sync, next_pool = head_weights(k, io, branch, (h + 1) % H, w_loaded, w_scaled)

    def tensor(pe, at):
        m, n = ORDER[at // NC], at % NC
        if at >= 2:
            pe.wait_ge(proj_taken, at - 1)
        for j in range(KT):
            last = pe.matmul(k.ps[at % 2][:, 0:CH], k.w[:, j, m * P:(m + 1) * P],
                             k.xT[:, j, n * CH:(n + 1) * CH], start=(j == 0), stop=(j == KT - 1))
        last.then_inc(proj_ready, 1)

    def vector(dve, at):
        m, n = ORDER[at // NC], at % NC
        dve.wait_ge(proj_ready, at + 1)
        for out, a, b in dst(m, n):
            r = k.rstd[:, n * CH + a:n * CH + b]
            src = k.ps[at % 2][:, a:b]
            if len(out.shape) == 3:
                r = r.rearrange("p (x y) -> p x y", y=L)
                src = src.rearrange("p (x y) -> p x y", y=L)
            last = dve.tensor_tensor(out, src, r, ALU.mult)
        last.then_inc(proj_taken, 1)

    return [w_loaded, w_scaled, proj_ready, proj_taken], next_sync, next_pool, tensor, vector


ORDER = (3, 0, 1, 2)
PROJ = 4 * NC
SUMS = 2


def feature_sums(pe, k, src):
    for n in range(NC):
        last = pe.matmul(k.ps[SUMS + n][:, 0:CH], k.c("ones"), src[:, n * CH:(n + 1) * CH], start=True, stop=True)
    return last


class Order:

    def __init__(self, eng, sem):
        self.eng, self.sem, self.n = eng, sem, 0

    def after(self, ins):
        ins.then_inc(self.sem, 1)
        self.n += 1
        self.eng.wait_ge(self.sem, self.n)


def head_A(nc, k, io, h):
    with ExitStack() as c:
        sbuf = lambda n, s: c.enter_context(nc.sbuf_tensor(n, s, F32))[:]
        sem = lambda n: c.enter_context(nc.semaphore(n))
        raw = sbuf("raw", [P, 3, 3 + T + B * 7])
        g_row, g_exp, g_tile = sbuf("g_row", [P, NT]), sbuf("g_exp", [P, G * P]), sbuf("g_tile", [P, TILES + B])
        grp, more, kept = k.w, sbuf("grp", [P, 8, G * P]), k.qd[:, 0:4 * G * P].rearrange("p (m n) -> p m n", m=4)
        Kb, DT, A, N, NTr, N2, N2T, N4 = [grp[:, i, :] for i in range(8)]
        N4T, X0, X1 = [more[:, i, :] for i in range(3)]
        Kt, Vb, XT, QK, WK = [(kept[:, i, :], more[:, 3 + i, :]) for i in range(4)] + [(more[:, 7, :], sbuf("wk", [P, G * P]))]
        hcol = sbuf("hcol", [P, 4, 17])
        S = sbuf("S", [P, 2, P])
        S0 = raw[:, 2, 0:B * P].rearrange("p (b v) -> p b v", b=B)
        u = sbuf("u", [P, P])
        tail = sbuf("tailbuf", [TS, 1])
        convo = sbuf("convo", [P, 27])
        convr = sbuf("convr", [27, 3 * P])
        sq = raw[:, 1, 0:NT]
        O = raw[:, 0, 0:NT]
        squares = [more.rearrange("p m n -> p (m n)")[:, 0:NT], k.qd]
        Q = k.qkvz
        w_sems, p_sync, p_pool, p_tensor, p_vector = project_head(
            nc, k, io, c, "A", h,
            lambda m, n: [(Q[:, 3, n * CH:(n + 1) * CH], 0, CH)] if m == 3 else
            ([(raw[:, m, 3 + n * CH:3 + (n + 1) * CH], 0, CH)] if n < NC - 1 else
             [(raw[:, m, 3 + n * CH:3 + T], 0, T - n * CH),
              (raw[:, m, 3 + T:].rearrange("p (b r) -> p b r", r=7)[:, :, 3:7], T - n * CH, CH)]))
        names = ["g_loaded", "s_loaded", "conv_set", "conv_done", "conv_kept", "conv_turned", "conv_out",
                 "silu_done", "sq_done", "ss_done", "ln_done", "root_done", "normed",
                 "dve_order", "act_order", "grams", "rows_turned", "o_made", "exp_in", "exp_out", "product", "operand", "u_made", "u_kept",
                 "s_made", "s_kept", "o_kept", "um_ready", "sn_made", "sn_kept", "out_stored", "post_sq", "post_ss",
                 "post_root", "post_ready", "gate_done", "cols_done"]
        s = {n: sem(n) for n in names}
        block = c.enter_context(nc.Block())
        u_bank, s_bank, o_bank = k.ps[0][:, 0:P], k.ps[0][:, P:2 * P], k.ps[1][:, 0:P]
        place = lambda n, h2: {5: k.ps[2 + 2 * h2][:, 0:256], 6: k.ps[2 + 2 * h2][:, 256:512], 4: k.ps[3 + 2 * h2][:, 0:256]}[n]

        groups = [(g * G * P, G, P) for g in range(TILES // G)] + [(T, 1, TS)]

        @block.sync
        def _(sp):
            sp.dma_start(g_row, io.scr_g[bass.ds(h, 1), :].broadcast_to([P, NT])).then_inc(s["g_loaded"], 16)
            sp.wait_ge(s["conv_out"], 1)
            for m in range(3):
                col = bass.ds(h * P + m * HD, P)
                sp.dma_start(io.out_delta_conv_prompt[0, 0, :, col], convr[0:3, m * P:(m + 1) * P]).then_inc(s["out_stored"], 16)
                sp.dma_start(io.out_delta_conv_sample[0, :, :, col].rearrange("b r c -> (b r) c"),
                             convr[3:27, m * P:(m + 1) * P]).then_inc(s["out_stored"], 16)
            sp.wait_ge(s["conv_out"], 1)
            sp.dma_start(S0, io.state_delta[0, :, bass.ds(h, 1), :, :].rearrange("b o k v -> k (b o) v")).then_inc(s["s_loaded"], 16)
            sp.wait_ge(s["s_kept"], TILES)
            sp.dma_start(io.out_delta_prompt[0, 0, bass.ds(h, 1)].rearrange("o k v -> (o k) v"), S[:, TILES % 2, :]).then_inc(s["out_stored"], 16)
            sp.wait_ge(s["sn_kept"], 1)
            sp.dma_start(io.out_delta_sample[0, :, bass.ds(h, 1), :, :].rearrange("b o k v -> k (b o) v"), S0).then_inc(s["out_stored"], 16)
            sp.wait_ge(s["post_sq"], 1)
            p_sync(sp)
            sp.wait_ge(s["post_ready"], 1)
            sp.dma_start(io.scr_o[bass.ds(h, 1)].rearrange("o p n -> (o p) n"), O).then_inc(s["out_stored"], 16)
            sp.wait_ge(s["out_stored"], 16 * 9)

        @block.gpsimd
        def _(pool):
            p_pool(pool)

        @block.tensor
        def _(pe):
            def turn_conv(m):
                pe.wait_ge(s["conv_kept"], m + 1)
                if m:
                    pe.wait_ge(s["cols_done"], m)
                pe.transpose(k.ps[7][0:27, 0:P], convo, k.c("ident")).then_inc(s["conv_turned"], 1)

            for at in range(PROJ):
                p_tensor(pe, at)
                if at == 11:
                    turn_conv(0)
                if at == 13 or at == 18:
                    m = 0 if at == 13 else 1
                    pe.wait_ge(s["sq_done"], m + 1)
                    if m:
                        pe.wait_ge(s["ln_done"], NC)
                    feature_sums(pe, k, squares[m]).then_inc(s["ss_done"], 1)
                if at == 16:
                    turn_conv(1)
            turn_conv(2)
            pe.wait_ge(s["normed"], 2)
            pe.wait_ge(s["cols_done"], 3)
            used = 0

            def recur(step):
                if step < 0:
                    return
                tile, odd = divmod(step, 2)
                f, sl = (tile // G) % 2, slice(tile % G * P, (tile % G + 1) * P)
                if not odd:
                    if tile:
                        pe.wait_ge(s["s_kept"], tile)
                    pe.matmul(u_bank, XT[f][:, sl], Vb[f][:, sl], start=True, stop=False)
                    pe.matmul(u_bank, WK[f][:, sl], S[:, tile % 2, :], start=False, stop=True).then_inc(s["u_made"], 1)
                    if tile:
                        pe.wait_ge(s["o_kept"], tile)
                    pe.matmul(o_bank, S[:, tile % 2, :], Q[:, 0, tile * P:(tile + 1) * P], start=True, stop=False)
                else:
                    pe.wait_ge(s["u_kept"], tile + 1)
                    pe.matmul(s_bank, Kt[f][:, sl], u, start=True, stop=True).then_inc(s["s_made"], 1)
                    pe.matmul(o_bank, u, QK[f][:, sl], start=False, stop=True).then_inc(s["o_made"], 1)

            for gi, (t0, ng, w) in enumerate(groups):
                sample = w != P
                f = gi % 2
                idn = k.c("ident")[0:w, 0:w]
                sl = [slice(i * w, (i + 1) * w) for i in range(ng)]
                hs = [slice(i * P, (i + 1) * P) for i in range(ng)]
                tok = [slice(t0 + i * w, t0 + (i + 1) * w) for i in range(ng)]
                halves = [range(ng)] if sample else [range(0, 2), range(2, 4)]
                step, last_step = (2 * G * (gi - 1), 2 * G * gi) if gi else (-20, -20)
                for i in range(ng):
                    last = pe.matmul(k.ps[6][0:w, sl[i]], Q[:, 1, tok[i]], Q[:, 1, tok[i]], start=True, stop=True)
                last.then_inc(s["grams"], 1)
                for i in range(ng):
                    last = pe.matmul(k.ps[7][0:w, sl[i]], Q[:, 1, tok[i]], Q[:, 0, tok[i]], start=True, stop=True)
                last.then_inc(s["grams"], 1)
                recur(step)
                recur(step + 1)
                step += 2

                def turn(bank, src):
                    if gi == 0 and src == 2:
                        pe.wait_ge(s["silu_done"], 3)
                    for i in range(ng):
                        last = pe.transpose(k.ps[bank][0:w, hs[i]], Q[:, src, tok[i]], k.c("ident"))
                    last.then_inc(s["rows_turned"], 1)

                def products(todo):
                    nonlocal used, step
                    for h2, half in enumerate(halves):
                        used += 1
                        pe.wait_ge(s["operand"], used)
                        for bank, lhs, rhs in todo:
                            for i in half:
                                dst = place(bank, h2)[0:w, (i - half.start) * w:(i - half.start + 1) * w]
                                if rhs is None:
                                    last = pe.transpose(dst, lhs[0:w, sl[i]], idn)
                                else:
                                    last = pe.matmul(dst, lhs[0:w, sl[i]], rhs[0:w, sl[i]], start=True, stop=True)
                        last.then_inc(s["product"], 1)
                    if step < last_step:
                        recur(step)
                        step += 1

                products([(4, N, None)])
                turn(6, 1)
                if sample:
                    products([(5, NTr, N)])
                    turn(7, 2)
                    products([(4, N2, X0)])
                else:
                    products([(5, NTr, N), (6, N, NTr)])
                    turn(7, 2)
                    products([(5, N2T, N2), (6, N2, N2T), (4, N2, X0)])
                    products([(5, N4T, N4), (4, N4, X1)])
                    products([(4, N, X0)])
                    cur, nxt = X1, X0
                    for _l in range(3):
                        products([(5, cur, None), (6, N, cur)])
                        products([(4, NTr, N2)])
                        cur, nxt = nxt, cur
                for h2, half in enumerate(halves):
                    used += 1
                    pe.wait_ge(s["operand"], used)
                    for i in half:
                        last = pe.matmul(place(5, h2)[:, (i - half.start) * w:(i - half.start + 1) * w], Kb[0:w, hs[i]], XT[f][0:w, sl[i]], start=True, stop=True)
                    last.then_inc(s["product"], 1)
                for rest in range(step, last_step):
                    recur(rest)
                used += len(halves)
                pe.wait_ge(s["operand"], used)
            f = len(groups) % 2 ^ 1
            pe.wait_ge(s["s_loaded"], 16)
            pe.wait_ge(s["s_kept"], TILES)
            pe.matmul(k.ps[0][0:TS, 0:P], XT[f][0:TS, 0:TS], Vb[f][0:TS, 0:P], start=True, stop=False)
            for b in range(B):
                last = pe.matmul(k.ps[0][0:TS, 0:P], WK[f][:, b * TS:(b + 1) * TS], S0[:, b, :], start=False, stop=(b == B - 1))
            last.then_inc(s["u_made"], 1)
            pe.wait_ge(s["o_kept"], TILES)
            pe.wait_ge(s["u_kept"], TILES + 1)
            pe.matmul(k.ps[1][:, 0:TS], u[0:TS, :], QK[f][0:TS, 0:TS], start=True, stop=False)
            for b in range(B):
                last = pe.matmul(k.ps[1][:, b * L:(b + 1) * L], S0[:, b, :], Q[:, 0, T + b * L:T + (b + 1) * L],
                                 start=False, stop=(b == B - 1))
            last.then_inc(s["o_made"], 1)
            pe.wait_ge(s["um_ready"], 1)
            for half in range(2):
                last = pe.matmul(k.ps[2 + half][:, 0:512], Kt[f][0:TS, 0:P], grp[0:TS, 4 + half, :], start=True, stop=True)
            last.then_inc(s["sn_made"], 1)
            pe.wait_ge(s["post_sq"], 1)
            feature_sums(pe, k, sq).then_inc(s["post_ss"], 1)

        @block.vector
        def _(dve):
            d = Order(dve, s["dve_order"])
            for m in range(3):
                dve.memset(raw[:, m, 0:3], 0.0)
                last = dve.tensor_copy(raw[:, m, 3 + T:].rearrange("p (b r) -> p b r", r=7)[:, :, 0:3],
                                       k.conv_cols[:, bass.ds(h + m * H, 1), 0:24].rearrange("p o (b r) -> p (o b) r", r=3))
            d.after(last)
            cw = k.cw_head
            for m in range(3):
                last = dve.tensor_copy(cw[:, m, :], k.conv_cols[:, bass.ds(h + m * H, 1), 24:28].rearrange("p o r -> p (o r)"))
            d.after(last)
            d.after(dve.tensor_copy(hcol[:, 0:2, :], k.gate_cols[:, :, bass.ds(h, 1), :].rearrange("p u o t -> p u (o t)")))
            def keep_rows(m):
                if m:
                    dve.wait_ge(s["conv_turned"], m)
                dve.tensor_copy(convo[:, 0:3], raw[:, m, T:T + 3])
                dve.tensor_copy(convo[:, 3:27].rearrange("p (b r) -> p b r", r=3),
                                raw[:, m, 3 + T:].rearrange("p (b r) -> p b r", r=7)[:, :, 4:7]).then_inc(s["conv_kept"], 1)

            def convolve(m, taps):
                pieces = ((Q[:, m, 0:T], lambda j: raw[:, m, j:j + T]),
                          (Q[:, m, T:NT].rearrange("p (b l) -> p b l", l=L),
                           lambda j: raw[:, m, 3 + T:].rearrange("p (b r) -> p b r", r=7)[:, :, j:j + L]))
                for j in taps:
                    for out, src in pieces:
                        if j == 0:
                            last = dve.tensor_scalar(out, src(0), cw[:, m, 0:1], None, ALU.mult)
                        else:
                            last = dve.scalar_tensor_tensor(out, src(j), cw[:, m, j:j + 1], out, ALU.mult, ALU.add)
                    d.after(last)
                if j == 3:
                    dve.engine_nop().then_inc(s["conv_done"], 1)

            def take_rows(m):
                dve.wait_ge(s["conv_turned"], m + 1)
                dve.tensor_copy(convr[:, m * P:(m + 1) * P], k.ps[7][0:27, 0:P]).then_inc(s["cols_done"], 1)

            def norm(m):
                dve.wait_ge(s["root_done"], m + 1)
                dve.scalar_tensor_tensor(Q[:, m, :], Q[:, m, :], SCALE if m == 0 else 1.0, squares[m], ALU.mult, ALU.mult).then_inc(s["normed"], 1)

            for at in range(PROJ):
                p_vector(dve, at)
                if at == 9 or at == 14 or at == 19:
                    d.after(dve.engine_nop())
                    keep_rows(at // NC - 1)
                if at == 10 or at == 15:
                    convolve(at // NC - 2, (0, 1))
                if at == 11 or at == 16:
                    convolve(at // NC - 2, (2, 3))
                if at == 12 or at == 17:
                    take_rows(at // NC - 2)
                if at == 15:
                    norm(0)
            convolve(2, (0, 1))
            norm(1)
            convolve(2, (2, 3))
            take_rows(2)
            dve.wait_ge(s["cols_done"], 3)
            dve.engine_nop().then_inc(s["conv_out"], 1)
            dve.wait_ge(s["exp_out"], 1)
            d.after(dve.tensor_tensor(hcol[:, 2, :], hcol[:, 2, :], hcol[:, 0, :], ALU.mult))
            d.after(dve.tensor_scalar(hcol[:, 3, :], hcol[:, 0, :], -1.0, None, ALU.mult))
            dve.memset(S[:, 0, :], 0.0)
            seen = 0

            def next_state(step):
                if step >= 0 and step % 2:
                    tile = step // 2
                    dve.wait_ge(s["s_made"], tile + 1)
                    if tile:
                        dve.wait_ge(s["s_kept"], tile)
                    dve.scalar_tensor_tensor(S[:, (tile + 1) % 2, :], S[:, tile % 2, :], g_tile[:, tile:tile + 1],
                                             s_bank, ALU.mult, ALU.add).then_inc(s["s_kept"], 1)

            for gi, (t0, ng, w) in enumerate(groups):
                sample = w != P
                f = gi % 2
                v3 = lambda ap, n=w: ap[0:w, 0:ng * n].rearrange("p (g n) -> p g n", g=ng)
                ti = t0 // P
                gcol = repeat(hcol[0:w, 1, ti:ti + ng], 2, w)
                mask = lambda n: repeat(k.c(n)[0:w, 0:w], 1, ng)
                row = g_row[0:w, t0:t0 + ng * w].rearrange("p (g n) -> p g n", g=ng)
                pre = "s_" if sample else ""
                halves = [range(ng)] if sample else [range(0, 2), range(2, 4)]
                step, last_step = (2 * G * (gi - 1), 2 * G * gi) if gi else (-20, -20)
                d.after(dve.tensor_tensor(v3(X0), row, gcol, ALU.subtract))
                dve.tensor_tensor(v3(X1), v3(X0), mask(pre + "not_lower"), ALU.add).then_inc(s["exp_in"], 1)
                dve.tensor_tensor(v3(DT), v3(X0), mask(pre + "not_causal"), ALU.subtract).then_inc(s["exp_in"], 1)
                dve.wait_ge(s["exp_out"], 3 * gi + 2)
                d.after(dve.tensor_tensor(v3(A), v3(X1), repeat(hcol[0:w, 3, ti:ti + ng], 2, w), ALU.mult))
                dve.wait_ge(s["grams"], 2 * gi + 1)
                d.after(dve.tensor_tensor(v3(A), v3(k.ps[6]), v3(A), ALU.mult))
                if sample:
                    dve.tensor_copy(v3(N), v3(A)).then_inc(s["operand"], 1)
                else:
                    dve.tensor_tensor(v3(N), v3(A), mask("diag16"), ALU.mult).then_inc(s["operand"], 2)
                dve.wait_ge(s["exp_out"], 3 * gi + 4)
                dve.wait_ge(s["grams"], 2 * gi + 2)
                dve.tensor_tensor(v3(QK[f]), v3(k.ps[7]), v3(DT), ALU.mult)
                next_state(step + 1)
                step += 2

                def others():
                    kt = lambda ap: v3(ap, P)
                    dve.wait_ge(s["rows_turned"], 2 * gi + 1)
                    dve.tensor_tensor(kt(Kb), kt(k.ps[6]), repeat(hcol[0:w, 2, ti:ti + ng], 2, P), ALU.mult)
                    dve.tensor_tensor(Q[:, 0, t0:t0 + ng * w], Q[:, 0, t0:t0 + ng * w], g_exp[:, 0:ng * w], ALU.mult)
                    if sample:
                        d.after(dve.tensor_tensor(N4[0:w, 0:w], DT[0:w, 0:w], k.c("s_last")[0:w, :], ALU.mult))
                        d.after(dve.tensor_reduce(tail, N4[0:w, 0:w], X, ALU.add))
                        dve.tensor_scalar(Kt[f][0:w, 0:P], k.ps[6][0:w, 0:P], tail, None, ALU.mult)
                    else:
                        dve.tensor_tensor(kt(Kt[f]), kt(k.ps[6]), repeat(DT.rearrange("p (g n) -> p g n", g=ng)[:, :, P - 1], 2, P), ALU.mult)
                    dve.wait_ge(s["rows_turned"], 2 * gi + 2)
                    dve.tensor_tensor(kt(Vb[f]), kt(k.ps[7]), repeat(hcol[0:w, 0, ti:ti + ng], 2, P), ALU.mult)

                def part(ap, half, n=w):
                    return ap[0:w, half.start * n:half.stop * n].rearrange("p (g n) -> p g n", n=n)

                def take(todo):
                    nonlocal seen, step
                    for h2, half in enumerate(halves):
                        seen += 1
                        dve.wait_ge(s["product"], seen)
                        for fn in todo:
                            last = fn(h2, half)
                        last.then_inc(s["operand"], 1)
                    if step < last_step:
                        next_state(step)
                        step += 1

                hmask = lambda n, half: repeat(k.c(n)[0:w, 0:w], 1, len(half))
                made = lambda bank, h2, half: place(bank, h2)[0:w, 0:len(half) * w].rearrange("p (g n) -> p g n", n=w)
                cp = lambda dst, bank: (lambda h2, half: dve.tensor_copy(part(dst, half), made(bank, h2, half)))
                plus = lambda dst, src, bank: (lambda h2, half: dve.tensor_tensor(part(dst, half), part(src, half), made(bank, h2, half), ALU.add))
                times = lambda dst, src, m: (lambda h2, half: dve.tensor_tensor(part(dst, half), part(src, half), hmask(m, half), ALU.mult))
                take([cp(NTr, 4), lambda h2, half: dve.tensor_tensor(part(X0, half), made(4, h2, half), hmask("ident", half), ALU.add)])
                if sample:
                    take([cp(N2, 5)])
                    others()
                    take([plus(XT[f], X0, 4)])
                else:
                    take([cp(N2, 5), cp(N2T, 6)])
                    others()
                    take([cp(N4, 5), cp(N4T, 6), plus(X1, X0, 4)])
                    take([cp(N, 5), plus(X0, X1, 4)])
                    take([plus(X1, X0, 4), times(N, A, "under32")])
                    cur, nxt = X1, X0
                    for lvl in (32, 64, 128):
                        take([cp(NTr, 5), cp(N2, 6)])
                        if lvl < 128:
                            take([plus(nxt, cur, 4), times(N, A, f"under{2 * lvl}")])
                        else:
                            take([plus(XT[f], cur, 4)])
                        cur, nxt = nxt, cur
                for h2, half in enumerate(halves):
                    seen += 1
                    dve.wait_ge(s["product"], seen)
                    if not sample:
                        dve.tensor_scalar(part(WK[f], half), made(5, h2, half), -1.0, None, ALU.mult).then_inc(s["operand"], 1)
                    else:
                        dve.scalar_tensor_tensor(WK[f][:, 0:B * TS].rearrange("p (b t) -> p b t", b=B), repeat(place(5, 0)[:, 0:TS], 1, B), -1.0,
                                                 k.c("s_cols").rearrange("p (b t) -> p b t", b=B), ALU.mult, ALU.mult).then_inc(s["operand"], 1)
                for rest in range(step, last_step):
                    next_state(rest)
            dve.wait_ge(s["u_kept"], TILES + 1)
            for half in range(2):
                last = dve.tensor_tensor(grp[0:TS, 4 + half, :].rearrange("p (b v) -> p b v", b=4), repeat(u[0:TS, :], 1, 4),
                                         repeat(k.c("s_rows")[0:TS, 4 * half:4 * half + 4], 2, P), ALU.mult)
            last.then_inc(s["um_ready"], 1)
            dve.wait_ge(s["o_made"], TILES + 1)
            d.after(dve.tensor_tensor(S0, S0, repeat(g_tile[:, TILES:], 2, P), ALU.mult))
            dve.wait_ge(s["sn_made"], 1)
            for half in range(2):
                last = dve.tensor_tensor(S0[:, 4 * half:4 * half + 4, :], S0[:, 4 * half:4 * half + 4, :],
                                         k.ps[2 + half].rearrange("p (b v) -> p b v", b=4), ALU.add)
            last.then_inc(s["sn_kept"], 1)
            dve.wait_ge(s["o_kept"], TILES + 1)
            dve.tensor_tensor(sq, O, O, ALU.mult).then_inc(s["post_sq"], 1)
            dve.wait_ge(s["post_root"], 1)
            d.after(dve.scalar_tensor_tensor(O, O, k.vec[:, 0:1], sq, ALU.mult, ALU.mult))
            dve.wait_ge(s["gate_done"], 1)
            dve.tensor_tensor(O, O, Q[:, 3, :], ALU.mult).then_inc(s["post_ready"], 1)

        @block.scalar
        def _(act):
            a = Order(act, s["act_order"])
            for b in (h, h + H):
                for dst, src in ((io.out_win_k_sample, io.cache_win_k), (io.out_win_v_sample, io.cache_win_v)):
                    act.dma_start(dst[0, bass.ds(b, 1), 0:WBUF - L].rearrange("b (g r) h d -> (b g) (r h d)", g=28),
                                  src[0, bass.ds(b, 1), L:WBUF].rearrange("b (g r) h d -> (b g) (r h d)", g=28)).then_inc(k.windows_shifted, 16)
            act.wait_ge(w_sems[3], NC)
            act.activation(Q[:, 3, :], Q[:, 3, :], ACT.Silu).then_inc(s["gate_done"], 1)
            for m in range(2):
                act.wait_ge(s["conv_done"], m + 1)
                act.activation(Q[:, m, :], Q[:, m, :], ACT.Silu).then_inc(s["silu_done"], 1)
                act.wait_ge(s["silu_done"], m + 1)
                act.activation(squares[m], Q[:, m, :], ACT.Square).then_inc(s["sq_done"], 1)
                act.wait_ge(s["ss_done"], m + 1)
                for n in range(NC):
                    act.activation(squares[m][:, n * CH:(n + 1) * CH], k.ps[SUMS + n][:, 0:CH], ACT.Ln, bias=k.eps).then_inc(s["ln_done"], 1)
                act.wait_ge(s["ln_done"], (m + 1) * NC)
                act.activation(squares[m], squares[m], ACT.Exp, scale=-0.5).then_inc(s["root_done"], 1)
                if m == 0:
                    act.wait_ge(s["g_loaded"], 16)
                    act.activation(g_tile[:, 0:TILES], g_row[:, P - 1:T:P], ACT.Exp)
                    act.activation(g_tile[:, TILES:], g_row[:, T + L - 1::L], ACT.Exp)
                    act.activation(hcol[:, 2, :], hcol[:, 1, :], ACT.Exp).then_inc(s["exp_out"], 1)
            act.wait_ge(s["conv_done"], 3)
            act.activation(Q[:, 2, :], Q[:, 2, :], ACT.Silu).then_inc(s["silu_done"], 1)
            for gi, (t0, ng, w) in enumerate(groups):
                act.wait_ge(s["exp_in"], 2 * gi + 1)
                act.activation(X1[0:w, 0:ng * w], X1[0:w, 0:ng * w], ACT.Exp, scale=-1.0).then_inc(s["exp_out"], 1)
                act.wait_ge(s["exp_in"], 2 * gi + 2)
                act.activation(DT[0:w, 0:ng * w], DT[0:w, 0:ng * w], ACT.Exp).then_inc(s["exp_out"], 1)
                act.activation(g_exp[:, 0:ng * w], g_row[:, t0:t0 + ng * w], ACT.Exp).then_inc(s["exp_out"], 1)
                for tile in range(G * (gi - 1), G * gi) if gi else ():
                    act.wait_ge(s["u_made"], tile + 1)
                    act.copy(u, u_bank).then_inc(s["u_kept"], 1)
                    act.wait_ge(s["o_made"], tile + 1)
                    act.copy(O[:, tile * P:(tile + 1) * P], o_bank).then_inc(s["o_kept"], 1)
            act.wait_ge(s["u_made"], TILES + 1)
            act.copy(u[0:TS, :], k.ps[0][0:TS, 0:P]).then_inc(s["u_kept"], 1)
            act.wait_ge(s["o_made"], TILES + 1)
            act.copy(O[:, T:NT], k.ps[1][:, 0:TS]).then_inc(s["o_kept"], 1)
            act.wait_ge(s["post_ss"], 1)
            for n in range(NC):
                last = act.activation(sq[:, n * CH:(n + 1) * CH], k.ps[SUMS + n][:, 0:CH], ACT.Ln, bias=k.eps, scale=1.0 / P)
            a.after(last)
            act.activation(sq, sq, ACT.Exp, scale=-0.5).then_inc(s["post_root"], 1)
    clear(nc, w_sems + list(s.values()))


def head_B(nc, k, io, h):
    with ExitStack() as c:
        sbuf = lambda n, s: c.enter_context(nc.sbuf_tensor(n, s, F32))[:]
        sem = lambda n: c.enter_context(nc.semaphore(n))
        ret = sbuf("ret", [P, RET])
        buf = sbuf("retbuf", [P, 2, 3, G * P])
        R = sbuf("R", [P, 2, P])
        R0 = sbuf("R0", [P, B, P])
        vm = sbuf("vm", [TS, B, P])
        sq, O, mean = sbuf("sqB", [P, NT]), sbuf("OB", [P, NT]), k.qd
        bn = sbuf("bn", [P, 1])
        Q = k.qkvz
        qd = k.qd
        w_sems, p_sync, p_pool, p_tensor, p_vector = project_head(
            nc, k, io, c, "B", h, lambda m, n: [(Q[:, m, n * CH:(n + 1) * CH], 0, CH)])
        names = ["ret_loaded", "r0_loaded", "qd_ready", "turned_b", "tiles_b", "o_made", "r_made", "r_kept", "o_kept_b",
                 "so_made", "rn_made", "rn_kept", "gate_b", "mean_in", "mean_out", "var_in", "var_out", "root_b", "post_b",
                 "stored_b", "order_b", "act_b"]
        s = {n: sem(n) for n in names}
        block = c.enter_context(nc.Block())
        groups = [(g * G * P, G, P) for g in range(TILES // G)] + [(T, 1, TS)]

        @block.sync
        def _(sp):
            sp.dma_start(ret, io.c_ret[bass.ds(h, 1)].rearrange("o p n -> (o p) n")).then_inc(s["ret_loaded"], 16)
            sp.dma_start(R0, io.state_ret[0, :, bass.ds(h, 1), :, :].rearrange("b o k v -> k (b o) v")).then_inc(s["r0_loaded"], 16)
            sp.wait_ge(w_sems[2], 4 * NC)
            p_sync(sp)
            sp.wait_ge(s["r_kept"], TILES)
            sp.dma_start(io.out_ret_prompt[0, 0, bass.ds(h, 1)].rearrange("o k v -> (o k) v"), R[:, TILES % 2, :]).then_inc(s["stored_b"], 16)
            sp.wait_ge(s["rn_kept"], 1)
            sp.dma_start(io.out_ret_sample[0, :, bass.ds(h, 1), :, :].rearrange("b o k v -> k (b o) v"), R0).then_inc(s["stored_b"], 16)
            sp.wait_ge(s["post_b"], 1)
            sp.dma_start(io.scr_o[bass.ds(h + H, 1)].rearrange("o p n -> (o p) n"), O).then_inc(s["stored_b"], 16)
            sp.wait_ge(s["stored_b"], 16 * 3)

        @block.gpsimd
        def _(pool):
            p_pool(pool)

        @block.tensor
        def _(pe):
            for at in range(PROJ):
                p_tensor(pe, at)
            tile = 0
            for gi, (t0, ng, w) in enumerate(groups):
                hs = [slice(i * P, (i + 1) * P) for i in range(ng)]
                sl = [slice(i * w, (i + 1) * w) for i in range(ng)]
                tok = [slice(t0 + i * w, t0 + (i + 1) * w) for i in range(ng)]
                Ktl, V, PT = [buf[:, gi % 2, i, :] for i in range(3)]
                if gi == 0:
                    pe.wait_ge(s["qd_ready"], 1)
                    pe.wait_ge(w_sems[3], PROJ)
                if gi:
                    pe.wait_ge(s["tiles_b"], gi)
                for i in range(ng):
                    pe.transpose(k.ps[2][0:w, hs[i]], Q[:, 1, tok[i]], k.c("ident"))
                    pe.transpose(k.ps[3][0:w, hs[i]], Q[:, 2, tok[i]], k.c("ident"))
                    last = pe.matmul(k.ps[4][0:w, sl[i]], Q[:, 1, tok[i]], Q[:, 0, tok[i]], start=True, stop=True)
                last.then_inc(s["turned_b"], 1)
                pe.wait_ge(s["tiles_b"], gi + 1)
                if w == P:
                    for i in range(ng):
                        if tile >= 2:
                            pe.wait_ge(s["r_kept"], tile - 1)
                        pe.matmul(k.ps[tile % 2][:, 0:P], Ktl[:, hs[i]], V[:, hs[i]], start=True, stop=True).then_inc(s["r_made"], 1)
                        if tile >= 2:
                            pe.wait_ge(s["o_kept_b"], tile - 1)
                        pe.matmul(k.ps[6 + tile % 2][:, 0:P], V[:, hs[i]], PT[:, sl[i]], start=True, stop=False)
                        pe.wait_ge(s["r_kept"], tile) if tile else None
                        pe.matmul(k.ps[6 + tile % 2][:, 0:P], R[:, tile % 2, :], qd[:, tok[i]], start=False, stop=True).then_inc(s["o_made"], 1)
                        tile += 1
                else:
                    pe.wait_ge(s["r0_loaded"], 16)
                    pe.wait_ge(s["o_kept_b"], tile)
                    pe.wait_ge(s["r_kept"], tile)
                    pe.matmul(k.ps[6][:, 0:TS], V[0:TS, 0:P], PT[0:TS, 0:TS], start=True, stop=False)
                    for b in range(B):
                        last = pe.matmul(k.ps[6][:, b * L:(b + 1) * L], R0[:, b, :], qd[:, T + b * L:T + (b + 1) * L],
                                         start=False, stop=(b == B - 1))
                    last.then_inc(s["o_made"], 1)
                    for half in range(2):
                        last = pe.matmul(k.ps[half], Ktl[0:TS, 0:P], vm[:, 4 * half:4 * half + 4, :].rearrange("p b v -> p (b v)"),
                                         start=True, stop=True)
                    last.then_inc(s["rn_made"], 1)
            pe.wait_ge(s["rn_kept"], 1)
            pe.wait_ge(s["o_kept_b"], TILES + 1)
            feature_sums(pe, k, O).then_inc(s["mean_in"], 1)
            pe.wait_ge(s["var_in"], 1)
            feature_sums(pe, k, sq).then_inc(s["var_out"], 1)

        @block.vector
        def _(dve):
            d = Order(dve, s["order_b"])
            dve.memset(R[:, 0, :], 0.0)
            dve.tensor_copy(bn, k.b_norm[:, bass.ds(h, 1)])
            for at in range(2 * NC):
                p_vector(dve, at)
            dve.wait_ge(w_sems[3], 2 * NC)
            dve.wait_ge(s["ret_loaded"], 16)
            dve.tensor_tensor(qd[:, 0:T].rearrange("p (t n) -> p t n", n=P), Q[:, 0, 0:T].rearrange("p (t n) -> p t n", n=P),
                              repeat(ret[:, P:2 * P], 1, TILES), ALU.mult)
            dve.tensor_tensor(qd[:, T:NT], Q[:, 0, T:NT], ret[:, 290:322], ALU.mult).then_inc(s["qd_ready"], 1)
            for at in range(2 * NC, PROJ):
                p_vector(dve, at)
            tile = 0
            for gi, (t0, ng, w) in enumerate(groups):
                Ktl, V, PT = [buf[:, gi % 2, i, :] for i in range(3)]
                dve.wait_ge(s["turned_b"], gi + 1)
                if w == P:
                    if gi >= 2:
                        dve.wait_ge(s["o_made"], (gi - 1) * G)
                    dve.tensor_copy(V, k.ps[3])
                    dve.tensor_scalar(Ktl, k.ps[2], ret[:, 256:257], None, ALU.mult)
                    dve.tensor_tensor(PT.rearrange("p (g n) -> p g n", g=G), k.ps[4].rearrange("p (g n) -> p g n", g=G),
                                      repeat(ret[:, 0:P], 1, G), ALU.mult).then_inc(s["tiles_b"], 1)
                    for i in range(ng):
                        dve.wait_ge(s["r_made"], tile + 1)
                        if tile >= 1:
                            dve.wait_ge(s["o_made"], tile)
                            dve.wait_ge(s["r_kept"], tile)
                        dve.scalar_tensor_tensor(R[:, (tile + 1) % 2, :], R[:, tile % 2, :], ret[:, 257:258], k.ps[tile % 2][:, 0:P],
                                                 ALU.mult, ALU.add).then_inc(s["r_kept"], 1)
                        tile += 1
                else:
                    d.after(dve.tensor_copy(V[0:TS, 0:P], k.ps[3][0:TS, 0:P]))
                    dve.tensor_tensor(vm, repeat(V[0:TS, 0:P], 1, B), repeat(k.c("s_rows")[0:TS, :], 2, P), ALU.mult)
                    dve.tensor_scalar(Ktl[0:TS, 0:P], k.ps[2][0:TS, 0:P], ret[0:TS, 322:323], None, ALU.mult)
                    dve.tensor_tensor(PT[0:TS, 0:TS], k.ps[4][0:TS, 0:TS], ret[0:TS, 258:290], ALU.mult).then_inc(s["tiles_b"], 1)
                    dve.wait_ge(s["rn_made"], 1)
                    for half in range(2):
                        last = dve.scalar_tensor_tensor(R0[:, 4 * half:4 * half + 4, :], R0[:, 4 * half:4 * half + 4, :], ret[:, 323:324],
                                                        k.ps[half].rearrange("p (b v) -> p b v", b=4), ALU.mult, ALU.add)
                    last.then_inc(s["rn_kept"], 1)
            dve.wait_ge(s["mean_in"], 1)
            for n in range(NC):
                a, b = n * CH, (n + 1) * CH
                last = dve.scalar_tensor_tensor(O[:, a:b], k.ps[SUMS + n][:, 0:CH], -1.0 / P, O[:, a:b], ALU.mult, ALU.add)
            d.after(last)
            dve.tensor_tensor(sq, O, O, ALU.mult).then_inc(s["var_in"], 1)
            dve.wait_ge(s["root_b"], 1)
            d.after(dve.scalar_tensor_tensor(O, O, bn, sq, ALU.mult, ALU.mult))
            dve.wait_ge(s["gate_b"], 1)
            dve.tensor_tensor(O, O, Q[:, 3, :], ALU.mult).then_inc(s["post_b"], 1)

        @block.scalar
        def _(act):
            a = Order(act, s["act_b"])
            act.wait_ge(w_sems[3], NC)
            act.activation(Q[:, 3, :], Q[:, 3, :], ACT.Silu).then_inc(s["gate_b"], 1)
            tile = 0
            for gi, (t0, ng, w) in enumerate(groups):
                for i in range(ng):
                    act.wait_ge(s["o_made"], tile + 1)
                    act.copy(O[:, t0 + i * w:t0 + (i + 1) * w], k.ps[6 + tile % 2][:, 0:w]).then_inc(s["o_kept_b"], 1)
                    tile += 1
            act.wait_ge(s["var_out"], 1)
            for n in range(NC):
                last = act.activation(sq[:, n * CH:(n + 1) * CH], k.ps[SUMS + n][:, 0:CH], ACT.Ln, bias=k.eps, scale=1.0 / P)
            a.after(last)
            act.activation(sq, sq, ACT.Exp, scale=-0.5).then_inc(s["root_b"], 1)
    clear(nc, w_sems + list(s.values()))


def output_projection(nc, k, io, layer):
    with ExitStack() as c:
        sem = lambda n: c.enter_context(nc.semaphore(f"{n}_{layer}"))
        wout = c.enter_context(nc.sbuf_tensor(f"wout{layer}", [P, KT, D_MODEL], F32))[:]
        o = k.big[:, 0:2 * KT * CH].rearrange("p (s k n) -> p s k n", s=2, k=KT)
        wo_loaded, o_loaded = sem("wo_loaded"), [sem("o_loaded0"), sem("o_loaded1")]
        y_made, y_added = sem("y_made"), sem("y_added")
        block = c.enter_context(nc.Block())
        w = io.w_out_even[0] if layer == 0 else io.w_out_odd[0]

        @block.sync
        def _(sp):
            sp.dma_start(wout, w.rearrange("(k p) n -> p k n", p=P)).then_inc(wo_loaded, 16)
            for n in range(NC):
                if n >= 2:
                    sp.wait_ge(y_made, (n - 1) * KT)
                sp.dma_start(o[:, n % 2], io.scr_o[:, :, n * CH:(n + 1) * CH].rearrange("k p n -> p k n")).then_inc(o_loaded[n % 2], 16)

        @block.tensor
        def _(pe):
            pe.wait_ge(wo_loaded, 16)
            for n in range(NC):
                pe.wait_ge(o_loaded[n % 2], 16 * (n // 2 + 1))
                for m in range(KT):
                    at = n * KT + m
                    if at >= 4:
                        pe.wait_ge(y_added, at - 3)
                    for j in range(KT):
                        last = pe.matmul(k.ps[at % 4][:, 0:CH], wout[:, j, m * P:(m + 1) * P], o[:, n % 2, j, :],
                                         start=(j == 0), stop=(j == KT - 1))
                    last.then_inc(y_made, 1)

        @block.vector
        def _(dve):
            for n in range(NC):
                for m in range(KT):
                    at = n * KT + m
                    dve.wait_ge(y_made, at + 1)
                    x = k.xT[:, m, n * CH:(n + 1) * CH]
                    dve.tensor_tensor(x, x, k.ps[at % 4][:, 0:CH], ALU.add).then_inc(y_added, 1)
    clear(nc, [wo_loaded, *o_loaded, y_made, y_added])


def row_gates_odd(nc, k, io):
    with ExitStack() as c:
        sem = lambda n: c.enter_context(nc.semaphore(n))
        w_loaded, w_scaled = sem("fw_loaded"), sem("fw_scaled")
        row_ready, row_taken = sem("f_row_ready"), sem("f_row_taken")
        a_step, d_step = sem("f_act"), sem("f_dve")
        turned, cols_ready, stored = sem("f_turned"), sem("f_cols"), sem("f_stored")
        w = c.enter_context(nc.sbuf_tensor("fw", [P, KT, 4], F32))
        rows = c.enter_context(nc.sbuf_tensor("frows", [4, NT], F32))
        tmp = c.enter_context(nc.sbuf_tensor("ftmp", [4, NT], F32))
        one = c.enter_context(nc.sbuf_tensor("fones", [4, T], F32))
        block = c.enter_context(nc.Block())

        @block.sync
        def _(sp):
            sp.dma_start(w[:, :, :], io.w_in_odd[0].rearrange("(k p) c -> p k c", p=P)[:, :, 2048:2052]).then_inc(w_loaded, 16)
            sp.wait_ge(d_step, 4)
            sp.dma_start(io.scr_f, tmp[:, 0:T]).then_inc(stored, 16)
            sp.wait_ge(cols_ready, 1)
            sp.dma_start(io.out_fox_logf_prompt[0, 0].rearrange("(t p) h -> p t h", p=P), k.logf_cols[:, 0:TILES, :]).then_inc(stored, 16)
            sp.dma_start(io.out_fox_logf_sample.rearrange("b o l h -> (b o l) h"), k.logf_cols[0:TS, TILES, :]).then_inc(stored, 16)
            sp.wait_ge(stored, 48)

        @block.vector
        def _(dve):
            dve.memset(one[:, :], 1.0)
            dve.wait_ge(w_loaded, 16)
            dve.tensor_tensor(w[:, :, :], w[:, :, :], repeat(k.g_odd, 2, 4), ALU.mult).then_inc(w_scaled, 1)
            for n in range(NC):
                dve.wait_ge(row_ready, n + 1)
                dve.tensor_tensor(rows[:, n * CH:(n + 1) * CH], k.ps[n % 2][0:4, 0:CH], k.rstd[0:4, n * CH:(n + 1) * CH],
                                  ALU.mult).then_inc(row_taken, 1)
            dve.wait_ge(a_step, 3)
            dve.tensor_scalar(rows[:, :], rows[:, :], k.small[0:4, 2:3], 0.0, ALU.add, ALU.min).then_inc(d_step, 1)
            dve.wait_ge(d_step, 1)
            dve.tensor_tensor(rows[:, :], rows[:, :], tmp[:, :], ALU.subtract).then_inc(d_step, 1)
            dve.wait_ge(d_step, 2)
            dve.tensor_tensor_scan(tmp[:, 0:T], one[:, :], rows[:, 0:T], 0.0, ALU.mult, ALU.add).then_inc(d_step, 1)
            dve.wait_ge(d_step, 3)
            dve.tensor_scalar(tmp[:, 0:T], tmp[:, 0:T], -1.0, None, ALU.mult).then_inc(d_step, 1)
            dve.wait_ge(turned, 1)
            dve.tensor_copy(k.logf_cols.rearrange("p t h -> p (t h)"), k.ps[2][:, 0:68]).then_inc(cols_ready, 1)

        @block.scalar
        def _(act):
            act.wait_ge(row_taken, NC)
            act.activation(tmp[:, :], rows[:, :], ACT.Abs, bias=k.small[0:4, 2:3]).then_inc(a_step, 1)
            act.wait_ge(a_step, 1)
            act.activation(tmp[:, :], tmp[:, :], ACT.Exp, scale=-1.0).then_inc(a_step, 1)
            act.wait_ge(a_step, 2)
            act.activation(tmp[:, :], tmp[:, :], ACT.Ln, bias=k.one[0:4, :]).then_inc(a_step, 1)

        @block.tensor
        def _(pe):
            pe.wait_ge(w_scaled, 1)
            for n in range(NC):
                if n >= 2:
                    pe.wait_ge(row_taken, n - 1)
                for j in range(KT):
                    last = pe.matmul(k.ps[n % 2][0:4, 0:CH], w[:, j, :], k.xT[:, j, n * CH:(n + 1) * CH],
                                     start=(j == 0), stop=(j == KT - 1))
                last.then_inc(row_ready, 1)
            pe.wait_ge(d_step, 2)
            pe.matmul(k.ps[2][:, 0:68], k.c("ones"), k.zero[:, 0:68], start=True, stop=True)
            for t in range(TILES + 1):
                m = P if t < TILES else TS
                last = pe.transpose(k.ps[2][0:m, 4 * t:4 * t + 4], rows[:, t * P:t * P + m], k.c("ident")[0:4, 0:4])
            last.then_inc(turned, 1)
    clear(nc, [w_loaded, w_scaled, row_ready, row_taken, a_step, d_step, turned, cols_ready, stored])


def head_attention(nc, k, io, h, branch):
    with ExitStack() as c:
        sbuf = lambda n, s: c.enter_context(nc.sbuf_tensor(f"{n}{branch}", s, F32))[:]
        sem = lambda n: c.enter_context(nc.semaphore(f"{n}_{branch}"))
        fox = branch == "C"
        ktok, vtok = sbuf("ktok", [P, TILES + 1, P]), sbuf("vtok", [P, TILES + 1, P])
        bias = sbuf("bias", [P, T])
        sc = sbuf("sc", [P, 2, T])
        wt = sbuf("wt", [P, 2, G * P])
        otok = sbuf("otok", [P, 2, P])
        qgain = sbuf("qgain", [P, 1])
        cmax, stat = sbuf("cmax", [P, 3, G]), sbuf("stat", [P, 3, 3])
        sq = sc[:, 0:2, :].rearrange("p a n -> p (a n)")[:, 0:NT]
        O = k.qd
        squares = [sq, k.qd]
        Q = k.qkvz
        slots = [sc[:, 0, :], sc[:, 1, :], Q[:, 2, 0:T]]
        keep = k.foxs if fox else k.wins
        gq, gk = (k.vec[:, 1:2], k.vec[:, 2:3]) if fox else (k.vec[:, 3:4], k.vec[:, 4:5])
        w_sems, p_sync, p_pool, p_tensor, p_vector = project_head(
            nc, k, io, c, branch, h, lambda m, n: [(Q[:, m, n * CH:(n + 1) * CH], 0, CH)])
        names = ["bias_loaded", "sq_done", "ss_done", "ln_done", "root_done", "normed", "gate_done", "kv_turned", "kv_kept",
                 "scores_made", "scores_kept", "max_ready", "exp_done", "wt_made", "wt_kept_v", "wt_kept_s", "o_made",
                 "recip_ready", "otok_ready", "o_turned", "o_done", "stored", "order", "gain_ready"]
        s = {n: sem(n) for n in names}
        block = c.enter_context(nc.Block())
        kout, vout, ks, vs = ((io.out_fox_k_prompt[0, 0], io.out_fox_v_prompt[0, 0],
                               io.out_fox_k_sample.rearrange("b o l h d -> (b o l) h d"), io.out_fox_v_sample.rearrange("b o l h d -> (b o l) h d"))
                              if fox else (io.out_win_k_prompt[0, 0], io.out_win_v_prompt[0, 0], None, None))
        n_chunks = [i // G + 1 for i in range(TILES)]
        first = [sum(n_chunks[:i]) for i in range(TILES)]
        in_chunk = lambda i, ch: min(G, i + 1 - G * ch)
        kept_by = lambda i, ch: ("wt_kept_v", sum(min(n, 2) for n in n_chunks[:i]) + ch + 1) if ch < 2 else \
            ("wt_kept_s", sum(max(n - 2, 0) for n in n_chunks[:i]) + ch - 1)
        steps = lambda i: max(n_chunks[i] + 1, n_chunks[i + 2] if i + 2 < TILES else 0, 3)

        @block.sync
        def _(sp):
            src = io.scr_f[bass.ds(h, 1), :].broadcast_to([P, T]) if fox else io.c_window[bass.ds(h, 1)].rearrange("o p n -> (o p) n")
            sp.dma_start(bias, src).then_inc(s["bias_loaded"], 16)
            sp.wait_ge(w_sems[2], 4 * NC)
            p_sync(sp)
            sp.wait_ge(s["kv_kept"], 10)
            n = 2
            for dst, ap in ((kout, ktok), (vout, vtok)):
                sp.dma_start(dst[:, bass.ds(h, 1), :].rearrange("(t p) o d -> p t (o d)", p=P), ap[:, 0:TILES, :]).then_inc(s["stored"], 16)
            if fox:
                for dst, ap in ((ks, ktok), (vs, vtok)):
                    sp.dma_start(dst[:, bass.ds(h, 1), :].rearrange("t o d -> t (o d)"), ap[0:TS, TILES, :]).then_inc(s["stored"], 16)
            else:
                for dst, ap in ((io.out_win_k_sample, ktok), (io.out_win_v_sample, vtok)):
                    for b in range(B):
                        sp.dma_start(dst[0, b, WBUF - L:WBUF, bass.ds(h, 1), :].rearrange("l o d -> l (o d)"), ap[b * L:(b + 1) * L, TILES, :]).then_inc(s["stored"], 16)
            sp.wait_ge(s["o_done"], TILES)
            sp.dma_start(io.scr_o[bass.ds(h + (0 if fox else H), 1)].rearrange("o p n -> (o p) n")[:, 0:T], O[:, 0:T]).then_inc(s["stored"], 16)
            sp.wait_ge(s["stored"], 16 * (2 + (2 if fox else 2 * B) + 1))

        @block.gpsimd
        def _(pool):
            p_pool(pool)

        @block.tensor
        def _(pe):
            for at in range(PROJ):
                p_tensor(pe, at)
                if at == 11 or at == 16:
                    m = 0 if at == 11 else 1
                    pe.wait_ge(s["sq_done"], m + 1)
                    if m:
                        pe.wait_ge(s["ln_done"], NC)
                    feature_sums(pe, k, squares[m]).then_inc(s["ss_done"], 1)
            pe.wait_ge(s["normed"], 2)
            pe.wait_ge(w_sems[3], PROJ)
            for g in range(5):
                ts = range(4 * g, min(4 * g + 4, TILES + 1))
                for which in range(2):
                    at = 2 * g + which
                    if at >= 2:
                        pe.wait_ge(s["kv_kept"], at - 1)
                    for t in ts:
                        w = P if t < TILES else TS
                        last = pe.transpose(k.ps[5 + which][0:w, (t % 4) * P:(t % 4 + 1) * P], Q[:, 1 + which, t * P:t * P + w], k.c("ident"))
                    last.then_inc(s["kv_turned"], 1)
            pe.wait_ge(s["kv_kept"], 10)

            def scores(i, ch):
                if i and ch < n_chunks[i - 1]:
                    pe.wait_ge(s["scores_kept"], first[i - 1] + ch + 1)
                j, n = G * ch, in_chunk(i, ch) * P
                diag = fox and ch == n_chunks[i] - 1
                last = pe.matmul(k.ps[ch][:, 0:n], Q[:, 0, i * P:(i + 1) * P], Q[:, 1, j * P:j * P + n], start=True, stop=not diag)
                if diag:
                    last = pe.matmul(k.ps[ch][:, n - P:n], k.c("ident"), k.c("causal_bias"), start=False, stop=True)
                last.then_inc(s["scores_made"], 1)

            def turn(i, ch):
                at = first[i] + ch
                if at >= 2:
                    i2 = i if ch >= 2 else max(x for x in range(i + 1) if first[x] <= at - 2)
                    name, count = kept_by(i2, at - 2 - first[i2])
                    pe.wait_ge(s[name], count)
                for jj in range(in_chunk(i, ch)):
                    j = G * ch + jj
                    last = pe.transpose(k.ps[4 + at % 2][:, jj * P:(jj + 1) * P], slots[i % 3][:, j * P:(j + 1) * P], k.c("ident"))
                last.then_inc(s["wt_made"], 1)

            def weigh(i, ch):
                name, count = kept_by(i, ch)
                pe.wait_ge(s[name], count)
                if ch == 0 and i >= 2:
                    pe.wait_ge(s["otok_ready"], i - 1)
                for jj in range(in_chunk(i, ch)):
                    j = G * ch + jj
                    last = pe.matmul(k.ps[6 + i % 2][:, 0:P], wt[:, (first[i] + ch) % 2, jj * P:(jj + 1) * P], vtok[:, j, :],
                                     start=(j == 0), stop=(j == i))
                if ch == n_chunks[i] - 1:
                    last.then_inc(s["o_made"], 1)

            def turn_output(i):
                pe.wait_ge(s["otok_ready"], i + 1)
                if i >= 2:
                    pe.wait_ge(s["o_done"], i - 1)
                pe.transpose(k.ps[6 + i % 2][:, P:2 * P], otok[:, i % 2, :], k.c("ident")).then_inc(s["o_turned"], 1)

            for i in range(2):
                scores(i, 0)
            for i in range(TILES):
                for step in range(steps(i)):
                    if i + 2 < TILES and step < n_chunks[i + 2]:
                        scores(i + 2, step)
                    if step == 0:
                        pe.wait_ge(s["exp_done"], i + 1)
                    if step < n_chunks[i]:
                        turn(i, step)
                    if 1 <= step <= n_chunks[i]:
                        weigh(i, step - 1)
                    if step == 1 and i:
                        turn_output(i - 1)
            turn_output(TILES - 1)

        @block.vector
        def _(dve):
            d = Order(dve, s["order"])
            dve.tensor_scalar(qgain, gq, SCALE, None, ALU.mult).then_inc(s["gain_ready"], 1)
            dve.wait_ge(s["gain_ready"], 1)
            for at in range(PROJ):
                p_vector(dve, at)
                if at == 14 or at == 18:
                    m = 0 if at == 14 else 1
                    dve.wait_ge(s["root_done"], m + 1)
                    dve.scalar_tensor_tensor(Q[:, m, :], Q[:, m, :], qgain if m == 0 else gk, squares[m], ALU.mult, ALU.mult).then_inc(s["normed"], 1)
            for g in range(5):
                n = 4 if g < 4 else 1
                w = P if g < 4 else TS
                for which, dst in ((0, ktok), (1, vtok)):
                    dve.wait_ge(s["kv_turned"], 2 * g + which + 1)
                    dve.tensor_copy(dst[0:w, 4 * g:4 * g + n, :], k.ps[5 + which][0:w, 0:n * P].rearrange("p (t d) -> p t d", t=n)).then_inc(s["kv_kept"], 1)
            dve.wait_ge(s["normed"], 2)
            dve.wait_ge(s["gate_done"], 1)
            dve.wait_ge(s["kv_kept"], 10)
            for which, src in ((0, Q[:, 0, T:NT]), (1, Q[:, 1, T:NT]), (2, Q[:, 3, T:NT])):
                dve.tensor_copy(keep[:, which, bass.ds(h, 1), :].rearrange("p o t -> p (o t)"), src)
            dve.tensor_copy((k.foxv if fox else k.winv)[:, bass.ds(h, 1), :].rearrange("t o d -> t (o d)"), vtok[0:TS, TILES, :])
            dve.wait_ge(s["bias_loaded"], 16)

            def soften(i, ch):
                j, n = G * ch, in_chunk(i, ch) * P
                dve.wait_ge(s["scores_made"], first[i] + ch + 1)
                if i >= 3 and ch == 0:
                    dve.wait_ge(s["o_made"], i - 2)
                at = j * P + (0 if fox else T - (i + 1) * P)
                dve.tensor_tensor_reduce(slots[i % 3][:, j * P:j * P + n], k.ps[ch][:, 0:n], bias[:, at:at + n], 1.0, -3e38,
                                         ALU.add, ALU.max, cmax[:, i % 3, ch:ch + 1]).then_inc(s["scores_kept"], 1)

            def maximum(i):
                dve.wait_ge(s["scores_kept"], first[i] + n_chunks[i])
                d.after(dve.tensor_reduce(stat[:, i % 3, 0:1], cmax[:, i % 3, 0:n_chunks[i]], X, ALU.max))
                dve.tensor_scalar(stat[:, i % 3, 0:1], stat[:, i % 3, 0:1], -1.0, None, ALU.mult).then_inc(s["max_ready"], 1)

            for i in range(2):
                soften(i, 0)
                maximum(i)
            for i in range(TILES + 1):
                for step in range(steps(i) if i < TILES else 3):
                    if i + 2 < TILES and step < n_chunks[i + 2]:
                        soften(i + 2, step)
                    if i < TILES and step < min(2, n_chunks[i]):
                        at = first[i] + step
                        n = in_chunk(i, step) * P
                        dve.wait_ge(s["wt_made"], at + 1)
                        dve.tensor_copy(wt[:, at % 2, 0:n], k.ps[4 + at % 2][:, 0:n]).then_inc(s["wt_kept_v"], 1)
                    if step == 0 and i:
                        dve.wait_ge(s["exp_done"], i)
                        dve.reciprocal(stat[:, (i - 1) % 3, 2:3], stat[:, (i - 1) % 3, 1:2]).then_inc(s["recip_ready"], 1)
                        dve.wait_ge(s["recip_ready"], i)
                        dve.wait_ge(s["o_made"], i)
                        dve.tensor_scalar(otok[:, (i - 1) % 2, :], k.ps[6 + (i - 1) % 2][:, 0:P], stat[:, (i - 1) % 3, 2:3], None,
                                          ALU.mult).then_inc(s["otok_ready"], 1)
                    if step == 2 and i:
                        dve.wait_ge(s["o_turned"], i)
                        dve.tensor_tensor(O[:, (i - 1) * P:i * P], k.ps[6 + (i - 1) % 2][:, P:2 * P], Q[:, 3, (i - 1) * P:i * P],
                                          ALU.mult).then_inc(s["o_done"], 1)
                if i + 2 < TILES:
                    maximum(i + 2)

        @block.scalar
        def _(act):
            act.wait_ge(w_sems[3], NC)
            act.activation(Q[:, 3, :], Q[:, 3, :], ACT.Silu).then_inc(s["gate_done"], 1)
            for m in range(2):
                act.wait_ge(w_sems[3], (m + 2) * NC)
                act.activation(squares[m], Q[:, m, :], ACT.Square).then_inc(s["sq_done"], 1)
                act.wait_ge(s["ss_done"], m + 1)
                for n in range(NC):
                    act.activation(squares[m][:, n * CH:(n + 1) * CH], k.ps[SUMS + n][:, 0:CH], ACT.Ln, bias=k.eps, scale=1.0 / P).then_inc(s["ln_done"], 1)
                act.wait_ge(s["ln_done"], (m + 1) * NC)
                act.activation(squares[m], squares[m], ACT.Exp, scale=-0.5).then_inc(s["root_done"], 1)

            def soft(i):
                n = (i + 1) * P
                act.wait_ge(s["max_ready"], i + 1)
                act.activation(slots[i % 3][:, 0:n], slots[i % 3][:, 0:n], ACT.Exp, bias=stat[:, i % 3, 0:1],
                               accum_out=stat[:, i % 3, 1:2]).then_inc(s["exp_done"], 1)

            soft(0)
            for i in range(TILES):
                if i + 1 < TILES:
                    soft(i + 1)
                for ch in range(2, n_chunks[i]):
                    at = first[i] + ch
                    n = in_chunk(i, ch) * P
                    act.wait_ge(s["wt_made"], at + 1)
                    act.copy(wt[:, at % 2, 0:n], k.ps[4 + at % 2][:, 0:n]).then_inc(s["wt_kept_s"], 1)
    clear(nc, w_sems + list(s.values()))


def sample_new_scores(nc, k, io):
    with ExitStack() as c:
        sem = lambda n: c.enter_context(nc.semaphore(n))
        prefix, dot, negated, centred = sem("new_prefix"), sem("new_dot"), sem("new_negated"), sem("new_centred")
        col = c.enter_context(nc.sbuf_tensor("newcol", [TS, H], F32))[:]
        block = c.enter_context(nc.Block())

        @block.tensor
        def _(pe):
            pe.matmul(k.ps[0][0:TS, 0:H], k.c("s_prefix")[0:TS, :], k.logf_cols[0:TS, TILES, :], start=True, stop=True).then_inc(prefix, 1)
            for f, keep in enumerate((k.foxs, k.wins)):
                for hh in range(H):
                    last = pe.matmul(k.ps[1 + f][0:TS, hh * TS:(hh + 1) * TS], keep[:, 1, hh, :], keep[:, 0, hh, :], start=True, stop=True)
                last.then_inc(dot, 1)

        @block.vector
        def _(dve):
            dve.memset(k.sc_all[:, :, :], -BIG)
            dve.memset(k.qpad[:, :, :, :], 0.0)
            dve.wait_ge(prefix, 1)
            dve.tensor_scalar(col, k.ps[0][0:TS, 0:H], -1.0, None, ALU.mult).then_inc(negated, 1)
            dve.wait_ge(dot, 2)
            dve.wait_ge(negated, 1)
            dve.tensor_tensor(k.snew[:, 0], k.ps[1][0:TS, 0:P].rearrange("p (h t) -> p h t", h=H), repeat(col, 2, TS), ALU.add).then_inc(centred, 1)
            dve.wait_ge(centred, 1)
            dve.tensor_tensor(k.snew[:, 0], k.snew[:, 0], repeat(k.c("s_bias")[0:TS, :], 1, H), ALU.add)
            dve.tensor_tensor(k.snew[:, 1], k.ps[2][0:TS, 0:P].rearrange("p (h t) -> p h t", h=H),
                              k.c("s_window")[0:TS, :].rearrange("p (h t) -> p h t", h=H), ALU.add)
    clear(nc, [prefix, dot, negated, centred])


def sample_attention(nc, k, io, b):
    with ExitStack() as c:
        sbuf = lambda n, s: c.enter_context(nc.sbuf_tensor(n, s, F32))[:]
        sem = lambda n: c.enter_context(nc.semaphore(n))
        RING = 4
        ITEMS = NPG + WT
        GR = 4 * H
        GROUPS = -(-ITEMS // G)
        FOX_GROUPS = NPG // G
        kring, kt = sbuf("kring", [P, RING, HD]), sbuf("kt", [P, 2, H, G * P])
        srow = sbuf("srow", [GR, 2, G * P])
        vwin = sbuf("vwin", [P, WT, HD])
        vslot = [k.big[:, i * HD:(i + 1) * HD] for i in range(28)] + [k.rstd[:, i * HD:(i + 1) * HD] for i in range(4)]
        pr = sbuf("pr", [P, NPG + 1 + WT + 1, GR])
        lfp = sbuf("lfp", [NPG, PAGE * H])
        lft, pre, later, fbias = [sbuf(n, [P, H * NPG]) for n in ("lft", "pre", "later", "fbias")]
        mx, sm, mrow, mdiag, rs = sbuf("mx", [P, 2, GR]), sbuf("sm", [P, 2, GR]), sbuf("mrow", [GR, 2]), sbuf("mdiag", [GR, 2, GR]), sbuf("rs", [P, 2, GR])
        ov, res = srow, sbuf("res", [P, 2, GR])
        k_loaded = [sem(f"k_loaded{i}") for i in range(RING)]
        VG = 8
        v_loaded = [sem(f"v_loaded{i}") for i in range(NPG // VG)]
        names = ["vw_loaded", "lf_loaded", "k_turned", "kt_kept_v", "kt_kept_s", "rows_made", "rows_kept",
                 "scores_turned", "q_ready", "lf_turned", "later_ready", "fbias_made", "max_cols", "max_turned",
                 "max_diag", "max_made", "shifted", "exp_done", "sums_ready", "sums_made", "pv_made", "ov_ready", "ot_made",
                 "order"]
        s = {n: sem(n) for n in names}
        block = c.enter_context(nc.Block())
        sc = k.sc_all
        kf, vf = io.cache_fox_k.rearrange("n o t h d -> n t (o h d)"), io.cache_fox_v.rearrange("n o t h d -> n t (o h d)")
        lf = io.cache_fox_logf.rearrange("n o t h -> n (o t h)")
        kw, vw = (a[0].rearrange("b r h d -> b r (h d)") for a in (io.cache_win_k, io.cache_win_v))
        by_act = lambda p: p % 2 == 1 or p >= 36
        kept_by = lambda p: ("kt_kept_s" if by_act(p) else "kt_kept_v", sum(by_act(x) == by_act(p) for x in range(p + 1)))
        in_group = lambda g: min(G, ITEMS - G * g)
        parts = (slice(0, NPG + 1), slice(NPG + 1, NPG + 2 + WT))
        scores_at = (k.ps[4], k.ps[5][:, 0:WT * GR])
        small = (k.ps[6], k.ps[7])

        def window_tile(src, i):
            if i < 3:
                return src[bass.ds(b, 1), 512 * i:512 * (i + 1), :].rearrange("o (g r) c -> (o g) r c", r=16)[:, 0:4, :]
            return src[bass.ds(b, 1), 1536 + P * (i - 3):1536 + P * (i - 2), :].rearrange("o r c -> (o r) c")

        def page_of(eng, p):
            return eng.value_load(k.pages[0:1, bass.ds(b * NPG + p, 1)], min_val=0, max_val=NPHYS - 1)

        @block.sync
        def _(sp):
            for p in range(ITEMS):
                if p >= RING:
                    sp.wait_ge(s["k_turned"], p - RING + 1)
                if p < NPG:
                    page = page_of(sp, p)
                    sp.dma_start(kring[:, p % RING, :], kf[bass.ds(page, 1)].rearrange("o t c -> (o t) c")).then_inc(k_loaded[p % RING], 16)
                    sp.dma_start(lfp[p:p + 1, :], lf[bass.ds(page, 1), :]).then_inc(s["lf_loaded"], 16)
                else:
                    sp.dma_start(kring[:, p % RING, :], window_tile(kw, p - NPG)).then_inc(k_loaded[p % RING], 16)

        @block.tensor
        def _(pe):
            def turn_keys(p):
                pe.wait_ge(k_loaded[p % RING], 16 * (p // RING + 1))
                if p >= 2:
                    name, count = kept_by(p - 2)
                    pe.wait_ge(s[name], count)
                for hh in range(H):
                    last = pe.transpose(k.ps[p % 2][:, hh * P:(hh + 1) * P], kring[:, p % RING, hh * P:(hh + 1) * P], k.c("ident"))
                last.then_inc(s["k_turned"], 1)

            def score(g):
                for p in range(G * g, G * g + in_group(g)):
                    name, count = kept_by(p)
                    pe.wait_ge(s[name], count)
                if g == 0:
                    pe.wait_ge(s["q_ready"], 1)
                if g >= 2:
                    pe.wait_ge(s["rows_kept"], g - 1)
                n = in_group(g) * P
                for hh in range(H):
                    last = pe.matmul(k.ps[2 + g % 2][0:GR, 0:n], k.qpad[:, int(g >= FOX_GROUPS), hh, :], kt[:, g % 2, hh, 0:n],
                                     start=(hh == 0), stop=(hh == H - 1))
                last.then_inc(s["rows_made"], 1)

            def turn_scores(g):
                pe.wait_ge(s["rows_kept"], g + 1)
                f = int(g >= FOX_GROUPS)
                for i in range(in_group(g)):
                    at = GR * (G * g + i - NPG * f)
                    last = pe.transpose(scores_at[f][:, at:at + GR], srow[:, g % 2, i * P:(i + 1) * P], k.c("ident")[0:GR, 0:GR])
                last.then_inc(s["scores_turned"], 1)

            def turn_maxima(f):
                pe.wait_ge(s["max_cols"], f + 1)
                pe.transpose(small[f][0:GR, 0:P], mx[:, f, :], k.c("ident")).then_inc(s["max_turned"], 1)

            def spread_maxima(f):
                pe.wait_ge(s["max_diag"], f + 1)
                pe.matmul(small[f][:, P:P + GR], k.c("ones")[0:GR, :], mdiag[:, f, :], start=True, stop=True).then_inc(s["max_made"], 1)

            def output(f):
                pe.wait_ge(s["sums_ready"], f + 1)
                pe.matmul(k.ps[2 + f][:, 0:GR], k.c("ones"), sm[:, f, :], start=True, stop=True).then_inc(s["sums_made"], 1)
                pe.wait_ge(s["ov_ready"], f + 1)
                for hh in range(H):
                    last = pe.matmul(k.ps[4 + f][:, 0:GR], ov[:, f, hh * P:(hh + 1) * P], k.c("ident")[0:GR, 0:GR],
                                     start=(hh == 0), stop=(hh == H - 1))
                last.then_inc(s["ot_made"], 1)

            for p in range(ITEMS):
                turn_keys(p)
                if p % G == 1 and p > G:
                    score(p // G - 1)
                if p % G == 3 and p > G:
                    turn_scores(p // G - 1)
                if p == NPG + 2:
                    pe.wait_ge(s["lf_loaded"], 16 * NPG)
                    for hh in range(H):
                        last = pe.transpose(k.ps[6][:, hh * NPG:(hh + 1) * NPG], lfp.rearrange("p (t h) -> p h t", h=H)[:, hh, :], k.c("ident")[0:NPG, 0:NPG])
                    last.then_inc(s["lf_turned"], 1)
                if p == NPG + 4:
                    pe.wait_ge(s["later_ready"], 1)
                    pe.matmul(k.ps[7][:, 0:P], k.c("later"), lft, start=True, stop=False)
                    pe.matmul(k.ps[7][:, 0:P], k.c("ones"), later, start=False, stop=True).then_inc(s["fbias_made"], 1)
            score(GROUPS - 1)
            turn_scores(GROUPS - 2)
            turn_maxima(0)
            turn_scores(GROUPS - 1)
            spread_maxima(0)
            pe.wait_ge(s["exp_done"], 1)
            for p in range(NPG):
                if p % VG == 0:
                    pe.wait_ge(v_loaded[p // VG], 16 * VG)
                pe.matmul(k.ps[0][0:GR, :], pr[:, p, :], vslot[p], start=(p == 0), stop=False)
                if p == 6:
                    turn_maxima(1)
                if p == 12:
                    spread_maxima(1)
            pe.matmul(k.ps[0][0:GR, :], pr[0:TS, NPG, :], k.foxv.rearrange("t h d -> t (h d)"), start=False, stop=True).then_inc(s["pv_made"], 1)
            pe.wait_ge(s["exp_done"], 2)
            pe.wait_ge(s["vw_loaded"], 16 * WT)
            for i in range(WT):
                pe.matmul(k.ps[1][0:GR, :], pr[:, NPG + 1 + i, :], vwin[:, i, :], start=(i == 0), stop=False)
            pe.matmul(k.ps[1][0:GR, :], pr[0:TS, NPG + 1 + WT, :], k.winv.rearrange("t h d -> t (h d)"), start=False, stop=True).then_inc(s["pv_made"], 1)
            output(0)
            output(1)

        def take_keys(eng, copy, p, kept):
            g = p // G
            eng.wait_ge(s["k_turned"], p + 1)
            if g >= 2 and p % G < 2:
                eng.wait_ge(s["rows_made"], g - 1)
            copy(kt[:, g % 2, :, (p % G) * P:(p % G + 1) * P], k.ps[p % 2].rearrange("p (h t) -> p h t", h=H)).then_inc(s[kept], 1)

        @block.vector
        def _(dve):
            d = Order(dve, s["order"])
            for f, keep in enumerate((k.foxs, k.wins)):
                for hh in range(H):
                    last = dve.tensor_copy(k.qpad[:, f, hh, L * hh:L * hh + L], keep[:, 0, hh, bass.ds(b * L, L)])
            last.then_inc(s["q_ready"], 1)
            for f, blk in ((0, NPG), (1, NPG + 1 + WT)):
                dve.tensor_copy(sc[0:TS, blk, :].rearrange("p (h q) -> p h q", h=H), k.snew[:, f, :, bass.ds(b * L, L)])
            for p in range(ITEMS):
                if not by_act(p):
                    take_keys(dve, dve.tensor_copy, p, "kt_kept_v")
            dve.wait_ge(s["lf_turned"], 1)
            d.after(dve.tensor_copy(lft, k.ps[6][:, 0:P]))
            d.after(dve.tensor_tensor_scan(pre, k.c("page_reset"), lft, 0.0, ALU.mult, ALU.add))
            p3 = pre.rearrange("p (h n) -> p h n", h=H)
            dve.tensor_tensor(later.rearrange("p (h n) -> p h n", h=H), repeat(p3[:, :, NPG - 1], 2, NPG), p3, ALU.subtract).then_inc(s["later_ready"], 1)
            dve.wait_ge(s["fbias_made"], 1)
            d.after(dve.tensor_copy(fbias, k.ps[7][:, 0:P]))

            def maxima(f):
                dve.tensor_reduce(mx[:, f, :], sc[:, parts[f], :].rearrange("p n g -> p g n"), X, ALU.max).then_inc(s["max_cols"], 1)

            def shift(f):
                dve.wait_ge(s["max_turned"], f + 1)
                d.after(dve.tensor_reduce(mrow[:, f:f + 1], small[f][0:GR, 0:P], X, ALU.max))
                dve.tensor_scalar(mdiag[:, f, :], k.c("ident")[0:GR, 0:GR], mrow[:, f:f + 1], None, ALU.mult).then_inc(s["max_diag"], 1)
                dve.wait_ge(s["max_made"], f + 1)
                n = parts[f].stop - parts[f].start
                dve.tensor_tensor(pr[:, parts[f], :], sc[:, parts[f], :], repeat(small[f][:, P:P + GR], 1, n), ALU.subtract).then_inc(s["shifted"], 1)

            def sums(f):
                dve.wait_ge(s["exp_done"], f + 1)
                dve.tensor_reduce(sm[:, f, :], pr[:, parts[f], :].rearrange("p n g -> p g n"), X, ALU.add).then_inc(s["sums_ready"], 1)

            dve.wait_ge(s["scores_turned"], FOX_GROUPS)
            d.after(dve.tensor_tensor(sc[:, 0:NPG, :].rearrange("p n (h q) -> p n h q", h=H), scores_at[0].rearrange("p (n h q) -> p n h q", n=NPG, h=H),
                                      repeat(fbias.rearrange("p (h n) -> p n h", h=H), 3, L), ALU.add))
            maxima(0)
            shift(0)
            dve.wait_ge(s["scores_turned"], GROUPS)
            d.after(dve.tensor_tensor(sc[:, NPG + 1:NPG + 1 + WT, :], scores_at[1].rearrange("p (n g) -> p n g", n=WT),
                                      k.c("window_past").rearrange("p (n g) -> p n g", n=WT), ALU.add))
            maxima(1)
            shift(1)
            sums(0)
            sums(1)
            for f in range(2):
                dve.wait_ge(s["pv_made"], f + 1)
                dve.tensor_tensor(ov[:, f, :], k.ps[f][0:GR, :], k.c("head_cols")[0:GR, :], ALU.mult).then_inc(s["ov_ready"], 1)
            for f, keep in enumerate((k.foxs, k.wins)):
                dve.wait_ge(s["sums_made"], f + 1)
                d.after(dve.reciprocal(rs[:, f, :], k.ps[2 + f][:, 0:GR]))
                dve.wait_ge(s["ot_made"], f + 1)
                d.after(dve.tensor_tensor(res[:, f, :], k.ps[4 + f][:, 0:GR], rs[:, f, :], ALU.mult))
                dve.tensor_tensor(k.osample[:, f * H:(f + 1) * H, bass.ds(b * L, L)], res[:, f, :].rearrange("p (h q) -> p h q", h=H),
                                  keep[:, 2, :, bass.ds(b * L, L)], ALU.mult)

        @block.scalar
        def _(act):
            def take_scores(g):
                act.wait_ge(s["rows_made"], g + 1)
                if g >= 2:
                    act.wait_ge(s["scores_turned"], g - 1)
                n = in_group(g) * P
                act.copy(srow[:, g % 2, 0:n], k.ps[2 + g % 2][0:GR, 0:n]).then_inc(s["rows_kept"], 1)

            def values(p):
                if p < NPG:
                    act.dma_start(vslot[p], vf[bass.ds(page_of(act, p), 1)].rearrange("o t c -> (o t) c")).then_inc(v_loaded[p // VG], 16)
                else:
                    act.dma_start(vwin[:, p - NPG, :], window_tile(vw, p - NPG)).then_inc(s["vw_loaded"], 16)

            for p in range(ITEMS):
                if by_act(p):
                    take_keys(act, act.copy, p, "kt_kept_s")
                if p >= RING:
                    values(p - RING)
                if p % G == 1 and p > G:
                    take_scores(p // G - 1)
            for p in range(ITEMS - RING, ITEMS):
                values(p)
            take_scores(GROUPS - 1)
            for f in range(2):
                act.wait_ge(s["shifted"], f + 1)
                act.activation(pr[:, parts[f], :], pr[:, parts[f], :], ACT.Exp).then_inc(s["exp_done"], 1)
    clear(nc, k_loaded + v_loaded + list(s.values()))


def store_sample_heads(nc, k, io):
    with nc.semaphore("sample_stored") as stored:
        with nc.Block() as block:
            @block.sync
            def _(sp):
                sp.dma_start(io.scr_o[:, :, T:NT].rearrange("k p n -> p k n"), k.osample).then_inc(stored, 16)
                sp.wait_ge(stored, 16)
        clear(nc, [stored])


def write_tokens(nc, k, io):
    with ExitStack() as c:
        sem = lambda n: c.enter_context(nc.semaphore(n))
        turned, left, right, stored = sem("y_turned"), sem("y_left"), sem("y_right"), [sem("y_stored0"), sem("y_stored1")]
        row = c.enter_context(nc.sbuf_tensor("yrow", [P, 2, D_MODEL], F32))
        block = c.enter_context(nc.Block())

        @block.tensor
        def _(pe):
            for t in range(TILES + 1):
                n = P if t < TILES else TS
                for half, taken in ((0, left), (1, right)):
                    if t >= 2:
                        pe.wait_ge(taken, t - 1)
                    for j in range(4):
                        last = pe.transpose(k.ps[half + 2 * (t % 2)][0:n, j * P:(j + 1) * P], k.xT[:, 4 * half + j, t * P:t * P + n], k.c("ident"))
                    last.then_inc(turned, 1)

        @block.vector
        def _(dve):
            for t in range(TILES + 1):
                n = P if t < TILES else TS
                dve.wait_ge(turned, 2 * t + 1)
                if t >= 2:
                    dve.wait_ge(stored[t % 2], 16 * (t // 2))
                dve.tensor_copy(row[0:n, t % 2, 0:512], k.ps[2 * (t % 2)][0:n, :]).then_inc(left, 1)

        @block.scalar
        def _(act):
            for t in range(TILES + 1):
                n = P if t < TILES else TS
                act.wait_ge(turned, 2 * t + 2)
                if t >= 2:
                    act.wait_ge(stored[t % 2], 16 * (t // 2))
                act.copy(row[0:n, t % 2, 512:1024], k.ps[1 + 2 * (t % 2)][0:n, :]).then_inc(right, 1)

        @block.sync
        def _(sp):
            for t in range(TILES + 1):
                n = P if t < TILES else TS
                sp.wait_ge(left, t + 1)
                sp.wait_ge(right, t + 1)
                dst = io.out_y_prompt[0, t * P:t * P + n, :] if t < TILES else io.out_y_sample.rearrange("b l d -> (b l) d")
                sp.dma_start(dst, row[0:n, t % 2, :]).then_inc(stored[t % 2], 16)
            sp.wait_ge(stored[0], 16 * 9)
            sp.wait_ge(stored[1], 16 * 8)


def build(nc, io, const_names, stop=99):
    with ExitStack() as c:
        sb = lambda n, s, dt=F32: c.enter_context(nc.sbuf_tensor(n, s, dt))[:]
        k = Chip()
        width = io.c_pack.shape[1]
        k.xT, k.rstd = sb("xT", [P, KT, NT]), sb("rstd", [P, NT])
        k.pack = sb("pack", [P, width])
        k.c = lambda n: k.pack[:, const_names[n][0]:const_names[n][0] + const_names[n][1]]
        k.big = sb("big", [P, 4 * NT + KT * 4 * P + NT])
        k.qkvz = k.big[:, 0:4 * NT].rearrange("p (m n) -> p m n", m=4)
        k.w = k.big[:, 4 * NT:4 * NT + KT * 4 * P].rearrange("p (k n) -> p k n", k=KT)
        k.qd = k.big[:, 4 * NT + KT * 4 * P:]
        k.conv_cols, k.cw_head = sb("conv_cols", [P, 12, 28]), sb("cw_head", [P, 3, 4])
        k.gate_cols, k.logf_cols = sb("gate_cols", [P, 2, H, TILES + 1]), sb("logf_cols", [P, TILES + 1, H])
        k.g_even, k.g_odd, k.b_norm = sb("g_even", [P, KT]), sb("g_odd", [P, KT]), sb("b_norm", [P, H])
        k.vec, k.small, k.pages = sb("vec", [P, 5]), sb("small", [36, 4]), sb("pages", [1, B * NPG], I32)
        k.eps, k.one, k.zero = sb("eps", [P, 1]), sb("one", [P, 1]), sb("zero", [P, 324])
        k.ps4 = c.enter_context(nc.psum_tensor("ps0123", [P, 4 * 512], F32))[:]
        k.ps = [k.ps4[:, i * 512:(i + 1) * 512] for i in range(4)]
        k.ps += [c.enter_context(nc.psum_tensor(f"ps{i}", [P, 512], F32))[:] for i in range(4, 8)]
        with nc.semaphore("windows_shifted") as windows_shifted:
            k.windows_shifted = windows_shifted
            with nc.Block() as block:
                @block.vector
                def _(dve):
                    dve.memset(k.eps, EPS)
                    dve.memset(k.one, 1.0)
                    dve.memset(k.zero, 0.0)
                    dve.memset(k.small, 0.0)
            with nc.allow_non_contiguous_dma(reason="a few thousand single words, once"):
                load_tokens(nc, k, io)
            token_norms(nc, k, 0)
            row_gates_even(nc, k, io)
            if stop > 1:
                first_weights(nc, k, io, "A")
                with nc.Fori(0, H) as h:
                    head_A(nc, k, io, h)
            if stop > 2:
                first_weights(nc, k, io, "B")
                with nc.Fori(0, H) as h:
                    head_B(nc, k, io, h)
            if stop > 3:
                output_projection(nc, k, io, 0)
                token_norms(nc, k, 1)
                row_gates_odd(nc, k, io)
                k.foxs, k.wins = sb("foxs", [P, 3, H, TS]), sb("wins", [P, 3, H, TS])
                k.foxv, k.winv = sb("foxv", [TS, H, P]), sb("winv", [TS, H, P])
                k.snew, k.osample = sb("snew", [TS, 2, H, TS]), sb("osample", [P, 2 * H, TS])
            if stop > 4:
                first_weights(nc, k, io, "C")
                with nc.Fori(0, H) as h:
                    head_attention(nc, k, io, h, "C")
            if stop > 5:
                first_weights(nc, k, io, "D")
                with nc.Fori(0, H) as h:
                    head_attention(nc, k, io, h, "D")
            if stop > 6:
                k.qpad = sb("qpad", [P, 2, H, 4 * H])
                k.sc_all = sb("sc_all", [P, NPG + 1 + WT + 1, 4 * H])
                sample_new_scores(nc, k, io)
                with nc.Fori(0, B) as b:
                    sample_attention(nc, k, io, b)
                store_sample_heads(nc, k, io)
                output_projection(nc, k, io, 1)
            if stop > 3:
                write_tokens(nc, k, io)
            with nc.Block() as block:
                @block.sync
                def _(sp):
                    sp.wait_ge(windows_shifted, 16 * 2 * B)


_INS = ["x_prompt", "x_sample", "cache_fox_k", "cache_fox_v", "cache_fox_logf", "page_table", "cache_win_k", "cache_win_v",
        "state_delta", "state_delta_conv", "state_ret", "norm_even", "w_in_even", "conv_w", "a_log", "dt_bias", "a_norm",
        "b_norm", "w_out_even", "norm_odd", "w_in_odd", "c_q_norm", "c_k_norm", "f_bias", "d_q_norm", "d_k_norm", "w_out_odd"]
_OUTS = [("y_prompt", (1, T, D_MODEL)), ("y_sample", (B, L, D_MODEL)),
         ("fox_k_prompt", (1, 1, T, H, P)), ("fox_v_prompt", (1, 1, T, H, P)), ("fox_logf_prompt", (1, 1, T, H)),
         ("fox_k_sample", (B, 1, L, H, P)), ("fox_v_sample", (B, 1, L, H, P)), ("fox_logf_sample", (B, 1, L, H)),
         ("win_k_prompt", (1, 1, T, H, P)), ("win_v_prompt", (1, 1, T, H, P)),
         ("win_k_sample", (1, B, WBUF, H, P)), ("win_v_sample", (1, B, WBUF, H, P)),
         ("delta_prompt", (1, 1, H, P, P)), ("delta_conv_prompt", (1, 1, 3, 3 * HD)),
         ("delta_sample", (1, B, H, P, P)), ("delta_conv_sample", (1, B, 3, 3 * HD)),
         ("ret_prompt", (1, 1, H, P, P)), ("ret_sample", (1, B, H, P, P))]


class Dram:

    def __init__(self, t):
        self.a_log = t["a_log"]
        self.a_norm = t["a_norm"]
        self.b_norm = t["b_norm"]
        self.c_k_norm = t["c_k_norm"]
        self.c_pack = t["c_pack"]
        self.c_q_norm = t["c_q_norm"]
        self.c_reset = t["c_reset"]
        self.c_ret = t["c_ret"]
        self.c_window = t["c_window"]
        self.cache_fox_k = t["cache_fox_k"]
        self.cache_fox_logf = t["cache_fox_logf"]
        self.cache_fox_v = t["cache_fox_v"]
        self.cache_win_k = t["cache_win_k"]
        self.cache_win_v = t["cache_win_v"]
        self.conv_w = t["conv_w"]
        self.d_k_norm = t["d_k_norm"]
        self.d_q_norm = t["d_q_norm"]
        self.dt_bias = t["dt_bias"]
        self.f_bias = t["f_bias"]
        self.norm_even = t["norm_even"]
        self.norm_odd = t["norm_odd"]
        self.out_delta_conv_prompt = t["out_delta_conv_prompt"]
        self.out_delta_conv_sample = t["out_delta_conv_sample"]
        self.out_delta_prompt = t["out_delta_prompt"]
        self.out_delta_sample = t["out_delta_sample"]
        self.out_fox_k_prompt = t["out_fox_k_prompt"]
        self.out_fox_k_sample = t["out_fox_k_sample"]
        self.out_fox_logf_prompt = t["out_fox_logf_prompt"]
        self.out_fox_logf_sample = t["out_fox_logf_sample"]
        self.out_fox_v_prompt = t["out_fox_v_prompt"]
        self.out_fox_v_sample = t["out_fox_v_sample"]
        self.out_ret_prompt = t["out_ret_prompt"]
        self.out_ret_sample = t["out_ret_sample"]
        self.out_win_k_prompt = t["out_win_k_prompt"]
        self.out_win_k_sample = t["out_win_k_sample"]
        self.out_win_v_prompt = t["out_win_v_prompt"]
        self.out_win_v_sample = t["out_win_v_sample"]
        self.out_y_prompt = t["out_y_prompt"]
        self.out_y_sample = t["out_y_sample"]
        self.page_table = t["page_table"]
        self.scr_f = t["scr_f"]
        self.scr_g = t["scr_g"]
        self.scr_o = t["scr_o"]
        self.state_delta = t["state_delta"]
        self.state_delta_conv = t["state_delta_conv"]
        self.state_ret = t["state_ret"]
        self.w_in_even = t["w_in_even"]
        self.w_in_odd = t["w_in_odd"]
        self.w_out_even = t["w_out_even"]
        self.w_out_odd = t["w_out_odd"]
        self.x_prompt = t["x_prompt"]
        self.x_sample = t["x_sample"]


def declare(nc, inputs):
    tensors, arrays = {}, {}
    consts, names = shape_constants()
    given = {n: np.ascontiguousarray(inputs[n]) for n in _INS}
    given.update(consts)
    for n, a in given.items():
        arrays[f"in_{n}"] = a
        tensors[n] = nc.dram_tensor(f"in_{n}", a.shape, mybir.dt.from_np(a.dtype), kind="ExternalInput").ap()
    for n, shape in _OUTS:
        tensors[f"out_{n}"] = nc.dram_tensor(f"out_{n}", shape, F32, kind="ExternalOutput").ap()
    tensors["scr_g"] = nc.dram_tensor("scr_g", (H, NT), F32).ap()
    tensors["scr_f"] = nc.dram_tensor("scr_f", (H, T), F32).ap()
    tensors["scr_o"] = nc.dram_tensor("scr_o", (2 * H, P, NT), F32).ap()
    return Dram(tensors), arrays, names


def kernel(**inputs):
    import concourse.bacc as _bacc
    from concourse.bass_utils import run_bass_kernel_spmd as _run

    nc = _bacc.Bacc("TRN2", target_bir_lowering=False, num_devices=1)
    io, arrays, names = declare(nc, inputs)
    build(nc, io, names)
    r = _run(nc, [arrays], core_ids=[0])
    return tuple(r.results[0][f"out_{n}"] for n, _ in _OUTS)
```

```python
from contextlib import ExitStack

import numpy as np
import concourse.bass as bass
from concourse import mybir
from concourse.alu_op_type import AluOpType as ALU

F32 = mybir.dt.float32
I32 = mybir.dt.int32
ACT = mybir.ActivationFunctionType
X = mybir.AxisListType.X

P = 128
D_MODEL = 1024
KT = D_MODEL // P
T = 2048
TILES = T // P
B = 8
L = 4
TS = B * L
NT = T + TS
CH = 416
NC = NT // CH
H = 4
HD = H * P
G = 4
PAGE = 128
NPG = 32
NPHYS = 320
WBUF = 2048
WT = 7
EPS = 1e-6
BIG = 1e30
SCALE = P ** -0.5
EVEN_OFF = {"A": (0, 512, 1024, 1536), "B": (2056, 2568, 3080, 3592)}
ODD_OFF = {"C": (0, 512, 1024, 1536), "D": (2052, 2564, 3076, 3588)}
NEXT = {"A": EVEN_OFF["B"][0] - EVEN_OFF["A"][0], "C": ODD_OFF["D"][0] - ODD_OFF["C"][0]}


def shape_constants():
    i = np.arange(P)
    f = np.float32
    lower = i[:, None] > i[None, :]
    c = {
        "ident": np.eye(P), "ones": np.ones((P, P)),
        "not_lower": np.where(lower, 0, BIG), "not_causal": np.where(lower, BIG, 0),
        "diag16": i[:, None] // 16 == i[None, :] // 16,
    }
    for s in (16, 32, 64):
        c[f"under{2 * s}"] = (i[:, None] // (2 * s) == i[None, :] // (2 * s)) & (i[:, None] // s > i[None, :] // s)
    c["causal_bias"] = np.where(i[None, :] > i[:, None], -BIG, 0)
    c["later"] = lower
    s = np.arange(TS)
    same = s[:, None] // L == s[None, :] // L
    pad = lambda a: np.pad(a, ((0, P - a.shape[0]), (0, 0)))
    c["s_not_lower"] = pad(np.where(same & (s[:, None] > s[None, :]), 0, BIG))
    c["s_not_causal"] = pad(np.where(same & (s[:, None] <= s[None, :]), 0, BIG))
    c["s_last"] = pad(same & (s[None, :] % L == L - 1))
    c["s_prefix"] = pad(same & (s[:, None] <= s[None, :]))
    c["s_bias"] = pad(np.where(same & (s[:, None] <= s[None, :]), 0, -BIG))
    c["s_cols"] = np.broadcast_to((s[None, :] // L == np.arange(B)[:, None]).reshape(1, -1), (P, B * TS))
    c["s_rows"] = pad(s[:, None] // L == np.arange(B)[None, :])
    r = np.arange(4 * H)
    c["head_cols"] = pad((r[:, None] // L == np.arange(HD)[None, :] // P))
    c["page_reset"] = np.broadcast_to((np.arange(H * NPG) % NPG != 0)[None, :], (P, H * NPG))
    slope = 2.0 ** (-8.0 * np.arange(1, H + 1) / H)

    def reach(d):
        n = ((d >= 0) & (d <= 128)).astype(int) + ((d >= 0) & (d <= 512) & (d % 4 == 0)) \
            + ((d >= 0) & (d <= 2048) & (d % 16 == 0))
        return n

    def bias(d, h):
        n = reach(d)
        return np.where(n > 0, np.log(np.maximum(n, 1)) - slope[h] * d, -BIG)

    new = np.stack([np.where(same, bias(s[None, :] - s[:, None], h), -BIG) for h in range(H)], 1)
    c["s_window"] = np.pad(new.reshape(TS, H * TS), ((0, P - TS), (0, 0)))
    rows = window_rows().reshape(WT, P)
    past = np.zeros((P, WT, H, L))
    for h in range(H):
        for q in range(L):
            past[:, :, h, q] = bias(WBUF + q - rows, h).T
    c["window_past"] = past.reshape(P, -1)
    names, cols, at = {}, [], 0
    for k, v in c.items():
        v = np.asarray(v, f)
        names[k] = (at, v.shape[1])
        at += v.shape[1]
        cols.append(v)
    pack = np.concatenate(cols, 1)
    m = np.arange(T)
    window = np.stack([bias(i[:, None] + (T - P) - m[None, :], h) for h in range(H)]).astype(f)
    lg = np.log1p(-np.exp2(-5.0 - np.arange(H, dtype=np.float64)))
    ret = np.zeros((H, P, RET), f)
    for h in range(H):
        d = i[None, :] - i[:, None]
        ret[h, :, 0:P] = np.where(d >= 0, np.exp(np.maximum(d, 0) * lg[h]) * SCALE, 0)
        ret[h, :, P:2 * P] = np.exp((i + 1.0) * lg[h])[None, :]
        ret[h, :, 256] = np.exp((P - 1.0 - i) * lg[h]) * SCALE
        ret[h, :, 257] = np.exp(P * lg[h])
        ds = s[None, :] - s[:, None]
        ret[h, :TS, 258:290] = np.where(same & (ds >= 0), np.exp(np.maximum(ds, 0) * lg[h]) * SCALE, 0)
        ret[h, :, 290:322] = np.exp((s % L + 1.0) * lg[h])[None, :]
        ret[h, :TS, 322] = np.exp((L - 1.0 - s % L) * lg[h]) * SCALE
        ret[h, :, 323] = np.exp(L * lg[h])
    reset = np.ones((1, NT), f)
    reset[0, 0:T:P] = 0
    reset[0, T::L] = 0
    return {"c_pack": pack, "c_window": window, "c_ret": ret, "c_reset": reset}, names


RET = 324


def window_rows():
    g = np.arange(96)[:, None] * 16 + np.arange(4)[None, :]
    return np.concatenate([g.reshape(-1), np.arange(1536, 2048)])


def repeat(ap, axis, n):
    ap = ap.unsqueeze(axis)
    shape = list(ap.shape)
    shape[axis] = n
    return ap.broadcast_to(shape)


def clear(nc, sems):
    with nc.Block() as block:
        @block.gpsimd
        def _(pool):
            for s in sems[0::5]:
                pool.sem_clear(s)

        @block.vector
        def _(dve):
            for s in sems[1::5]:
                dve.sem_clear(s)

        @block.scalar
        def _(act):
            for s in sems[2::5]:
                act.sem_clear(s)

        @block.sync
        def _(sp):
            for s in sems[3::5]:
                sp.sem_clear(s)

        @block.tensor
        def _(pe):
            for s in sems[4::5]:
                pe.sem_clear(s)


class Chip:
    pass


def load_tokens(nc, k, io):
    with ExitStack() as c:
        sem = lambda n: c.enter_context(nc.semaphore(n))
        const_loaded, vec_loaded = sem("const_loaded"), sem("vec_loaded")
        SLOTS = 4
        x_loaded = [sem(f"x_loaded{i}") for i in range(SLOTS)]
        rows_loaded, rows_turned, rows_copied = sem("rows_loaded"), sem("rows_turned"), sem("rows_copied")
        x_turned, left_copied, right_copied = sem("x_turned"), sem("left_copied"), sem("right_copied")
        xrow = c.enter_context(nc.sbuf_tensor("xrow", [P, SLOTS, D_MODEL], F32))
        conv_rows = c.enter_context(nc.sbuf_tensor("conv_rows", [28, 3 * HD], F32))
        block = c.enter_context(nc.Block())
        vectors = [(k.g_even, io.norm_even[0].rearrange("(k p) -> p k", p=P)),
                   (k.g_odd, io.norm_odd[0].rearrange("(k p) -> p k", p=P)),
                   (k.b_norm, io.b_norm[0].rearrange("(k p) -> p k", p=P)),
                   (k.vec[:, 0:1], io.a_norm[0].unsqueeze(1)), (k.vec[:, 1:2], io.c_q_norm[0].unsqueeze(1)),
                   (k.vec[:, 2:3], io.c_k_norm[0].unsqueeze(1)), (k.vec[:, 3:4], io.d_q_norm[0].unsqueeze(1)),
                   (k.vec[:, 4:5], io.d_k_norm[0].unsqueeze(1)),
                   (k.small[32:36, 0:1], io.a_log[0].unsqueeze(1)), (k.small[32:36, 1:2], io.dt_bias[0].unsqueeze(1)),
                   (k.small[0:4, 2:3], io.f_bias[0].unsqueeze(1)),
                   (k.pages, io.page_table.rearrange("b n -> (b n)").unsqueeze(0))]

        @block.sync
        def _(sp):
            sp.dma_start(k.pack, io.c_pack).then_inc(const_loaded, 16)
            sp.dma_start(conv_rows[0:24, :], io.state_delta_conv[0].rearrange("b r c -> (b r) c")).then_inc(rows_loaded, 16)
            sp.dma_start(conv_rows[24:28, :], io.conv_w[0]).then_inc(rows_loaded, 16)
            for t in range(TILES + 1):
                if t >= SLOTS:
                    sp.wait_ge(x_turned, 2 * (t - SLOTS + 1))
                src = io.x_prompt[0, t * P:(t + 1) * P, :] if t < TILES else io.x_sample.rearrange("b l d -> (b l) d")
                n = P if t < TILES else TS
                sp.dma_start(xrow[0:n, t % SLOTS, :], src).then_inc(x_loaded[t % SLOTS], 16)
            for dst, src in vectors:
                sp.dma_start(dst, src).then_inc(vec_loaded, 16)
            sp.wait_ge(vec_loaded, 16 * len(vectors))

        @block.tensor
        def _(pe):
            pe.wait_ge(const_loaded, 16)
            pe.wait_ge(rows_loaded, 32)
            for j in range(12):
                last = pe.transpose(k.ps[2][:, j * 28:(j + 1) * 28], conv_rows[:, j * P:(j + 1) * P], k.c("ident")[0:28, 0:28])
            last.then_inc(rows_turned, 1)
            for t in range(TILES + 1):
                n = P if t < TILES else TS
                pe.wait_ge(x_loaded[t % SLOTS], 16 * (t // SLOTS + 1))
                for half, copied in ((0, left_copied), (1, right_copied)):
                    if t >= 1:
                        pe.wait_ge(copied, t)
                    for j in range(4):
                        kk = 4 * half + j
                        last = pe.transpose(k.ps[half][:, j * P:j * P + n], xrow[0:n, t % SLOTS, kk * P:(kk + 1) * P],
                                            k.c("ident")[0:n, 0:n])
                    last.then_inc(x_turned, 1)

        @block.vector
        def _(dve):
            dve.wait_ge(rows_turned, 1)
            dve.tensor_copy(k.conv_cols.rearrange("p a b -> p (a b)"), k.ps[2][:, 0:336]).then_inc(rows_copied, 1)
            for t in range(TILES + 1):
                n = P if t < TILES else TS
                dve.wait_ge(x_turned, 2 * t + 1)
                dve.tensor_copy(k.xT[:, 0:4, t * P:t * P + n],
                                k.ps[0].rearrange("p (j n) -> p j n", j=4)[:, :, 0:n]).then_inc(left_copied, 1)

        @block.scalar
        def _(act):
            for t in range(TILES + 1):
                n = P if t < TILES else TS
                act.wait_ge(x_turned, 2 * t + 2)
                act.copy(k.xT[:, 4:8, t * P:t * P + n],
                         k.ps[1].rearrange("p (j n) -> p j n", j=4)[:, :, 0:n]).then_inc(right_copied, 1)
    clear(nc, [const_loaded, vec_loaded, *x_loaded, rows_loaded, rows_turned, rows_copied, x_turned, left_copied, right_copied])


def token_norms(nc, k, io):
    with ExitStack() as c:
        sem = lambda n: c.enter_context(nc.semaphore(n))
        squared, added, summed, logged, rooted = sem("squared"), sem("added"), sem("summed"), sem("logged_x"), sem("rooted")
        w_loaded, w_scaled = sem("w_loaded_first"), sem("w_scaled_first")
        load_weights, scale_weights = head_weights(k, io, "A", 0, w_loaded, w_scaled)
        sq = c.enter_context(nc.sbuf_tensor("sq", [P, 2, NT], F32))
        total = c.enter_context(nc.sbuf_tensor("sq_total", [P, NT], F32))
        block = c.enter_context(nc.Block())

        @block.sync
        def _(sp):
            load_weights(sp)

        @block.gpsimd
        def _(pool):
            scale_weights(pool)

        @block.scalar
        def _(act):
            for j in range(KT):
                if j >= 2:
                    act.wait_ge(added, j - 1)
                act.activation(sq[:, j % 2, :], k.xT[:, j, :], ACT.Square).then_inc(squared, 1)
            act.wait_ge(summed, 1)
            for n in range(NC):
                act.activation(total[:, n * CH:(n + 1) * CH], k.ps[n][:, 0:CH], ACT.Ln, bias=k.eps,
                               scale=1.0 / D_MODEL).then_inc(logged, 1)
            act.wait_ge(logged, NC)
            act.activation(k.rstd[:, :], total[:, :], ACT.Exp, scale=-0.5).then_inc(rooted, 1)

        @block.vector
        def _(dve):
            for j in range(KT):
                dve.wait_ge(squared, j + 1)
                if j == 0:
                    dve.tensor_copy(total[:, :], sq[:, 0, :]).then_inc(added, 1)
                else:
                    dve.wait_ge(added, j)
                    dve.tensor_tensor(total[:, :], total[:, :], sq[:, j % 2, :], ALU.add).then_inc(added, 1)

        @block.tensor
        def _(pe):
            pe.wait_ge(added, KT)
            for n in range(NC):
                last = pe.matmul(k.ps[n][:, 0:CH], k.c("ones"), total[:, n * CH:(n + 1) * CH], start=True, stop=True)
            last.then_inc(summed, 1)
    clear(nc, [squared, added, summed, logged, rooted, w_loaded, w_scaled])


def row_gates_even(nc, k, io):
    with ExitStack() as c:
        sem = lambda n: c.enter_context(nc.semaphore(n))
        w_loaded, w_zero, w_scaled = sem("gw_loaded"), sem("gw_zero"), sem("gw_scaled")
        row_ready, row_taken = sem("row_ready"), sem("row_taken")
        a_step, d_step = sem("gate_act"), sem("gate_dve")
        turned, cols_ready, stored = sem("gates_turned"), sem("gate_cols"), sem("g_stored")
        w = c.enter_context(nc.sbuf_tensor("gw", [P, KT, 36], F32))
        rows = c.enter_context(nc.sbuf_tensor("rows", [36, NT], F32))
        tmp = c.enter_context(nc.sbuf_tensor("rtmp", [36, NT], F32))
        tmp2 = c.enter_context(nc.sbuf_tensor("rtmp2", [36, NT], F32))
        reset = c.enter_context(nc.sbuf_tensor("reset", [36, NT], F32))
        block = c.enter_context(nc.Block())
        HI = slice(32, 36)

        @block.sync
        def _(sp):
            sp.wait_ge(w_zero, 1)
            wv = io.w_in_even[0].rearrange("(k p) c -> p k c", p=P)
            sp.dma_start(w[:, :, 0:4], wv[:, :, 2048:2052]).then_inc(w_loaded, 16)
            sp.dma_start(w[:, :, 32:36], wv[:, :, 2052:2056]).then_inc(w_loaded, 16)
            sp.dma_start(reset[HI, :], io.c_reset.broadcast_to([4, NT])).then_inc(w_loaded, 16)
            sp.wait_ge(d_step, 6)
            sp.dma_start(io.scr_g, rows[HI, :]).then_inc(stored, 16)
            sp.wait_ge(stored, 16)

        @block.vector
        def _(dve):
            dve.memset(w[:, :, :], 0.0).then_inc(w_zero, 1)
            dve.wait_ge(w_loaded, 48)
            dve.tensor_tensor(w[:, :, :], w[:, :, :], repeat(k.g_even, 2, 36), ALU.mult).then_inc(w_scaled, 1)
            for n in range(NC):
                dve.wait_ge(row_ready, n + 1)
                dve.tensor_tensor(rows[:, n * CH:(n + 1) * CH], k.ps[n % 2][0:36, 0:CH], k.rstd[0:36, n * CH:(n + 1) * CH],
                                  ALU.mult).then_inc(row_taken, 1)
            dve.wait_ge(a_step, 1)
            dve.tensor_scalar(rows[0:4, :], tmp[0:4, :], 0.5, 0.5, ALU.mult, ALU.add).then_inc(d_step, 1)
            dve.tensor_scalar(tmp2[HI, :], rows[HI, :], k.small[HI, 1:2], 0.0, ALU.add, ALU.max).then_inc(d_step, 1)
            dve.wait_ge(a_step, 4)
            dve.wait_ge(d_step, 2)
            dve.tensor_tensor(tmp2[HI, :], tmp2[HI, :], tmp[HI, :], ALU.add).then_inc(d_step, 1)
            dve.wait_ge(a_step, 5)
            dve.tensor_scalar(k.small[HI, 3:4], k.small[HI, 3:4], -1.0, None, ALU.mult).then_inc(d_step, 1)
            dve.wait_ge(d_step, 4)
            dve.tensor_scalar(tmp2[HI, :], tmp2[HI, :], k.small[HI, 3:4], None, ALU.mult).then_inc(d_step, 1)
            dve.wait_ge(d_step, 5)
            dve.tensor_tensor_scan(rows[HI, :], reset[HI, :], tmp2[HI, :], 0.0, ALU.mult, ALU.add).then_inc(d_step, 1)
            for half in range(2):
                dve.wait_ge(turned, half + 1)
                n = 9 - half
                for what in range(2):
                    last = dve.tensor_copy(k.gate_cols[:, what, :, 9 * half:9 * half + n],
                                           k.ps[2 + half][:, 0:36 * n].rearrange("p (t r) -> p r t", r=36)[:, 32 * what:32 * what + H, :])
                last.then_inc(cols_ready, 1)

        @block.scalar
        def _(act):
            act.wait_ge(row_taken, NC)
            act.activation(tmp[0:4, :], rows[0:4, :], ACT.Tanh, scale=0.5).then_inc(a_step, 1)
            act.activation(tmp[HI, :], rows[HI, :], ACT.Abs, bias=k.small[HI, 1:2]).then_inc(a_step, 1)
            act.wait_ge(a_step, 2)
            act.activation(tmp[HI, :], tmp[HI, :], ACT.Exp, scale=-1.0).then_inc(a_step, 1)
            act.wait_ge(a_step, 3)
            act.activation(tmp[HI, :], tmp[HI, :], ACT.Ln, bias=k.one[HI, :]).then_inc(a_step, 1)
            act.activation(k.small[HI, 3:4], k.small[HI, 0:1], ACT.Exp).then_inc(a_step, 1)

        @block.tensor
        def _(pe):
            pe.wait_ge(w_scaled, 1)
            for n in range(NC):
                if n >= 2:
                    pe.wait_ge(row_taken, n - 1)
                for j in range(KT):
                    last = pe.matmul(k.ps[n % 2][0:36, 0:CH], w[:, j, :], k.xT[:, j, n * CH:(n + 1) * CH],
                                     start=(j == 0), stop=(j == KT - 1))
                last.then_inc(row_ready, 1)
            pe.wait_ge(d_step, 6)
            for half in range(2):
                pe.matmul(k.ps[2 + half][:, 0:324], k.c("ones"), k.zero[:, 0:324], start=True, stop=True)
                for t in range(9 * half, 17 if half else 9):
                    m = P if t < TILES else TS
                    a = 36 * (t - 9 * half)
                    last = pe.transpose(k.ps[2 + half][0:m, a:a + 36], rows[:, t * P:t * P + m], k.c("ident")[0:36, 0:36])
                last.then_inc(turned, 1)
    clear(nc, [w_loaded, w_zero, w_scaled, row_ready, row_taken, a_step, d_step, turned, cols_ready, stored])


def head_weights(k, io, branch, col, w_loaded, w_scaled):
    layer = 0 if branch in EVEN_OFF else 1
    wv = (io.w_in_even if layer == 0 else io.w_in_odd)[0].rearrange("(k p) c -> p k c", p=P)
    offs = (EVEN_OFF if layer == 0 else ODD_OFF)[branch]
    gain = k.g_even if layer == 0 else k.g_odd

    def sync(sp):
        for m in range(4):
            sp.dma_start(k.w[:, :, m * P:(m + 1) * P], wv[:, :, bass.ds(col + offs[m], P)]).then_inc(w_loaded, 16)

    def gpsimd(pool):
        pool.wait_ge(w_loaded, 64)
        pool.tensor_tensor(k.w[:, :, :], k.w[:, :, :], repeat(gain, 2, 4 * P), ALU.mult).then_inc(w_scaled, 1)
        pool.wait_ge(w_scaled, 1)

    return sync, gpsimd


def project_head(nc, k, io, c, branch, h, dst):
    sem = lambda n: c.enter_context(nc.semaphore(f"{n}_{branch}"))
    w_loaded, w_scaled, proj_ready, proj_taken = sem("w_loaded"), sem("w_scaled"), sem("proj_ready"), sem("proj_taken")
    if branch in NEXT:
        col = (h + 1) * P + (h + 1) // H * (NEXT[branch] - HD)
    else:
        col = (h + 1) % H * P
    next_sync, next_pool = head_weights(k, io, branch, col, w_loaded, w_scaled)

    def tensor(pe, at):
        m, n = divmod(at, NC)
        if at >= 2:
            pe.wait_ge(proj_taken, at - 1)
        for j in range(KT):
            last = pe.matmul(k.ps[at % 2][:, 0:CH], k.w[:, j, m * P:(m + 1) * P],
                             k.xT[:, j, n * CH:(n + 1) * CH], start=(j == 0), stop=(j == KT - 1))
        last.then_inc(proj_ready, 1)

    def vector(dve, at):
        m, n = divmod(at, NC)
        dve.wait_ge(proj_ready, at + 1)
        for out, a, b in dst(m, n):
            r = k.rstd[:, n * CH + a:n * CH + b]
            src = k.ps[at % 2][:, a:b]
            if len(out.shape) == 3:
                r = r.rearrange("p (x y) -> p x y", y=L)
                src = src.rearrange("p (x y) -> p x y", y=L)
            last = dve.tensor_tensor(out, src, r, ALU.mult)
        last.then_inc(proj_taken, 1)

    return [w_loaded, w_scaled, proj_ready, proj_taken], next_sync, next_pool, tensor, vector


PROJ = 4 * NC
SUMS = 2


def feature_sums(pe, k, src):
    for n in range(NC):
        last = pe.matmul(k.ps[SUMS + n][:, 0:CH], k.c("ones"), src[:, n * CH:(n + 1) * CH], start=True, stop=True)
    return last


def silu_gate(act, k, taken, done):
    for n in range(NC):
        act.wait_ge(taken, 3 * NC + n + 1)
        act.activation(k.qkvz[:, 3, n * CH:(n + 1) * CH], k.qkvz[:, 3, n * CH:(n + 1) * CH], ACT.Silu).then_inc(done, 1)


class Order:

    def __init__(self, eng, sem):
        self.eng, self.sem, self.n = eng, sem, 0

    def after(self, ins):
        ins.then_inc(self.sem, 1)
        self.n += 1
        self.eng.wait_ge(self.sem, self.n)


def head_A(nc, k, io, h):
    with ExitStack() as c:
        sbuf = lambda n, s: c.enter_context(nc.sbuf_tensor(n, s, F32))[:]
        sem = lambda n: c.enter_context(nc.semaphore(n))
        raw = sbuf("raw", [P, 3, 3 + T + B * 7])
        g_row, g_exp, g_tile = sbuf("g_row", [P, NT]), sbuf("g_exp", [P, G * P]), sbuf("g_tile", [P, TILES + B])
        grp, more, kept = k.w, sbuf("grp", [P, 8, G * P]), k.qd[:, 0:4 * G * P].rearrange("p (m n) -> p m n", m=4)
        prompt_set = [grp[:, i, :] for i in range(8)] + [more[:, i, :] for i in range(3)]
        small_set = [raw[:, 1, 0:P]] + [raw[:, 1, P + i * TS:P + (i + 1) * TS] for i in range(10)]
        u_masked = raw[0:TS, 1, 512:512 + B * P].rearrange("t (b v) -> t b v", b=B)
        EARLY = 3
        parts = (slice(0, EARLY * CH), slice(EARLY * CH, NT))
        post = (more.rearrange("p m n -> p (m n)")[:, 0:EARLY * CH], raw[:, 1, EARLY * CH:NT])
        Kt, Vb, XT, QK, WK = [(kept[:, i, :], more[:, 3 + i, :]) for i in range(4)] + [(more[:, 7, :], sbuf("wk", [P, G * P]))]
        hcol = sbuf("hcol", [P, 4, 17])
        S = sbuf("S", [P, 2, P])
        S0 = raw[:, 2, 0:B * P].rearrange("p (b v) -> p b v", b=B)
        u = sbuf("u", [P, P])
        tail = sbuf("tailbuf", [TS, 1])
        convo = sbuf("convo", [P, 27])
        convr = sbuf("convr", [27, 3 * P])
        O = raw[:, 0, 0:NT]
        squares = [more.rearrange("p m n -> p (m n)")[:, 0:NT], k.qd]
        Q = k.qkvz
        w_sems, p_sync, p_pool, p_tensor, p_vector = project_head(
            nc, k, io, c, "A", h,
            lambda m, n: [(Q[:, 3, n * CH:(n + 1) * CH], 0, CH)] if m == 3 else
            ([(raw[:, m, 3 + n * CH:3 + (n + 1) * CH], 0, CH)] if n < NC - 1 else
             [(raw[:, m, 3 + n * CH:3 + T], 0, T - n * CH),
              (raw[:, m, 3 + T:].rearrange("p (b r) -> p b r", r=7)[:, :, 3:7], T - n * CH, CH)]))
        names = ["g_loaded", "s_loaded", "conv_done", "conv_kept", "conv_turned", "conv_out",
                 "silu_done", "sq_done", "ss_done", "ln_done", "root_done", "normed",
                 "dve_order", "grams", "rows_turned", "o_made", "exp_in", "exp_out", "product", "operand", "operand_s", "u_made", "u_kept",
                 "s_made", "s_kept", "o_kept", "um_ready", "sn_made", "sn_kept", "out_stored", "matrices_used", "post_sq", "post_ss", "post_ln",
                 "post_root", "post_ready", "gate_done", "cols_done"]
        s = {n: sem(n) for n in names}
        block = c.enter_context(nc.Block())
        u_bank, s_bank, o_bank = k.ps[0][:, 0:P], k.ps[0][:, P:2 * P], k.ps[1][:, 0:P]
        FIRST, SECOND, SUM = range(3)
        place = lambda n, h2: (k.ps[2 + 2 * h2][:, 0:2 * P], k.ps[3 + 2 * h2][:, 2 * P:4 * P], k.ps[3 + 2 * h2][:, 0:2 * P])[n]

        groups = [(g * G * P, G, P) for g in range(TILES // G)] + [(T, 1, TS)]

        @block.sync
        def _(sp):
            sp.dma_start(g_row, io.scr_g[bass.ds(h, 1), :].broadcast_to([P, NT])).then_inc(s["g_loaded"], 16)
            sp.wait_ge(s["conv_out"], 1)
            for m in range(3):
                col = bass.ds(h * P + m * HD, P)
                sp.dma_start(io.out_delta_conv_prompt[0, 0, :, col], convr[0:3, m * P:(m + 1) * P]).then_inc(s["out_stored"], 16)
                sp.dma_start(io.out_delta_conv_sample[0, :, :, col].rearrange("b r c -> (b r) c"),
                             convr[3:27, m * P:(m + 1) * P]).then_inc(s["out_stored"], 16)
            sp.wait_ge(s["conv_out"], 1)
            sp.dma_start(S0, io.state_delta[0, :, bass.ds(h, 1), :, :].rearrange("b o k v -> k (b o) v")).then_inc(s["s_loaded"], 16)
            sp.wait_ge(s["matrices_used"], 1)
            p_sync(sp)
            sp.wait_ge(s["s_kept"], TILES)
            sp.dma_start(io.out_delta_prompt[0, 0, bass.ds(h, 1)].rearrange("o k v -> (o k) v"), S[:, TILES % 2, :]).then_inc(s["out_stored"], 16)
            sp.wait_ge(s["sn_kept"], 1)
            sp.dma_start(io.out_delta_sample[0, :, bass.ds(h, 1), :, :].rearrange("b o k v -> k (b o) v"), S0).then_inc(s["out_stored"], 16)
            for i in range(2):
                sp.wait_ge(s["post_ready"], i + 1)
                sp.dma_start(io.scr_o[bass.ds(h, 1)].rearrange("o p n -> (o p) n")[:, parts[i]], O[:, parts[i]]).then_inc(s["out_stored"], 16)
            sp.wait_ge(s["out_stored"], 16 * 10)

        @block.gpsimd
        def _(pool):
            p_pool(pool)

        @block.tensor
        def _(pe):
            def turn_conv(m):
                pe.wait_ge(s["conv_kept"], m + 1)
                if m:
                    pe.wait_ge(s["cols_done"], m)
                pe.transpose(k.ps[7][0:27, 0:P], convo, k.c("ident")).then_inc(s["conv_turned"], 1)

            for at in range(PROJ):
                p_tensor(pe, at)
                if at in (NC + 1, 2 * NC + 1, 3 * NC + 1):
                    turn_conv(at // NC - 1)
                if at in (NC + 3, 2 * NC + 3):
                    m = at // NC - 1
                    pe.wait_ge(s["sq_done"], m + 1)
                    if m:
                        pe.wait_ge(s["ln_done"], NC)
                    feature_sums(pe, k, squares[m]).then_inc(s["ss_done"], 1)
            pe.wait_ge(s["normed"], 2)
            pe.wait_ge(s["cols_done"], 3)
            used = used_s = 0

            def recur(step):
                if step < 0:
                    return
                tile, odd = divmod(step, 2)
                f, sl = (tile // G) % 2, slice(tile % G * P, (tile % G + 1) * P)
                if not odd:
                    if tile:
                        pe.wait_ge(s["s_kept"], tile)
                    pe.matmul(u_bank, XT[f][:, sl], Vb[f][:, sl], start=True, stop=False)
                    pe.matmul(u_bank, WK[f][:, sl], S[:, tile % 2, :], start=False, stop=True).then_inc(s["u_made"], 1)
                    if tile:
                        pe.wait_ge(s["o_kept"], tile)
                    pe.matmul(o_bank, S[:, tile % 2, :], Q[:, 0, tile * P:(tile + 1) * P], start=True, stop=False)
                else:
                    pe.wait_ge(s["u_kept"], tile + 1)
                    pe.matmul(s_bank, Kt[f][:, sl], u, start=True, stop=True).then_inc(s["s_made"], 1)
                    pe.matmul(o_bank, u, QK[f][:, sl], start=False, stop=True).then_inc(s["o_made"], 1)

            def early_sums(chunks):
                pe.wait_ge(s["post_sq"], 1)
                for n in chunks:
                    if n >= 2:
                        pe.wait_ge(s["post_ln"], n - 1)
                    pe.matmul(k.ps[4 + n % 2][:, 0:CH], k.c("ones"), post[0][:, n * CH:(n + 1) * CH], start=True, stop=True).then_inc(s["post_ss"], 1)

            for gi, (t0, ng, w) in enumerate(groups):
                sample = w != P
                Kb, DT, A, N, NTr, N2, N2T, N4, N4T, X0, X1 = small_set if sample else prompt_set
                f = gi % 2
                idn = k.c("ident")[0:w, 0:w]
                sl = [slice(i * w, (i + 1) * w) for i in range(ng)]
                hs = [slice(i * P, (i + 1) * P) for i in range(ng)]
                tok = [slice(t0 + i * w, t0 + (i + 1) * w) for i in range(ng)]
                halves = [range(ng)] if sample else [range(0, 2), range(2, 4)]
                step, last_step = (2 * G * (gi - 1), 2 * G * gi) if gi else (-20, -20)
                for i in range(ng):
                    last = pe.matmul(k.ps[6][0:w, sl[i]], Q[:, 1, tok[i]], Q[:, 1, tok[i]], start=True, stop=True)
                last.then_inc(s["grams"], 1)
                for i in range(ng):
                    last = pe.matmul(k.ps[7][0:w, sl[i]], Q[:, 1, tok[i]], Q[:, 0, tok[i]], start=True, stop=True)
                last.then_inc(s["grams"], 1)
                recur(step)
                recur(step + 1)
                step += 2

                def turn(bank, src):
                    if gi == 0 and src == 2:
                        pe.wait_ge(s["silu_done"], 3)
                    for i in range(ng):
                        last = pe.transpose(k.ps[bank][0:w, hs[i]], Q[:, src, tok[i]], k.c("ident"))
                    last.then_inc(s["rows_turned"], 1)

                def products(todo, by_act=False):
                    nonlocal used, used_s, step
                    for h2, half in enumerate(halves):
                        used += 1
                        pe.wait_ge(s["operand"], used)
                        if by_act and not sample:
                            used_s += 1
                            pe.wait_ge(s["operand_s"], used_s)
                        for bank, lhs, rhs in todo:
                            for i in half:
                                dst = place(bank, h2)[0:w, (i - half.start) * w:(i - half.start + 1) * w]
                                if rhs is None:
                                    last = pe.transpose(dst, lhs[0:w, sl[i]], idn)
                                else:
                                    last = pe.matmul(dst, lhs[0:w, sl[i]], rhs[0:w, sl[i]], start=True, stop=True)
                        last.then_inc(s["product"], 1)
                    if step < last_step:
                        recur(step)
                        step += 1

                products([(SUM, N, None)])
                turn(6, 1)
                if sample:
                    products([(FIRST, NTr, N)])
                    early_sums(range(0, 2))
                    turn(7, 2)
                    products([(SUM, N2, X0)])
                    early_sums(range(2, EARLY))
                else:
                    products([(FIRST, NTr, N), (SECOND, N, NTr)])
                    turn(7, 2)
                    products([(FIRST, N2T, N2), (SECOND, N2, N2T), (SUM, N2, X0)], by_act=True)
                    products([(FIRST, N4T, N4), (SUM, N4, X1)], by_act=True)
                    products([(SUM, N, X0)], by_act=True)
                    cur, nxt = X1, X0
                    for _l in range(3):
                        products([(FIRST, cur, None), (SECOND, N, cur)])
                        products([(SUM, NTr, N2)], by_act=True)
                        cur, nxt = nxt, cur
                for h2, half in enumerate(halves):
                    used += 1
                    pe.wait_ge(s["operand"], used)
                    for i in half:
                        last = pe.matmul(place(FIRST, h2)[:, (i - half.start) * w:(i - half.start + 1) * w], Kb[0:w, hs[i]], XT[f][0:w, sl[i]], start=True, stop=True)
                    last.then_inc(s["product"], 1)
                for rest in range(step, last_step):
                    recur(rest)
                if sample:
                    used += 1
                    pe.wait_ge(s["operand"], used)
                else:
                    used_s += 2
                    pe.wait_ge(s["operand_s"], used_s)
            f = len(groups) % 2 ^ 1
            pe.wait_ge(s["s_loaded"], 16)
            pe.wait_ge(s["s_kept"], TILES)
            pe.matmul(k.ps[0][0:TS, 0:P], XT[f][0:TS, 0:TS], Vb[f][0:TS, 0:P], start=True, stop=False)
            for b in range(B):
                last = pe.matmul(k.ps[0][0:TS, 0:P], WK[f][:, b * TS:(b + 1) * TS], S0[:, b, :], start=False, stop=(b == B - 1))
            last.then_inc(s["u_made"], 1)
            pe.wait_ge(s["o_kept"], TILES)
            pe.wait_ge(s["u_kept"], TILES + 1)
            pe.matmul(k.ps[1][:, 0:TS], u[0:TS, :], QK[f][0:TS, 0:TS], start=True, stop=False)
            for b in range(B):
                last = pe.matmul(k.ps[1][:, b * L:(b + 1) * L], S0[:, b, :], Q[:, 0, T + b * L:T + (b + 1) * L],
                                 start=False, stop=(b == B - 1))
            last.then_inc(s["o_made"], 1)
            pe.wait_ge(s["um_ready"], 1)
            for half in range(2):
                last = pe.matmul(k.ps[2 + half][:, 0:512], Kt[f][0:TS, 0:P], u_masked[:, 4 * half:4 * half + 4, :].rearrange("t b v -> t (b v)"), start=True, stop=True)
            last.then_inc(s["sn_made"], 1)
            pe.wait_ge(s["post_sq"], 2)
            pe.wait_ge(s["post_ln"], EARLY)
            for n in range(EARLY, NC):
                pe.matmul(k.ps[4 + n % 2][:, 0:CH], k.c("ones"), post[1][:, (n - EARLY) * CH:(n - EARLY + 1) * CH],
                          start=True, stop=True).then_inc(s["post_ss"], 1)

        @block.vector
        def _(dve):
            d = Order(dve, s["dve_order"])
            for m in range(3):
                dve.memset(raw[:, m, 0:3], 0.0)
                last = dve.tensor_copy(raw[:, m, 3 + T:].rearrange("p (b r) -> p b r", r=7)[:, :, 0:3],
                                       k.conv_cols[:, bass.ds(h + m * H, 1), 0:24].rearrange("p o (b r) -> p (o b) r", r=3))
            d.after(last)
            cw = k.cw_head
            for m in range(3):
                last = dve.tensor_copy(cw[:, m, :], k.conv_cols[:, bass.ds(h + m * H, 1), 24:28].rearrange("p o r -> p (o r)"))
            d.after(last)
            d.after(dve.tensor_copy(hcol[:, 0:2, :], k.gate_cols[:, :, bass.ds(h, 1), :].rearrange("p u o t -> p u (o t)")))
            def keep_rows(m):
                if m:
                    dve.wait_ge(s["conv_turned"], m)
                dve.tensor_copy(convo[:, 0:3], raw[:, m, T:T + 3])
                dve.tensor_copy(convo[:, 3:27].rearrange("p (b r) -> p b r", r=3),
                                raw[:, m, 3 + T:].rearrange("p (b r) -> p b r", r=7)[:, :, 4:7]).then_inc(s["conv_kept"], 1)

            def convolve(m, taps):
                pieces = ((Q[:, m, 0:T], lambda j: raw[:, m, j:j + T]),
                          (Q[:, m, T:NT].rearrange("p (b l) -> p b l", l=L),
                           lambda j: raw[:, m, 3 + T:].rearrange("p (b r) -> p b r", r=7)[:, :, j:j + L]))
                for j in taps:
                    for out, src in pieces:
                        if j == 0:
                            last = dve.tensor_scalar(out, src(0), cw[:, m, 0:1], None, ALU.mult)
                        else:
                            last = dve.scalar_tensor_tensor(out, src(j), cw[:, m, j:j + 1], out, ALU.mult, ALU.add)
                    d.after(last)
                if j == 3:
                    dve.engine_nop().then_inc(s["conv_done"], 1)

            def take_rows(m):
                dve.wait_ge(s["conv_turned"], m + 1)
                dve.tensor_copy(convr[:, m * P:(m + 1) * P], k.ps[7][0:27, 0:P]).then_inc(s["cols_done"], 1)

            def norm(m):
                dve.wait_ge(s["root_done"], m + 1)
                dve.scalar_tensor_tensor(Q[:, m, :], Q[:, m, :], SCALE if m == 0 else 1.0, squares[m], ALU.mult, ALU.mult).then_inc(s["normed"], 1)

            for at in range(PROJ):
                p_vector(dve, at)
                m, n = divmod(at, NC)
                if m < 3 and n == NC - 1:
                    d.after(dve.engine_nop())
                    keep_rows(m)
                if m and n == 0:
                    convolve(m - 1, (0, 1))
                    if m > 1:
                        norm(m - 2)
                if m and n == 1:
                    convolve(m - 1, (2, 3))
                if m and n == 2:
                    take_rows(m - 1)
            dve.wait_ge(s["cols_done"], 3)
            dve.engine_nop().then_inc(s["conv_out"], 1)
            dve.wait_ge(s["exp_out"], 1)
            d.after(dve.tensor_tensor(hcol[:, 2, :], hcol[:, 2, :], hcol[:, 0, :], ALU.mult))
            d.after(dve.tensor_scalar(hcol[:, 3, :], hcol[:, 0, :], -1.0, None, ALU.mult))
            dve.memset(S[:, 0, :], 0.0)
            seen = 0

            def finish(i):
                dve.wait_ge(s["post_root"], i + 1)
                out = O[:, parts[i]]
                d.after(dve.scalar_tensor_tensor(out, out, k.vec[:, 0:1], post[i], ALU.mult, ALU.mult))
                dve.wait_ge(s["gate_done"], NC)
                dve.tensor_tensor(out, out, Q[:, 3, parts[i]], ALU.mult).then_inc(s["post_ready"], 1)

            def next_state(step):
                if step >= 0 and step % 2:
                    tile = step // 2
                    dve.wait_ge(s["s_made"], tile + 1)
                    if tile:
                        dve.wait_ge(s["s_kept"], tile)
                    dve.scalar_tensor_tensor(S[:, (tile + 1) % 2, :], S[:, tile % 2, :], g_tile[:, tile:tile + 1],
                                             s_bank, ALU.mult, ALU.add).then_inc(s["s_kept"], 1)

            for gi, (t0, ng, w) in enumerate(groups):
                sample = w != P
                Kb, DT, A, N, NTr, N2, N2T, N4, N4T, X0, X1 = small_set if sample else prompt_set
                f = gi % 2
                v3 = lambda ap, n=w: ap[0:w, 0:ng * n].rearrange("p (g n) -> p g n", g=ng)
                ti = t0 // P
                gcol = repeat(hcol[0:w, 1, ti:ti + ng], 2, w)
                mask = lambda n: repeat(k.c(n)[0:w, 0:w], 1, ng)
                row = g_row[0:w, t0:t0 + ng * w].rearrange("p (g n) -> p g n", g=ng)
                pre = "s_" if sample else ""
                halves = [range(ng)] if sample else [range(0, 2), range(2, 4)]
                step, last_step = (2 * G * (gi - 1), 2 * G * gi) if gi else (-20, -20)
                d.after(dve.tensor_tensor(v3(X0), row, gcol, ALU.subtract))
                dve.tensor_tensor(v3(X1), v3(X0), mask(pre + "not_lower"), ALU.add).then_inc(s["exp_in"], 1)
                dve.tensor_tensor(v3(DT), v3(X0), mask(pre + "not_causal"), ALU.subtract).then_inc(s["exp_in"], 1)
                dve.wait_ge(s["exp_out"], 3 * gi + 2)
                d.after(dve.tensor_tensor(v3(A), v3(X1), repeat(hcol[0:w, 3, ti:ti + ng], 2, w), ALU.mult))
                dve.wait_ge(s["grams"], 2 * gi + 1)
                d.after(dve.tensor_tensor(v3(A), v3(k.ps[6]), v3(A), ALU.mult))
                if sample:
                    dve.tensor_copy(v3(N), v3(A)).then_inc(s["operand"], 1)
                else:
                    dve.tensor_tensor(v3(N), v3(A), mask("diag16"), ALU.mult).then_inc(s["operand"], 2)
                dve.wait_ge(s["exp_out"], 3 * gi + 4)
                dve.wait_ge(s["grams"], 2 * gi + 2)
                dve.tensor_tensor(v3(QK[f]), v3(k.ps[7]), v3(DT), ALU.mult)
                next_state(step + 1)
                step += 2

                def others():
                    kt = lambda ap: v3(ap, P)
                    dve.wait_ge(s["rows_turned"], 2 * gi + 1)
                    dve.tensor_tensor(kt(Kb), kt(k.ps[6]), repeat(hcol[0:w, 2, ti:ti + ng], 2, P), ALU.mult)
                    dve.tensor_tensor(Q[:, 0, t0:t0 + ng * w], Q[:, 0, t0:t0 + ng * w], g_exp[:, 0:ng * w], ALU.mult)
                    if sample:
                        d.after(dve.tensor_tensor(N4[0:w, 0:w], DT[0:w, 0:w], k.c("s_last")[0:w, :], ALU.mult))
                        d.after(dve.tensor_reduce(tail, N4[0:w, 0:w], X, ALU.add))
                        dve.tensor_scalar(Kt[f][0:w, 0:P], k.ps[6][0:w, 0:P], tail, None, ALU.mult)
                    else:
                        dve.tensor_tensor(kt(Kt[f]), kt(k.ps[6]), repeat(DT.rearrange("p (g n) -> p g n", g=ng)[:, :, P - 1], 2, P), ALU.mult)
                    dve.wait_ge(s["rows_turned"], 2 * gi + 2)
                    dve.tensor_tensor(kt(Vb[f]), kt(k.ps[7]), repeat(hcol[0:w, 0, ti:ti + ng], 2, P), ALU.mult)

                def part(ap, half, n=w):
                    return ap[0:w, half.start * n:half.stop * n].rearrange("p (g n) -> p g n", n=n)

                def take(todo):
                    nonlocal seen, step
                    for h2, half in enumerate(halves):
                        seen += 1
                        dve.wait_ge(s["product"], seen)
                        for fn in todo:
                            last = fn(h2, half)
                        last.then_inc(s["operand"], 1)
                    if step < last_step:
                        next_state(step)
                        step += 1

                hmask = lambda n, half: repeat(k.c(n)[0:w, 0:w], 1, len(half))
                made = lambda bank, h2, half: place(bank, h2)[0:w, 0:len(half) * w].rearrange("p (g n) -> p g n", n=w)
                cp = lambda dst, bank: (lambda h2, half: dve.tensor_copy(part(dst, half), made(bank, h2, half)))
                plus = lambda dst, src, bank: (lambda h2, half: dve.tensor_tensor(part(dst, half), part(src, half), made(bank, h2, half), ALU.add))
                times = lambda dst, src, m: (lambda h2, half: dve.tensor_tensor(part(dst, half), part(src, half), hmask(m, half), ALU.mult))
                take([cp(NTr, SUM), lambda h2, half: dve.tensor_tensor(part(X0, half), made(SUM, h2, half), hmask("ident", half), ALU.add)])
                if sample:
                    take([cp(N2, FIRST)])
                    others()
                    take([plus(XT[f], X0, SUM)])
                else:
                    take([cp(N2T, SECOND)])
                    others()
                    take([cp(N4T, SECOND), plus(X1, X0, SUM)])
                    take([plus(X0, X1, SUM)])
                    take([plus(X1, X0, SUM), times(N, A, "under32")])
                    cur, nxt = X1, X0
                    for lvl in (32, 64, 128):
                        take([cp(N2, SECOND)])
                        if lvl < 128:
                            take([plus(nxt, cur, SUM), times(N, A, f"under{2 * lvl}")])
                        else:
                            take([plus(XT[f], cur, SUM)])
                        cur, nxt = nxt, cur
                for h2, half in enumerate(halves):
                    seen += 1
                    dve.wait_ge(s["product"], seen)
                    if sample:
                        dve.scalar_tensor_tensor(WK[f][:, 0:B * TS].rearrange("p (b t) -> p b t", b=B), repeat(place(FIRST, 0)[:, 0:TS], 1, B), -1.0,
                                                 k.c("s_cols").rearrange("p (b t) -> p b t", b=B), ALU.mult, ALU.mult).then_inc(s["operand"], 1)
                if gi == len(groups) - 2:
                    dve.engine_nop().then_inc(s["matrices_used"], 1)
                for rest in range(step, last_step):
                    next_state(rest)
            dve.wait_ge(s["u_kept"], TILES + 1)
            for half in range(2):
                last = dve.tensor_tensor(u_masked[:, 4 * half:4 * half + 4, :], repeat(u[0:TS, :], 1, 4),
                                         repeat(k.c("s_rows")[0:TS, 4 * half:4 * half + 4], 2, P), ALU.mult)
            last.then_inc(s["um_ready"], 1)
            dve.wait_ge(s["o_made"], TILES + 1)
            d.after(dve.tensor_tensor(S0, S0, repeat(g_tile[:, TILES:], 2, P), ALU.mult))
            finish(0)
            dve.wait_ge(s["sn_made"], 1)
            for half in range(2):
                last = dve.tensor_tensor(S0[:, 4 * half:4 * half + 4, :], S0[:, 4 * half:4 * half + 4, :],
                                         k.ps[2 + half].rearrange("p (b v) -> p b v", b=4), ALU.add)
            last.then_inc(s["sn_kept"], 1)
            finish(1)

        @block.scalar
        def _(act):
            for b in (h, h + H):
                for dst, src in ((io.out_win_k_sample, io.cache_win_k), (io.out_win_v_sample, io.cache_win_v)):
                    act.dma_start(dst[0, bass.ds(b, 1), 0:WBUF - L].rearrange("b (g r) h d -> (b g) (r h d)", g=28),
                                  src[0, bass.ds(b, 1), L:WBUF].rearrange("b (g r) h d -> (b g) (r h d)", g=28)).then_inc(k.windows_shifted, 16)
            for m in range(2):
                act.wait_ge(s["conv_done"], m + 1)
                act.activation(Q[:, m, :], Q[:, m, :], ACT.Silu).then_inc(s["silu_done"], 1)
                act.wait_ge(s["silu_done"], m + 1)
                act.activation(squares[m], Q[:, m, :], ACT.Square).then_inc(s["sq_done"], 1)
                act.wait_ge(s["ss_done"], m + 1)
                for n in range(NC):
                    act.activation(squares[m][:, n * CH:(n + 1) * CH], k.ps[SUMS + n][:, 0:CH], ACT.Ln, bias=k.eps).then_inc(s["ln_done"], 1)
                act.wait_ge(s["ln_done"], (m + 1) * NC)
                act.activation(squares[m], squares[m], ACT.Exp, scale=-0.5).then_inc(s["root_done"], 1)
                if m == 0:
                    act.wait_ge(s["g_loaded"], 16)
                    act.activation(g_tile[:, 0:TILES], g_row[:, P - 1:T:P], ACT.Exp)
                    act.activation(g_tile[:, TILES:], g_row[:, T + L - 1::L], ACT.Exp)
                    act.activation(hcol[:, 2, :], hcol[:, 1, :], ACT.Exp).then_inc(s["exp_out"], 1)
            act.wait_ge(s["conv_done"], 3)
            act.activation(Q[:, 2, :], Q[:, 2, :], ACT.Silu).then_inc(s["silu_done"], 1)
            silu_gate(act, k, w_sems[3], s["gate_done"])

            def log_sums(chunks):
                for n in chunks:
                    act.wait_ge(s["post_ss"], n + 1)
                    i = n >= EARLY
                    at = (n - EARLY * i) * CH
                    act.activation(post[i][:, at:at + CH], k.ps[4 + n % 2][:, 0:CH], ACT.Ln, bias=k.eps, scale=1.0 / P).then_inc(s["post_ln"], 1)

            def root(i, chunks):
                act.wait_ge(s["post_ln"], chunks)
                act.activation(post[i], post[i], ACT.Exp, scale=-0.5).then_inc(s["post_root"], 1)

            made = 0

            def copy_product(dst, scale=1.0):
                nonlocal made
                for h2 in range(2):
                    made += 1
                    act.wait_ge(s["product"], made)
                    act.activation(dst[:, h2 * 2 * P:(h2 + 1) * 2 * P], place(FIRST, h2), ACT.Copy, scale=scale).then_inc(s["operand_s"], 1)

            def keep_u(tile):
                act.wait_ge(s["u_made"], tile + 1)
                act.copy(u, u_bank).then_inc(s["u_kept"], 1)

            def keep_o(tile):
                act.wait_ge(s["o_made"], tile + 1)
                act.copy(O[:, tile * P:(tile + 1) * P], o_bank).then_inc(s["o_kept"], 1)

            def follow(step):
                if step >= 0:
                    if step % 2:
                        keep_o(step // 2)
                    else:
                        keep_u(step // 2)

            for gi, (t0, ng, w) in enumerate(groups):
                Kb, DT, A, N, NTr, N2, N2T, N4, N4T, X0, X1 = small_set if w != P else prompt_set
                act.wait_ge(s["exp_in"], 2 * gi + 1)
                act.activation(X1[0:w, 0:ng * w], X1[0:w, 0:ng * w], ACT.Exp, scale=-1.0).then_inc(s["exp_out"], 1)
                act.wait_ge(s["exp_in"], 2 * gi + 2)
                act.activation(DT[0:w, 0:ng * w], DT[0:w, 0:ng * w], ACT.Exp).then_inc(s["exp_out"], 1)
                act.activation(g_exp[:, 0:ng * w], g_row[:, t0:t0 + ng * w], ACT.Exp).then_inc(s["exp_out"], 1)
                f = gi % 2
                step, last_step = (2 * G * (gi - 1), 2 * G * gi) if gi else (-20, -20)
                if w != P:
                    act.wait_ge(s["matrices_used"], 1)
                    act.wait_ge(s["o_kept"], -(-EARLY * CH // P))
                    act.activation(post[0], O[:, parts[0]], ACT.Square).then_inc(s["post_sq"], 1)
                else:
                    follow(step)
                    follow(step + 1)
                    step += 2
                    for dst in (None, N2, N4, N, None, NTr, None, NTr, None, NTr, None):
                        if dst is None:
                            made += 2
                        else:
                            copy_product(dst)
                        if step < last_step:
                            follow(step)
                            step += 1
                    copy_product(WK[f], -1.0)
                    for rest in range(step, last_step):
                        follow(rest)
                    continue
                for tile in range(G * (gi - 1), G * gi):
                    keep_u(tile)
                    keep_o(tile)
                    if tile == TILES - 3:
                        log_sums(range(0, 2))
                    if tile == TILES - 2:
                        log_sums(range(2, EARLY))
                        root(0, EARLY)
            act.wait_ge(s["u_made"], TILES + 1)
            act.copy(u[0:TS, :], k.ps[0][0:TS, 0:P]).then_inc(s["u_kept"], 1)
            act.wait_ge(s["o_made"], TILES + 1)
            act.copy(O[:, T:NT], k.ps[1][:, 0:TS]).then_inc(s["o_kept"], 1)
            act.wait_ge(s["o_kept"], TILES + 1)
            act.wait_ge(s["sn_made"], 1)
            act.activation(post[1], O[:, parts[1]], ACT.Square).then_inc(s["post_sq"], 1)
            log_sums(range(EARLY, NC))
            root(1, NC)
    clear(nc, w_sems + list(s.values()))


def head_B(nc, k, io, h):
    with ExitStack() as c:
        sbuf = lambda n, s: c.enter_context(nc.sbuf_tensor(n, s, F32))[:]
        sem = lambda n: c.enter_context(nc.semaphore(n))
        ret = sbuf("ret", [P, RET])
        buf = sbuf("retbuf", [P, 2, 3, G * P])
        R = sbuf("R", [P, 2, P])
        R0 = sbuf("R0", [P, B, P])
        vm = sbuf("vm", [TS, B, P])
        sq, O = sbuf("sqB", [P, NT]), sbuf("OB", [P, NT])
        bn = sbuf("bn", [P, 1])
        Q = k.qkvz
        qd = k.qd
        w_sems, p_sync, p_pool, p_tensor, p_vector = project_head(
            nc, k, io, c, "B", h, lambda m, n: [(Q[:, m, n * CH:(n + 1) * CH], 0, CH)])
        names = ["ret_loaded", "r0_loaded", "qd_ready", "turned_b", "tiles_b", "o_made", "r_made", "r_kept", "o_kept_b",
                 "rn_made", "rn_kept", "gate_b", "mean_made", "centred", "squared_b", "var_made", "logged_b", "root_b", "post_b",
                 "stored_b", "order_b"]
        s = {n: sem(n) for n in names}
        block = c.enter_context(nc.Block())
        groups = [(g * G * P, G, P) for g in range(TILES // G)] + [(T, 1, TS)]
        EARLY, NORM_AT = 3, 11
        parts = (slice(0, EARLY * CH), slice(EARLY * CH, NT))
        norm_bank = lambda n: k.ps[5 if n < EARLY else n - EARLY + 2][:, 0:CH]
        chunk = lambda n: slice(n * CH, (n + 1) * CH)

        @block.sync
        def _(sp):
            sp.dma_start(ret, io.c_ret[bass.ds(h, 1)].rearrange("o p n -> (o p) n")).then_inc(s["ret_loaded"], 16)
            sp.dma_start(R0, io.state_ret[0, :, bass.ds(h, 1), :, :].rearrange("b o k v -> k (b o) v")).then_inc(s["r0_loaded"], 16)
            sp.wait_ge(w_sems[2], 4 * NC)
            p_sync(sp)
            sp.wait_ge(s["r_kept"], TILES)
            sp.dma_start(io.out_ret_prompt[0, 0, bass.ds(h, 1)].rearrange("o k v -> (o k) v"), R[:, TILES % 2, :]).then_inc(s["stored_b"], 16)
            sp.wait_ge(s["rn_kept"], 1)
            sp.dma_start(io.out_ret_sample[0, :, bass.ds(h, 1), :, :].rearrange("b o k v -> k (b o) v"), R0).then_inc(s["stored_b"], 16)
            for i in range(2):
                sp.wait_ge(s["post_b"], i + 1)
                sp.dma_start(io.scr_o[bass.ds(h + H, 1)].rearrange("o p n -> (o p) n")[:, parts[i]], O[:, parts[i]]).then_inc(s["stored_b"], 16)
            sp.wait_ge(s["stored_b"], 16 * 4)

        @block.gpsimd
        def _(pool):
            p_pool(pool)

        @block.tensor
        def _(pe):
            for at in range(PROJ):
                p_tensor(pe, at)
            def prepare(gi):
                t0, ng, w = groups[gi]
                hs = [slice(i * P, (i + 1) * P) for i in range(ng)]
                tok = [slice(t0 + i * w, t0 + (i + 1) * w) for i in range(ng)]
                if gi:
                    pe.wait_ge(s["tiles_b"], gi)
                for i in range(ng):
                    pe.transpose(k.ps[2][0:w, hs[i]], Q[:, 1, tok[i]], k.c("ident"))
                    pe.transpose(k.ps[3][0:w, hs[i]], Q[:, 2, tok[i]], k.c("ident"))
                    last = pe.matmul(k.ps[4][0:w, i * w:(i + 1) * w], Q[:, 1, tok[i]], Q[:, 0, tok[i]], start=True, stop=True)
                last.then_inc(s["turned_b"], 1)

            def mean(n):
                pe.wait_ge(s["o_kept_b"], TILES + 1 if n >= EARLY else -(-(n + 1) * CH // P))
                if 0 < n < EARLY:
                    pe.wait_ge(s["centred"], n)
                pe.matmul(norm_bank(n), k.c("ones"), O[:, chunk(n)], start=True, stop=True).then_inc(s["mean_made"], 1)

            def variance(n):
                pe.wait_ge(s["squared_b"], n + 1)
                if n < EARLY:
                    pe.wait_ge(s["centred"], EARLY)
                if 0 < n < EARLY:
                    pe.wait_ge(s["logged_b"], n)
                pe.matmul(norm_bank(n), k.c("ones"), sq[:, chunk(n)], start=True, stop=True).then_inc(s["var_made"], 1)

            pe.wait_ge(s["qd_ready"], 1)
            pe.wait_ge(w_sems[3], PROJ)
            prepare(0)
            for tile in range(TILES):
                gi, i = divmod(tile, G)
                Ktl, V, PT = [buf[:, gi % 2, j, i * P:(i + 1) * P] for j in range(3)]
                if i == 0:
                    pe.wait_ge(s["tiles_b"], gi + 1)
                if tile >= 2:
                    pe.wait_ge(s["r_kept"], tile - 1)
                pe.matmul(k.ps[tile % 2][:, 0:P], Ktl, V, start=True, stop=True).then_inc(s["r_made"], 1)
                if tile >= 2:
                    pe.wait_ge(s["o_kept_b"], tile - 1)
                pe.matmul(k.ps[6 + tile % 2][:, 0:P], V, PT, start=True, stop=False)
                if tile:
                    pe.wait_ge(s["r_kept"], tile)
                pe.matmul(k.ps[6 + tile % 2][:, 0:P], R[:, tile % 2, :], qd[:, tile * P:(tile + 1) * P], start=False, stop=True).then_inc(s["o_made"], 1)
                if i == 1:
                    prepare(gi + 1)
                step = tile - NORM_AT
                if 0 <= step < EARLY:
                    mean(step)
                if step >= EARLY:
                    variance(step - EARLY)
            Ktl, V, PT = [buf[:, (len(groups) - 1) % 2, j, :] for j in range(3)]
            pe.wait_ge(s["tiles_b"], len(groups))
            pe.wait_ge(s["r0_loaded"], 16)
            pe.wait_ge(s["o_kept_b"], TILES)
            pe.wait_ge(s["r_kept"], TILES)
            pe.matmul(k.ps[6][:, 0:TS], V[0:TS, 0:P], PT[0:TS, 0:TS], start=True, stop=False)
            for b in range(B):
                last = pe.matmul(k.ps[6][:, b * L:(b + 1) * L], R0[:, b, :], qd[:, T + b * L:T + (b + 1) * L],
                                 start=False, stop=(b == B - 1))
            last.then_inc(s["o_made"], 1)
            for half in range(2):
                last = pe.matmul(k.ps[half], Ktl[0:TS, 0:P], vm[:, 4 * half:4 * half + 4, :].rearrange("p b v -> p (b v)"),
                                 start=True, stop=True)
            last.then_inc(s["rn_made"], 1)
            for n in range(TILES - NORM_AT - EARLY, EARLY):
                variance(n)
            for n in range(EARLY, NC):
                mean(n)
            for n in range(EARLY, NC):
                variance(n)

        @block.vector
        def _(dve):
            d = Order(dve, s["order_b"])
            dve.memset(R[:, 0, :], 0.0)
            dve.tensor_copy(bn, k.b_norm[:, bass.ds(h, 1)])
            for at in range(NC):
                p_vector(dve, at)
            dve.wait_ge(w_sems[3], NC)
            dve.wait_ge(s["ret_loaded"], 16)
            dve.tensor_tensor(qd[:, 0:T].rearrange("p (t n) -> p t n", n=P), Q[:, 0, 0:T].rearrange("p (t n) -> p t n", n=P),
                              repeat(ret[:, P:2 * P], 1, TILES), ALU.mult)
            dve.tensor_tensor(qd[:, T:NT], Q[:, 0, T:NT], ret[:, 290:322], ALU.mult).then_inc(s["qd_ready"], 1)
            for at in range(NC, PROJ):
                p_vector(dve, at)
            def keep_group(gi):
                Ktl, V, PT = [buf[:, gi % 2, i, :] for i in range(3)]
                dve.wait_ge(s["turned_b"], gi + 1)
                if gi < len(groups) - 1:
                    if gi >= 2:
                        dve.wait_ge(s["o_made"], (gi - 1) * G)
                    dve.tensor_copy(V, k.ps[3])
                    dve.tensor_scalar(Ktl, k.ps[2], ret[:, 256:257], None, ALU.mult)
                    dve.tensor_tensor(PT.rearrange("p (g n) -> p g n", g=G), k.ps[4].rearrange("p (g n) -> p g n", g=G),
                                      repeat(ret[:, 0:P], 1, G), ALU.mult).then_inc(s["tiles_b"], 1)
                else:
                    dve.wait_ge(s["o_made"], (gi - 1) * G)
                    d.after(dve.tensor_copy(V[0:TS, 0:P], k.ps[3][0:TS, 0:P]))
                    dve.tensor_tensor(vm, repeat(V[0:TS, 0:P], 1, B), repeat(k.c("s_rows")[0:TS, :], 2, P), ALU.mult)
                    dve.tensor_scalar(Ktl[0:TS, 0:P], k.ps[2][0:TS, 0:P], ret[0:TS, 322:323], None, ALU.mult)
                    dve.tensor_tensor(PT[0:TS, 0:TS], k.ps[4][0:TS, 0:TS], ret[0:TS, 258:290], ALU.mult).then_inc(s["tiles_b"], 1)

            def centre(n):
                dve.wait_ge(s["mean_made"], n + 1)
                dve.scalar_tensor_tensor(O[:, chunk(n)], norm_bank(n), -1.0 / P, O[:, chunk(n)], ALU.mult, ALU.add).then_inc(s["centred"], 1)

            def finish(i):
                out = O[:, parts[i]]
                dve.wait_ge(s["root_b"], i + 1)
                d.after(dve.scalar_tensor_tensor(out, out, bn, sq[:, parts[i]], ALU.mult, ALU.mult))
                dve.wait_ge(s["gate_b"], NC)
                dve.tensor_tensor(out, out, Q[:, 3, parts[i]], ALU.mult).then_inc(s["post_b"], 1)

            keep_group(0)
            for tile in range(TILES):
                gi, i = divmod(tile, G)
                dve.wait_ge(s["r_made"], tile + 1)
                if tile >= 1:
                    dve.wait_ge(s["o_made"], tile)
                    dve.wait_ge(s["r_kept"], tile)
                dve.scalar_tensor_tensor(R[:, (tile + 1) % 2, :], R[:, tile % 2, :], ret[:, 257:258], k.ps[tile % 2][:, 0:P],
                                         ALU.mult, ALU.add).then_inc(s["r_kept"], 1)
                if i == 1:
                    keep_group(gi + 1)
                if 0 <= tile - NORM_AT < EARLY:
                    centre(tile - NORM_AT)
            dve.wait_ge(s["rn_made"], 1)
            for half in range(2):
                last = dve.scalar_tensor_tensor(R0[:, 4 * half:4 * half + 4, :], R0[:, 4 * half:4 * half + 4, :], ret[:, 323:324],
                                                k.ps[half].rearrange("p (b v) -> p b v", b=4), ALU.mult, ALU.add)
            last.then_inc(s["rn_kept"], 1)
            for n in range(EARLY, NC):
                centre(n)
            finish(0)
            finish(1)

        @block.scalar
        def _(act):
            def square(n):
                act.wait_ge(s["centred"], n + 1)
                act.activation(sq[:, chunk(n)], O[:, chunk(n)], ACT.Square).then_inc(s["squared_b"], 1)

            def log_variance(n):
                act.wait_ge(s["var_made"], n + 1)
                act.activation(sq[:, chunk(n)], norm_bank(n), ACT.Ln, bias=k.eps, scale=1.0 / P).then_inc(s["logged_b"], 1)

            def root(i, logged):
                act.wait_ge(s["logged_b"], logged)
                act.activation(sq[:, parts[i]], sq[:, parts[i]], ACT.Exp, scale=-0.5).then_inc(s["root_b"], 1)

            silu_gate(act, k, w_sems[3], s["gate_b"])
            for tile in range(TILES + 1):
                n = P if tile < TILES else TS
                act.wait_ge(s["o_made"], tile + 1)
                act.copy(O[:, tile * P:tile * P + n], k.ps[6 + tile % 2][:, 0:n]).then_inc(s["o_kept_b"], 1)
                step = tile - NORM_AT - 1
                if 0 <= step < EARLY:
                    square(step)
                elif step >= EARLY:
                    log_variance(step - EARLY)
            for n in range(TILES - NORM_AT - EARLY, EARLY):
                log_variance(n)
            root(0, EARLY)
            for n in range(EARLY, NC):
                square(n)
            for n in range(EARLY, NC):
                log_variance(n)
            root(1, NC)
    clear(nc, w_sems + list(s.values()))


def output_projection(nc, k, io, layer):
    with ExitStack() as c:
        sem = lambda n: c.enter_context(nc.semaphore(f"{n}_{layer}"))
        wout = c.enter_context(nc.sbuf_tensor(f"wout{layer}", [P, KT, D_MODEL], F32))[:]
        o = k.big[:, 0:2 * KT * CH].rearrange("p (s k n) -> p s k n", s=2, k=KT)
        wo_loaded, o_loaded = [sem(f"wo_loaded{m}") for m in range(KT)], [sem("o_loaded0"), sem("o_loaded1")]
        w_loaded, w_scaled = sem("w_loaded_next"), sem("w_scaled_next")
        load_weights, scale_weights = head_weights(k, io, "C", 0, w_loaded, w_scaled)
        y_made, y_added = sem("y_made"), sem("y_added")
        sq_made, sq_added, sq_summed, logged = sem("sq_made"), sem("sq_added"), sem("sq_summed"), sem("logged")
        if layer == 0:
            sq, total = [c.enter_context(nc.sbuf_tensor(n, [P, w, CH], F32))[:] for n, w in (("osq", 2), ("ototal", NC))]
        block = c.enter_context(nc.Block())
        w = io.w_out_even[0] if layer == 0 else io.w_out_odd[0]

        @block.sync
        def _(sp):
            for m in range(KT):
                sp.dma_start(wout[:, :, m * P:(m + 1) * P], w.rearrange("(k p) n -> p k n", p=P)[:, :, m * P:(m + 1) * P]).then_inc(wo_loaded[m], 16)
            if layer == 0:
                load_weights(sp)

        @block.gpsimd
        def _(pool):
            if layer == 0:
                scale_weights(pool)

        @block.tensor
        def _(pe):
            def sum_squares(n):
                pe.wait_ge(sq_added, (n + 1) * KT)
                if n >= 2:
                    pe.wait_ge(logged, n - 1)
                pe.matmul(k.ps[4 + n % 2][:, 0:CH], k.c("ones"), total[:, n, :], start=True, stop=True).then_inc(sq_summed, 1)

            for n in range(NC):
                pe.wait_ge(o_loaded[n % 2], 16 * (n // 2 + 1))
                for m in range(KT):
                    at = n * KT + m
                    if n == 0:
                        pe.wait_ge(wo_loaded[m], 16)
                    if at >= 4:
                        pe.wait_ge(y_added, at - 3)
                    for j in range(KT):
                        last = pe.matmul(k.ps[at % 4][:, 0:CH], wout[:, j, m * P:(m + 1) * P], o[:, n % 2, j, :],
                                         start=(j == 0), stop=(j == KT - 1))
                    last.then_inc(y_made, 1)
                    if layer == 0 and n and m == 2:
                        sum_squares(n - 1)
            if layer == 0:
                sum_squares(NC - 1)

        @block.vector
        def _(dve):
            def add_square(at):
                n, m = divmod(at, KT)
                dve.wait_ge(sq_made, at + 1)
                if m == 0:
                    dve.tensor_copy(total[:, n, :], sq[:, at % 2, :]).then_inc(sq_added, 1)
                else:
                    dve.wait_ge(sq_added, at)
                    dve.tensor_tensor(total[:, n, :], total[:, n, :], sq[:, at % 2, :], ALU.add).then_inc(sq_added, 1)

            for n in range(NC):
                for m in range(KT):
                    at = n * KT + m
                    dve.wait_ge(y_made, at + 1)
                    x = k.xT[:, m, n * CH:(n + 1) * CH]
                    dve.tensor_tensor(x, x, k.ps[at % 4][:, 0:CH], ALU.add).then_inc(y_added, 1)
                    if layer == 0 and at:
                        add_square(at - 1)
            if layer == 0:
                add_square(NC * KT - 1)

        @block.scalar
        def _(act):
            def log_sums(n):
                act.wait_ge(sq_summed, n + 1)
                act.activation(total[:, n, :], k.ps[4 + n % 2][:, 0:CH], ACT.Ln, bias=k.eps, scale=1.0 / D_MODEL).then_inc(logged, 1)

            for n in range(2):
                act.dma_start(o[:, n], io.scr_o[:, :, n * CH:(n + 1) * CH].rearrange("k p n -> p k n")).then_inc(o_loaded[n], 16)
            for n in range(NC):
                for m in range(KT):
                    at = n * KT + m
                    if layer == 0:
                        act.wait_ge(y_added, at + 1)
                        if at >= 2:
                            act.wait_ge(sq_added, at - 1)
                        act.activation(sq[:, at % 2, :], k.xT[:, m, n * CH:(n + 1) * CH], ACT.Square).then_inc(sq_made, 1)
                        if n and m == 4:
                            log_sums(n - 1)
                if n + 2 < NC:
                    act.wait_ge(y_made, (n + 1) * KT)
                    act.dma_start(o[:, n % 2], io.scr_o[:, :, (n + 2) * CH:(n + 3) * CH].rearrange("k p n -> p k n")).then_inc(o_loaded[n % 2], 16)
            if layer == 0:
                log_sums(NC - 1)
                act.wait_ge(logged, NC)
                act.activation(k.rstd, total.rearrange("p n c -> p (n c)"), ACT.Exp, scale=-0.5).then_inc(logged, 1)
    clear(nc, [*wo_loaded, *o_loaded, y_made, y_added, w_loaded, w_scaled, sq_made, sq_added, sq_summed, logged])


def row_gates_odd(nc, k, io):
    with ExitStack() as c:
        sem = lambda n: c.enter_context(nc.semaphore(n))
        w_loaded, w_scaled = sem("fw_loaded"), sem("fw_scaled")
        row_ready, row_taken = sem("f_row_ready"), sem("f_row_taken")
        a_step, d_step = sem("f_act"), sem("f_dve")
        turned, cols_ready, stored = sem("f_turned"), sem("f_cols"), sem("f_stored")
        w = c.enter_context(nc.sbuf_tensor("fw", [P, KT, 4], F32))
        rows = c.enter_context(nc.sbuf_tensor("frows", [4, NT], F32))
        tmp = c.enter_context(nc.sbuf_tensor("ftmp", [4, NT], F32))
        one = c.enter_context(nc.sbuf_tensor("fones", [4, T], F32))
        block = c.enter_context(nc.Block())

        @block.sync
        def _(sp):
            sp.dma_start(w[:, :, :], io.w_in_odd[0].rearrange("(k p) c -> p k c", p=P)[:, :, 2048:2052]).then_inc(w_loaded, 16)
            sp.wait_ge(d_step, 4)
            sp.dma_start(io.scr_f, tmp[:, 0:T]).then_inc(stored, 16)
            sp.wait_ge(cols_ready, 1)
            sp.dma_start(io.out_fox_logf_prompt[0, 0].rearrange("(t p) h -> p t h", p=P), k.logf_cols[:, 0:TILES, :]).then_inc(stored, 16)
            sp.dma_start(io.out_fox_logf_sample.rearrange("b o l h -> (b o l) h"), k.logf_cols[0:TS, TILES, :]).then_inc(stored, 16)
            sp.wait_ge(stored, 48)

        @block.vector
        def _(dve):
            dve.memset(one[:, :], 1.0)
            dve.wait_ge(w_loaded, 16)
            dve.tensor_tensor(w[:, :, :], w[:, :, :], repeat(k.g_odd, 2, 4), ALU.mult).then_inc(w_scaled, 1)
            for n in range(NC):
                dve.wait_ge(row_ready, n + 1)
                dve.tensor_tensor(rows[:, n * CH:(n + 1) * CH], k.ps[n % 2][0:4, 0:CH], k.rstd[0:4, n * CH:(n + 1) * CH],
                                  ALU.mult).then_inc(row_taken, 1)
            dve.wait_ge(a_step, 3)
            dve.tensor_scalar(rows[:, :], rows[:, :], k.small[0:4, 2:3], 0.0, ALU.add, ALU.min).then_inc(d_step, 1)
            dve.wait_ge(d_step, 1)
            dve.tensor_tensor(rows[:, :], rows[:, :], tmp[:, :], ALU.subtract).then_inc(d_step, 1)
            dve.wait_ge(d_step, 2)
            dve.tensor_tensor_scan(tmp[:, 0:T], one[:, :], rows[:, 0:T], 0.0, ALU.mult, ALU.add).then_inc(d_step, 1)
            dve.wait_ge(d_step, 3)
            dve.tensor_scalar(tmp[:, 0:T], tmp[:, 0:T], -1.0, None, ALU.mult).then_inc(d_step, 1)
            dve.wait_ge(turned, 1)
            dve.tensor_copy(k.logf_cols.rearrange("p t h -> p (t h)"), k.ps[2][:, 0:68]).then_inc(cols_ready, 1)

        @block.scalar
        def _(act):
            act.wait_ge(row_taken, NC)
            act.activation(tmp[:, :], rows[:, :], ACT.Abs, bias=k.small[0:4, 2:3]).then_inc(a_step, 1)
            act.wait_ge(a_step, 1)
            act.activation(tmp[:, :], tmp[:, :], ACT.Exp, scale=-1.0).then_inc(a_step, 1)
            act.wait_ge(a_step, 2)
            act.activation(tmp[:, :], tmp[:, :], ACT.Ln, bias=k.one[0:4, :]).then_inc(a_step, 1)

        @block.tensor
        def _(pe):
            pe.wait_ge(w_scaled, 1)
            for n in range(NC):
                if n >= 2:
                    pe.wait_ge(row_taken, n - 1)
                for j in range(KT):
                    last = pe.matmul(k.ps[n % 2][0:4, 0:CH], w[:, j, :], k.xT[:, j, n * CH:(n + 1) * CH],
                                     start=(j == 0), stop=(j == KT - 1))
                last.then_inc(row_ready, 1)
            pe.wait_ge(d_step, 2)
            pe.matmul(k.ps[2][:, 0:68], k.c("ones"), k.zero[:, 0:68], start=True, stop=True)
            for t in range(TILES + 1):
                m = P if t < TILES else TS
                last = pe.transpose(k.ps[2][0:m, 4 * t:4 * t + 4], rows[:, t * P:t * P + m], k.c("ident")[0:4, 0:4])
            last.then_inc(turned, 1)
    clear(nc, [w_loaded, w_scaled, row_ready, row_taken, a_step, d_step, turned, cols_ready, stored])


def head_attention(nc, k, io, h, branch):
    with ExitStack() as c:
        sbuf = lambda n, s: c.enter_context(nc.sbuf_tensor(f"{n}{branch}", s, F32))[:]
        sem = lambda n: c.enter_context(nc.semaphore(f"{n}_{branch}"))
        fox = branch == "C"
        ktok, vtok = sbuf("ktok", [P, TILES + 1, P]), sbuf("vtok", [P, TILES + 1, P])
        bias = sbuf("bias", [P, T])
        sc = sbuf("sc", [P, 2, T])
        wt = sbuf("wt", [P, 2, G * P])
        otok = sbuf("otok", [P, 2, P])
        qgain = sbuf("qgain", [P, 1])
        cmax, stat = sbuf("cmax", [P, 3, G]), sbuf("stat", [P, 3, 3])
        sq = sc[:, 0:2, :].rearrange("p a n -> p (a n)")[:, 0:NT]
        O = k.qd
        squares = [sq, k.qd]
        Q = k.qkvz
        slots = [sc[:, 0, :], sc[:, 1, :], Q[:, 2, 0:T]]
        keep = k.foxs if fox else k.wins
        gq, gk = (k.vec[:, 1:2], k.vec[:, 2:3]) if fox else (k.vec[:, 3:4], k.vec[:, 4:5])
        w_sems, p_sync, p_pool, p_tensor, p_vector = project_head(
            nc, k, io, c, branch, h, lambda m, n: [(Q[:, m, n * CH:(n + 1) * CH], 0, CH)])
        names = ["bias_loaded", "sq_done", "ss_done", "ln_done", "root_done", "normed", "gate_done", "kv_turned", "kv_kept",
                 "scores_made", "scores_kept", "max_ready", "exp_done", "wt_made", "wt_kept_v", "wt_kept_s", "o_made",
                 "recip_ready", "otok_ready", "o_turned", "o_done", "stored", "order", "gain_ready"]
        s = {n: sem(n) for n in names}
        block = c.enter_context(nc.Block())
        kout, vout, ks, vs = ((io.out_fox_k_prompt[0, 0], io.out_fox_v_prompt[0, 0],
                               io.out_fox_k_sample.rearrange("b o l h d -> (b o l) h d"), io.out_fox_v_sample.rearrange("b o l h d -> (b o l) h d"))
                              if fox else (io.out_win_k_prompt[0, 0], io.out_win_v_prompt[0, 0], None, None))
        n_chunks = [i // G + 1 for i in range(TILES)]
        first = [sum(n_chunks[:i]) for i in range(TILES)]
        in_chunk = lambda i, ch: min(G, i + 1 - G * ch)
        kept_by = lambda i, ch: ("wt_kept_v", sum(min(n, 2) for n in n_chunks[:i]) + ch + 1) if ch < 2 else \
            ("wt_kept_s", sum(max(n - 2, 0) for n in n_chunks[:i]) + ch - 1)
        steps = lambda i: max(n_chunks[i] + 1, n_chunks[i + 2] if i + 2 < TILES else 0, 3)

        @block.sync
        def _(sp):
            src = io.scr_f[bass.ds(h, 1), :].broadcast_to([P, T]) if fox else io.c_window[bass.ds(h, 1)].rearrange("o p n -> (o p) n")
            sp.dma_start(bias, src).then_inc(s["bias_loaded"], 16)
            sp.wait_ge(w_sems[2], 4 * NC)
            p_sync(sp)
            sp.wait_ge(s["kv_kept"], 10)
            n = 2
            for dst, ap in ((kout, ktok), (vout, vtok)):
                sp.dma_start(dst[:, bass.ds(h, 1), :].rearrange("(t p) o d -> p t (o d)", p=P), ap[:, 0:TILES, :]).then_inc(s["stored"], 16)
            if fox:
                for dst, ap in ((ks, ktok), (vs, vtok)):
                    sp.dma_start(dst[:, bass.ds(h, 1), :].rearrange("t o d -> t (o d)"), ap[0:TS, TILES, :]).then_inc(s["stored"], 16)
            else:
                for dst, ap in ((io.out_win_k_sample, ktok), (io.out_win_v_sample, vtok)):
                    for b in range(B):
                        sp.dma_start(dst[0, b, WBUF - L:WBUF, bass.ds(h, 1), :].rearrange("l o d -> l (o d)"), ap[b * L:(b + 1) * L, TILES, :]).then_inc(s["stored"], 16)
            for a, b in ((0, TILES - 2), (TILES - 2, TILES)):
                sp.wait_ge(s["o_done"], b)
                sp.dma_start(io.scr_o[bass.ds(h + (0 if fox else H), 1)].rearrange("o p n -> (o p) n")[:, a * P:b * P],
                             O[:, a * P:b * P]).then_inc(s["stored"], 16)
            sp.wait_ge(s["stored"], 16 * (2 + (2 if fox else 2 * B) + 2))

        @block.gpsimd
        def _(pool):
            p_pool(pool)

        @block.tensor
        def _(pe):
            def turn_kv(g):
                ts = range(4 * g, min(4 * g + 4, TILES + 1))
                if g == 0:
                    pe.wait_ge(s["normed"], 2)
                    pe.wait_ge(w_sems[3], 3 * NC)
                for which in range(2):
                    at = 2 * g + which
                    if at >= 2:
                        pe.wait_ge(s["kv_kept"], at - 1)
                    for t in ts:
                        w = P if t < TILES else TS
                        last = pe.transpose(k.ps[5 + which][0:w, (t % 4) * P:(t % 4 + 1) * P], Q[:, 1 + which, t * P:t * P + w], k.c("ident"))
                    last.then_inc(s["kv_turned"], 1)

            for at in range(PROJ):
                p_tensor(pe, at)
                if at in (NC + 1, 2 * NC + 1):
                    m = at // NC - 1
                    pe.wait_ge(s["sq_done"], m + 1)
                    if m:
                        pe.wait_ge(s["ln_done"], NC)
                    feature_sums(pe, k, squares[m]).then_inc(s["ss_done"], 1)
                if at >= 3 * NC:
                    turn_kv(at - 3 * NC)
            pe.wait_ge(w_sems[3], PROJ)
            pe.wait_ge(s["kv_kept"], 10)

            def scores(i, ch):
                if i and ch < n_chunks[i - 1]:
                    pe.wait_ge(s["scores_kept"], first[i - 1] + ch + 1)
                j, n = G * ch, in_chunk(i, ch) * P
                diag = fox and ch == n_chunks[i] - 1
                last = pe.matmul(k.ps[ch][:, 0:n], Q[:, 0, i * P:(i + 1) * P], Q[:, 1, j * P:j * P + n], start=True, stop=not diag)
                if diag:
                    last = pe.matmul(k.ps[ch][:, n - P:n], k.c("ident"), k.c("causal_bias"), start=False, stop=True)
                last.then_inc(s["scores_made"], 1)

            def turn(i, ch):
                at = first[i] + ch
                if at >= 2:
                    i2 = i if ch >= 2 else max(x for x in range(i + 1) if first[x] <= at - 2)
                    name, count = kept_by(i2, at - 2 - first[i2])
                    pe.wait_ge(s[name], count)
                for jj in range(in_chunk(i, ch)):
                    j = G * ch + jj
                    last = pe.transpose(k.ps[4 + at % 2][:, jj * P:(jj + 1) * P], slots[i % 3][:, j * P:(j + 1) * P], k.c("ident"))
                last.then_inc(s["wt_made"], 1)

            def weigh(i, ch):
                name, count = kept_by(i, ch)
                pe.wait_ge(s[name], count)
                if ch == 0 and i >= 2:
                    pe.wait_ge(s["otok_ready"], i - 1)
                for jj in range(in_chunk(i, ch)):
                    j = G * ch + jj
                    last = pe.matmul(k.ps[6 + i % 2][:, 0:P], wt[:, (first[i] + ch) % 2, jj * P:(jj + 1) * P], vtok[:, j, :],
                                     start=(j == 0), stop=(j == i))
                if ch == n_chunks[i] - 1:
                    last.then_inc(s["o_made"], 1)

            def turn_output(i):
                pe.wait_ge(s["otok_ready"], i + 1)
                if i >= 2:
                    pe.wait_ge(s["o_done"], i - 1)
                pe.transpose(k.ps[6 + i % 2][:, P:2 * P], otok[:, i % 2, :], k.c("ident")).then_inc(s["o_turned"], 1)

            for i in range(2):
                scores(i, 0)
            for i in range(TILES):
                for step in range(steps(i)):
                    if i + 2 < TILES and step < n_chunks[i + 2]:
                        scores(i + 2, step)
                    if step == 0:
                        pe.wait_ge(s["exp_done"], i + 1)
                    if step < n_chunks[i]:
                        turn(i, step)
                    if 1 <= step <= n_chunks[i]:
                        weigh(i, step - 1)
                    if step == 1 and i:
                        turn_output(i - 1)
            turn_output(TILES - 1)

        @block.vector
        def _(dve):
            d = Order(dve, s["order"])
            dve.tensor_scalar(qgain, gq, SCALE, None, ALU.mult).then_inc(s["gain_ready"], 1)
            dve.wait_ge(s["gain_ready"], 1)
            for at in range(PROJ):
                p_vector(dve, at)
                if at in (NC + 4, 2 * NC + 4):
                    m = at // NC - 1
                    dve.wait_ge(s["root_done"], m + 1)
                    dve.scalar_tensor_tensor(Q[:, m, :], Q[:, m, :], qgain if m == 0 else gk, squares[m], ALU.mult, ALU.mult).then_inc(s["normed"], 1)
                if at >= 3 * NC:
                    g = at - 3 * NC
                    n = 4 if g < 4 else 1
                    w = P if g < 4 else TS
                    for which, dst in ((0, ktok), (1, vtok)):
                        dve.wait_ge(s["kv_turned"], 2 * g + which + 1)
                        dve.tensor_copy(dst[0:w, 4 * g:4 * g + n, :], k.ps[5 + which][0:w, 0:n * P].rearrange("p (t d) -> p t d", t=n)).then_inc(s["kv_kept"], 1)
            dve.wait_ge(s["normed"], 2)
            dve.wait_ge(s["gate_done"], NC)
            dve.wait_ge(s["kv_kept"], 10)
            for which, src in ((0, Q[:, 0, T:NT]), (1, Q[:, 1, T:NT]), (2, Q[:, 3, T:NT])):
                dve.tensor_copy(keep[:, which, bass.ds(h, 1), :].rearrange("p o t -> p (o t)"), src)
            dve.tensor_copy((k.foxv if fox else k.winv)[:, bass.ds(h, 1), :].rearrange("t o d -> t (o d)"), vtok[0:TS, TILES, :])
            dve.wait_ge(s["bias_loaded"], 16)

            def soften(i, ch):
                j, n = G * ch, in_chunk(i, ch) * P
                dve.wait_ge(s["scores_made"], first[i] + ch + 1)
                if i >= 3 and ch == 0:
                    dve.wait_ge(s["o_made"], i - 2)
                at = j * P + (0 if fox else T - (i + 1) * P)
                dve.tensor_tensor_reduce(slots[i % 3][:, j * P:j * P + n], k.ps[ch][:, 0:n], bias[:, at:at + n], 1.0, -3e38,
                                         ALU.add, ALU.max, cmax[:, i % 3, ch:ch + 1]).then_inc(s["scores_kept"], 1)

            def maximum(i):
                dve.wait_ge(s["scores_kept"], first[i] + n_chunks[i])
                d.after(dve.tensor_reduce(stat[:, i % 3, 0:1], cmax[:, i % 3, 0:n_chunks[i]], X, ALU.max))
                dve.tensor_scalar(stat[:, i % 3, 0:1], stat[:, i % 3, 0:1], -1.0, None, ALU.mult).then_inc(s["max_ready"], 1)

            for i in range(2):
                soften(i, 0)
                maximum(i)
            for i in range(TILES + 1):
                for step in range(steps(i) if i < TILES else 3):
                    if i + 2 < TILES and step < n_chunks[i + 2]:
                        soften(i + 2, step)
                    if i < TILES and step < min(2, n_chunks[i]):
                        at = first[i] + step
                        n = in_chunk(i, step) * P
                        dve.wait_ge(s["wt_made"], at + 1)
                        dve.tensor_copy(wt[:, at % 2, 0:n], k.ps[4 + at % 2][:, 0:n]).then_inc(s["wt_kept_v"], 1)
                    if step == 0 and i:
                        dve.wait_ge(s["exp_done"], i)
                        dve.reciprocal(stat[:, (i - 1) % 3, 2:3], stat[:, (i - 1) % 3, 1:2]).then_inc(s["recip_ready"], 1)
                        dve.wait_ge(s["recip_ready"], i)
                        dve.wait_ge(s["o_made"], i)
                        dve.tensor_scalar(otok[:, (i - 1) % 2, :], k.ps[6 + (i - 1) % 2][:, 0:P], stat[:, (i - 1) % 3, 2:3], None,
                                          ALU.mult).then_inc(s["otok_ready"], 1)
                    if step == 2 and i:
                        dve.wait_ge(s["o_turned"], i)
                        dve.tensor_tensor(O[:, (i - 1) * P:i * P], k.ps[6 + (i - 1) % 2][:, P:2 * P], Q[:, 3, (i - 1) * P:i * P],
                                          ALU.mult).then_inc(s["o_done"], 1)
                if i + 2 < TILES:
                    maximum(i + 2)

        @block.scalar
        def _(act):
            for m in range(2):
                act.wait_ge(w_sems[3], (m + 1) * NC)
                act.activation(squares[m], Q[:, m, :], ACT.Square).then_inc(s["sq_done"], 1)
                act.wait_ge(s["ss_done"], m + 1)
                for n in range(NC):
                    act.activation(squares[m][:, n * CH:(n + 1) * CH], k.ps[SUMS + n][:, 0:CH], ACT.Ln, bias=k.eps, scale=1.0 / P).then_inc(s["ln_done"], 1)
                act.wait_ge(s["ln_done"], (m + 1) * NC)
                act.activation(squares[m], squares[m], ACT.Exp, scale=-0.5).then_inc(s["root_done"], 1)
            silu_gate(act, k, w_sems[3], s["gate_done"])

            def soft(i):
                n = (i + 1) * P
                act.wait_ge(s["max_ready"], i + 1)
                act.activation(slots[i % 3][:, 0:n], slots[i % 3][:, 0:n], ACT.Exp, bias=stat[:, i % 3, 0:1],
                               accum_out=stat[:, i % 3, 1:2]).then_inc(s["exp_done"], 1)

            soft(0)
            for i in range(TILES):
                if i + 1 < TILES:
                    soft(i + 1)
                for ch in range(2, n_chunks[i]):
                    at = first[i] + ch
                    n = in_chunk(i, ch) * P
                    act.wait_ge(s["wt_made"], at + 1)
                    act.copy(wt[:, at % 2, 0:n], k.ps[4 + at % 2][:, 0:n]).then_inc(s["wt_kept_s"], 1)
    clear(nc, w_sems + list(s.values()))


def sample_new_scores(nc, k, io):
    with ExitStack() as c:
        sem = lambda n: c.enter_context(nc.semaphore(n))
        prefix, dot, negated, centred = sem("new_prefix"), sem("new_dot"), sem("new_negated"), sem("new_centred")
        col = c.enter_context(nc.sbuf_tensor("newcol", [TS, H], F32))[:]
        block = c.enter_context(nc.Block())

        @block.tensor
        def _(pe):
            pe.matmul(k.ps[0][0:TS, 0:H], k.c("s_prefix")[0:TS, :], k.logf_cols[0:TS, TILES, :], start=True, stop=True).then_inc(prefix, 1)
            for f, keep in enumerate((k.foxs, k.wins)):
                for hh in range(H):
                    last = pe.matmul(k.ps[1 + f][0:TS, hh * TS:(hh + 1) * TS], keep[:, 1, hh, :], keep[:, 0, hh, :], start=True, stop=True)
                last.then_inc(dot, 1)

        @block.vector
        def _(dve):
            dve.memset(k.sc_all[:, :, :], -BIG)
            dve.memset(k.qpad[:, :, :, :], 0.0)
            dve.wait_ge(prefix, 1)
            dve.tensor_scalar(col, k.ps[0][0:TS, 0:H], -1.0, None, ALU.mult).then_inc(negated, 1)
            dve.wait_ge(dot, 2)
            dve.wait_ge(negated, 1)
            dve.tensor_tensor(k.snew[:, 0], k.ps[1][0:TS, 0:P].rearrange("p (h t) -> p h t", h=H), repeat(col, 2, TS), ALU.add).then_inc(centred, 1)
            dve.wait_ge(centred, 1)
            dve.tensor_tensor(k.snew[:, 0], k.snew[:, 0], repeat(k.c("s_bias")[0:TS, :], 1, H), ALU.add)
            dve.tensor_tensor(k.snew[:, 1], k.ps[2][0:TS, 0:P].rearrange("p (h t) -> p h t", h=H),
                              k.c("s_window")[0:TS, :].rearrange("p (h t) -> p h t", h=H), ALU.add)
    clear(nc, [prefix, dot, negated, centred])


RING = 4


def page_of(k, eng, b, p):
    return eng.value_load(k.pages[0:1, bass.ds(b * NPG + p, 1)], min_val=0, max_val=NPHYS - 1)


def load_first_keys(k, io, sp, b, loaded):
    for p in range(RING):
        page = page_of(k, sp, b, p)
        sp.dma_start(k.kring[:, p, :], io.cache_fox_k[bass.ds(page, 1)].rearrange("n o t h d -> (n o t) (h d)")).then_inc(loaded, 16)
    sp.wait_ge(loaded, 16 * RING)


def first_keys(nc, k, io):
    with nc.semaphore("first_keys_loaded") as loaded:
        with nc.Block() as block:
            @block.sync
            def _(sp):
                load_first_keys(k, io, sp, 0, loaded)
        clear(nc, [loaded])


def sample_attention(nc, k, io, b):
    with ExitStack() as c:
        sbuf = lambda n, s: c.enter_context(nc.sbuf_tensor(n, s, F32))[:]
        sem = lambda n: c.enter_context(nc.semaphore(n))
        ITEMS = NPG + WT
        GR = 4 * H
        GROUPS = -(-ITEMS // G)
        FOX_GROUPS = NPG // G
        kring, kt = k.kring, sbuf("kt", [P, 2, H, G * P])
        srow = sbuf("srow", [GR, 2, G * P])
        vwin = sbuf("vwin", [P, WT, HD])
        vslot = [k.big[:, i * HD:(i + 1) * HD] for i in range(28)] + [k.rstd[:, i * HD:(i + 1) * HD] for i in range(4)]
        pr = sbuf("pr", [P, NPG + 1 + WT + 1, GR])
        lfp = sbuf("lfp", [NPG, PAGE * H])
        lft, pre, later, fbias = [sbuf(n, [P, H * NPG]) for n in ("lft", "pre", "later", "fbias")]
        mx, sm, mrow, mdiag, rs = sbuf("mx", [P, 2, GR]), sbuf("sm", [P, 2, GR]), sbuf("mrow", [GR, 2]), sbuf("mdiag", [GR, 2, GR]), sbuf("rs", [P, 2, GR])
        ov, res = srow, sbuf("res", [P, 2, GR])
        k_loaded = [sem(f"k_loaded{i}") for i in range(RING)]
        VG = 8
        v_loaded = [sem(f"v_loaded{i}") for i in range(NPG // VG)]
        names = ["vw_loaded", "lf_loaded", "lf_loaded_s", "k_turned", "kt_kept_v", "kt_kept_s", "rows_made", "rows_kept",
                 "scores_turned", "q_ready", "lf_turned", "later_ready", "fbias_made", "max_cols", "max_turned",
                 "max_diag", "max_made", "shifted", "exp_done", "sums_ready", "sums_made", "pv_made", "ov_ready", "ot_made",
                 "next_keys", "order"]
        s = {n: sem(n) for n in names}
        block = c.enter_context(nc.Block())
        sc = k.sc_all
        kf, vf = io.cache_fox_k.rearrange("n o t h d -> n t (o h d)"), io.cache_fox_v.rearrange("n o t h d -> n t (o h d)")
        lf = io.cache_fox_logf.rearrange("n o t h -> n (o t h)")
        kw, vw = (a[0].rearrange("b r h d -> b r (h d)") for a in (io.cache_win_k, io.cache_win_v))
        by_act = lambda p: p % 2 == 1 or p >= 36
        kept_by = lambda p: ("kt_kept_s" if by_act(p) else "kt_kept_v", sum(by_act(x) == by_act(p) for x in range(p + 1)))
        in_group = lambda g: min(G, ITEMS - G * g)
        parts = (slice(0, NPG + 1), slice(NPG + 1, NPG + 2 + WT))
        scores_at = (k.ps[4], k.ps[5][:, 0:WT * GR])
        small = (k.ps[6], k.ps[7])

        def window_tile(src, i):
            if i < 3:
                return src[bass.ds(b, 1), 512 * i:512 * (i + 1), :].rearrange("o (g r) c -> (o g) r c", r=16)[:, 0:4, :]
            return src[bass.ds(b, 1), 1536 + P * (i - 3):1536 + P * (i - 2), :].rearrange("o r c -> (o r) c")

        @block.sync
        def _(sp):
            for p in range(ITEMS):
                if p >= RING:
                    sp.wait_ge(s["k_turned"], p - RING + 1)
                if p < NPG:
                    page = page_of(k, sp, b, p)
                    if p >= RING:
                        sp.dma_start(kring[:, p % RING, :], kf[bass.ds(page, 1)].rearrange("o t c -> (o t) c")).then_inc(k_loaded[p % RING], 16)
                    if p % 2 == 0:
                        sp.dma_start(lfp[p:p + 1, :], lf[bass.ds(page, 1), :]).then_inc(s["lf_loaded"], 16)
                else:
                    sp.dma_start(kring[:, p % RING, :], window_tile(kw, p - NPG)).then_inc(k_loaded[p % RING], 16)
            sp.wait_ge(s["k_turned"], ITEMS)
            load_first_keys(k, io, sp, (b + 1) % B, s["next_keys"])

        @block.tensor
        def _(pe):
            def turn_keys(p):
                if p >= RING:
                    pe.wait_ge(k_loaded[p % RING], 16 * (p // RING))
                if p >= 2:
                    name, count = kept_by(p - 2)
                    pe.wait_ge(s[name], count)
                for hh in range(H):
                    last = pe.transpose(k.ps[p % 2][:, hh * P:(hh + 1) * P], kring[:, p % RING, hh * P:(hh + 1) * P], k.c("ident"))
                last.then_inc(s["k_turned"], 1)

            def score(g):
                for p in range(G * g, G * g + in_group(g)):
                    name, count = kept_by(p)
                    pe.wait_ge(s[name], count)
                if g == 0:
                    pe.wait_ge(s["q_ready"], 1)
                if g >= 2:
                    pe.wait_ge(s["rows_kept"], g - 1)
                n = in_group(g) * P
                for hh in range(H):
                    last = pe.matmul(k.ps[2 + g % 2][0:GR, 0:n], k.qpad[:, int(g >= FOX_GROUPS), hh, :], kt[:, g % 2, hh, 0:n],
                                     start=(hh == 0), stop=(hh == H - 1))
                last.then_inc(s["rows_made"], 1)

            def turn_scores(g):
                pe.wait_ge(s["rows_kept"], g + 1)
                f = int(g >= FOX_GROUPS)
                for i in range(in_group(g)):
                    at = GR * (G * g + i - NPG * f)
                    last = pe.transpose(scores_at[f][:, at:at + GR], srow[:, g % 2, i * P:(i + 1) * P], k.c("ident")[0:GR, 0:GR])
                last.then_inc(s["scores_turned"], 1)

            def turn_maxima(f):
                pe.wait_ge(s["max_cols"], f + 1)
                pe.transpose(small[f][0:GR, 0:P], mx[:, f, :], k.c("ident")).then_inc(s["max_turned"], 1)

            def spread_maxima(f):
                pe.wait_ge(s["max_diag"], f + 1)
                pe.matmul(small[f][:, P:P + GR], k.c("ones")[0:GR, :], mdiag[:, f, :], start=True, stop=True).then_inc(s["max_made"], 1)

            def output(f):
                pe.wait_ge(s["sums_ready"], f + 1)
                pe.matmul(k.ps[2 + f][:, 0:GR], k.c("ones"), sm[:, f, :], start=True, stop=True).then_inc(s["sums_made"], 1)
                pe.wait_ge(s["ov_ready"], f + 1)
                for hh in range(H):
                    last = pe.matmul(k.ps[4 + f][:, 0:GR], ov[:, f, hh * P:(hh + 1) * P], k.c("ident")[0:GR, 0:GR],
                                     start=(hh == 0), stop=(hh == H - 1))
                last.then_inc(s["ot_made"], 1)

            for p in range(ITEMS):
                turn_keys(p)
                if p % G == 1 and p > G:
                    score(p // G - 1)
                if p % G == 3 and p > G:
                    turn_scores(p // G - 1)
                if p == NPG + 2:
                    pe.wait_ge(s["lf_loaded"], 16 * NPG // 2)
                    pe.wait_ge(s["lf_loaded_s"], 16 * NPG // 2)
                    for hh in range(H):
                        last = pe.transpose(k.ps[6][:, hh * NPG:(hh + 1) * NPG], lfp.rearrange("p (t h) -> p h t", h=H)[:, hh, :], k.c("ident")[0:NPG, 0:NPG])
                    last.then_inc(s["lf_turned"], 1)
                if p == NPG + 4:
                    pe.wait_ge(s["later_ready"], 1)
                    pe.matmul(k.ps[7][:, 0:P], k.c("later"), lft, start=True, stop=False)
                    pe.matmul(k.ps[7][:, 0:P], k.c("ones"), later, start=False, stop=True).then_inc(s["fbias_made"], 1)
            score(GROUPS - 1)
            turn_scores(GROUPS - 2)
            turn_maxima(0)
            turn_scores(GROUPS - 1)
            spread_maxima(0)
            pe.wait_ge(s["exp_done"], 1)
            for p in range(NPG):
                if p % VG == 0:
                    pe.wait_ge(v_loaded[p // VG], 16 * VG)
                pe.matmul(k.ps[0][0:GR, :], pr[:, p, :], vslot[p], start=(p == 0), stop=False)
                if p == 6:
                    turn_maxima(1)
                if p == 12:
                    spread_maxima(1)
            pe.matmul(k.ps[0][0:GR, :], pr[0:TS, NPG, :], k.foxv.rearrange("t h d -> t (h d)"), start=False, stop=True).then_inc(s["pv_made"], 1)
            pe.wait_ge(s["exp_done"], 2)
            pe.wait_ge(s["vw_loaded"], 16 * WT)
            for i in range(WT):
                pe.matmul(k.ps[1][0:GR, :], pr[:, NPG + 1 + i, :], vwin[:, i, :], start=(i == 0), stop=False)
            pe.matmul(k.ps[1][0:GR, :], pr[0:TS, NPG + 1 + WT, :], k.winv.rearrange("t h d -> t (h d)"), start=False, stop=True).then_inc(s["pv_made"], 1)
            output(0)
            output(1)

        def take_keys(eng, copy, p, kept):
            g = p // G
            eng.wait_ge(s["k_turned"], p + 1)
            if g >= 2 and p % G < 2:
                eng.wait_ge(s["rows_made"], g - 1)
            copy(kt[:, g % 2, :, (p % G) * P:(p % G + 1) * P], k.ps[p % 2].rearrange("p (h t) -> p h t", h=H)).then_inc(s[kept], 1)

        @block.vector
        def _(dve):
            d = Order(dve, s["order"])
            for f, keep in enumerate((k.foxs, k.wins)):
                for hh in range(H):
                    last = dve.tensor_copy(k.qpad[:, f, hh, L * hh:L * hh + L], keep[:, 0, hh, bass.ds(b * L, L)])
            last.then_inc(s["q_ready"], 1)
            for f, blk in ((0, NPG), (1, NPG + 1 + WT)):
                dve.tensor_copy(sc[0:TS, blk, :].rearrange("p (h q) -> p h q", h=H), k.snew[:, f, :, bass.ds(b * L, L)])
            for p in range(ITEMS):
                if not by_act(p):
                    take_keys(dve, dve.tensor_copy, p, "kt_kept_v")
            dve.wait_ge(s["lf_turned"], 1)
            d.after(dve.tensor_copy(lft, k.ps[6][:, 0:P]))
            d.after(dve.tensor_tensor_scan(pre, k.c("page_reset"), lft, 0.0, ALU.mult, ALU.add))
            p3 = pre.rearrange("p (h n) -> p h n", h=H)
            dve.tensor_tensor(later.rearrange("p (h n) -> p h n", h=H), repeat(p3[:, :, NPG - 1], 2, NPG), p3, ALU.subtract).then_inc(s["later_ready"], 1)
            dve.wait_ge(s["fbias_made"], 1)
            d.after(dve.tensor_copy(fbias, k.ps[7][:, 0:P]))

            def maxima(f):
                dve.tensor_reduce(mx[:, f, :], sc[:, parts[f], :].rearrange("p n g -> p g n"), X, ALU.max).then_inc(s["max_cols"], 1)

            def shift(f):
                dve.wait_ge(s["max_turned"], f + 1)
                d.after(dve.tensor_reduce(mrow[:, f:f + 1], small[f][0:GR, 0:P], X, ALU.max))
                dve.tensor_scalar(mdiag[:, f, :], k.c("ident")[0:GR, 0:GR], mrow[:, f:f + 1], None, ALU.mult).then_inc(s["max_diag"], 1)
                dve.wait_ge(s["max_made"], f + 1)
                n = parts[f].stop - parts[f].start
                dve.tensor_tensor(pr[:, parts[f], :], sc[:, parts[f], :], repeat(small[f][:, P:P + GR], 1, n), ALU.subtract).then_inc(s["shifted"], 1)

            def sums(f):
                dve.wait_ge(s["exp_done"], f + 1)
                dve.tensor_reduce(sm[:, f, :], pr[:, parts[f], :].rearrange("p n g -> p g n"), X, ALU.add).then_inc(s["sums_ready"], 1)

            dve.wait_ge(s["scores_turned"], FOX_GROUPS)
            d.after(dve.tensor_tensor(sc[:, 0:NPG, :].rearrange("p n (h q) -> p n h q", h=H), scores_at[0].rearrange("p (n h q) -> p n h q", n=NPG, h=H),
                                      repeat(fbias.rearrange("p (h n) -> p n h", h=H), 3, L), ALU.add))
            maxima(0)
            shift(0)
            dve.wait_ge(s["scores_turned"], GROUPS)
            d.after(dve.tensor_tensor(sc[:, NPG + 1:NPG + 1 + WT, :], scores_at[1].rearrange("p (n g) -> p n g", n=WT),
                                      k.c("window_past").rearrange("p (n g) -> p n g", n=WT), ALU.add))
            maxima(1)
            shift(1)
            sums(0)
            sums(1)
            for f in range(2):
                dve.wait_ge(s["pv_made"], f + 1)
                dve.tensor_tensor(ov[:, f, :], k.ps[f][0:GR, :], k.c("head_cols")[0:GR, :], ALU.mult).then_inc(s["ov_ready"], 1)
            for f, keep in enumerate((k.foxs, k.wins)):
                dve.wait_ge(s["sums_made"], f + 1)
                d.after(dve.reciprocal(rs[:, f, :], k.ps[2 + f][:, 0:GR]))
                dve.wait_ge(s["ot_made"], f + 1)
                d.after(dve.tensor_tensor(res[:, f, :], k.ps[4 + f][:, 0:GR], rs[:, f, :], ALU.mult))
                dve.tensor_tensor(k.osample[:, f * H:(f + 1) * H, bass.ds(b * L, L)], res[:, f, :].rearrange("p (h q) -> p h q", h=H),
                                  keep[:, 2, :, bass.ds(b * L, L)], ALU.mult)

        @block.scalar
        def _(act):
            def take_scores(g):
                act.wait_ge(s["rows_made"], g + 1)
                if g >= 2:
                    act.wait_ge(s["scores_turned"], g - 1)
                n = in_group(g) * P
                act.copy(srow[:, g % 2, 0:n], k.ps[2 + g % 2][0:GR, 0:n]).then_inc(s["rows_kept"], 1)

            def values(p):
                if p < NPG:
                    page = page_of(k, act, b, p)
                    act.dma_start(vslot[p], vf[bass.ds(page, 1)].rearrange("o t c -> (o t) c")).then_inc(v_loaded[p // VG], 16)
                    if p % 2:
                        act.dma_start(lfp[p:p + 1, :], lf[bass.ds(page, 1), :]).then_inc(s["lf_loaded_s"], 16)
                else:
                    act.dma_start(vwin[:, p - NPG, :], window_tile(vw, p - NPG)).then_inc(s["vw_loaded"], 16)

            for p in range(ITEMS):
                if by_act(p):
                    take_keys(act, act.copy, p, "kt_kept_s")
                if p >= 2:
                    values(p - 2)
                if p % G == 1 and p > G:
                    take_scores(p // G - 1)
            for p in range(ITEMS - 2, ITEMS):
                values(p)
            take_scores(GROUPS - 1)
            for f in range(2):
                act.wait_ge(s["shifted"], f + 1)
                act.activation(pr[:, parts[f], :], pr[:, parts[f], :], ACT.Exp).then_inc(s["exp_done"], 1)
    clear(nc, k_loaded + v_loaded + list(s.values()))


def store_sample_heads(nc, k, io):
    with nc.semaphore("sample_stored") as stored:
        with nc.Block() as block:
            @block.sync
            def _(sp):
                sp.dma_start(io.scr_o[:, :, T:NT].rearrange("k p n -> p k n"), k.osample).then_inc(stored, 16)
                sp.wait_ge(stored, 16)
        clear(nc, [stored])


def write_tokens(nc, k, io):
    with ExitStack() as c:
        sem = lambda n: c.enter_context(nc.semaphore(n))
        SLOTS = 4
        turned, left, right, stored = sem("y_turned"), sem("y_left"), sem("y_right"), [sem(f"y_stored{i}") for i in range(SLOTS)]
        row = c.enter_context(nc.sbuf_tensor("yrow", [P, SLOTS, D_MODEL], F32))
        block = c.enter_context(nc.Block())

        @block.tensor
        def _(pe):
            for t in range(TILES + 1):
                n = P if t < TILES else TS
                for half, taken in ((0, left), (1, right)):
                    if t >= 2:
                        pe.wait_ge(taken, t - 1)
                    for j in range(4):
                        last = pe.transpose(k.ps[half + 2 * (t % 2)][0:n, j * P:(j + 1) * P], k.xT[:, 4 * half + j, t * P:t * P + n], k.c("ident"))
                    last.then_inc(turned, 1)

        @block.vector
        def _(dve):
            for t in range(TILES + 1):
                n = P if t < TILES else TS
                dve.wait_ge(turned, 2 * t + 1)
                if t >= SLOTS:
                    dve.wait_ge(stored[t % SLOTS], 16 * (t // SLOTS))
                dve.tensor_copy(row[0:n, t % SLOTS, 0:512], k.ps[2 * (t % 2)][0:n, :]).then_inc(left, 1)

        @block.scalar
        def _(act):
            for t in range(TILES + 1):
                n = P if t < TILES else TS
                act.wait_ge(turned, 2 * t + 2)
                if t >= SLOTS:
                    act.wait_ge(stored[t % SLOTS], 16 * (t // SLOTS))
                act.copy(row[0:n, t % SLOTS, 512:1024], k.ps[1 + 2 * (t % 2)][0:n, :]).then_inc(right, 1)

        @block.sync
        def _(sp):
            for t in range(TILES + 1):
                n = P if t < TILES else TS
                sp.wait_ge(left, t + 1)
                sp.wait_ge(right, t + 1)
                dst = io.out_y_prompt[0, t * P:t * P + n, :] if t < TILES else io.out_y_sample.rearrange("b l d -> (b l) d")
                sp.dma_start(dst, row[0:n, t % SLOTS, :]).then_inc(stored[t % SLOTS], 16)
            for i in range(SLOTS):
                sp.wait_ge(stored[i], 16 * len(range(i, TILES + 1, SLOTS)))


def build(nc, io, const_names, stop=99):
    with ExitStack() as c:
        sb = lambda n, s, dt=F32: c.enter_context(nc.sbuf_tensor(n, s, dt))[:]
        k = Chip()
        width = io.c_pack.shape[1]
        k.xT, k.rstd = sb("xT", [P, KT, NT]), sb("rstd", [P, NT])
        k.pack = sb("pack", [P, width])
        k.c = lambda n: k.pack[:, const_names[n][0]:const_names[n][0] + const_names[n][1]]
        k.big = sb("big", [P, 4 * NT + KT * 4 * P + NT])
        k.qkvz = k.big[:, 0:4 * NT].rearrange("p (m n) -> p m n", m=4)
        k.w = k.big[:, 4 * NT:4 * NT + KT * 4 * P].rearrange("p (k n) -> p k n", k=KT)
        k.qd = k.big[:, 4 * NT + KT * 4 * P:]
        k.conv_cols, k.cw_head = sb("conv_cols", [P, 12, 28]), sb("cw_head", [P, 3, 4])
        k.gate_cols, k.logf_cols = sb("gate_cols", [P, 2, H, TILES + 1]), sb("logf_cols", [P, TILES + 1, H])
        k.g_even, k.g_odd, k.b_norm = sb("g_even", [P, KT]), sb("g_odd", [P, KT]), sb("b_norm", [P, H])
        k.vec, k.small, k.pages = sb("vec", [P, 5]), sb("small", [36, 4]), sb("pages", [1, B * NPG], I32)
        k.eps, k.one, k.zero = sb("eps", [P, 1]), sb("one", [P, 1]), sb("zero", [P, 324])
        k.ps4 = c.enter_context(nc.psum_tensor("ps0123", [P, 4 * 512], F32))[:]
        k.ps = [k.ps4[:, i * 512:(i + 1) * 512] for i in range(4)]
        k.ps += [c.enter_context(nc.psum_tensor(f"ps{i}", [P, 512], F32))[:] for i in range(4, 8)]
        with nc.semaphore("windows_shifted") as windows_shifted:
            k.windows_shifted = windows_shifted
            with nc.Block() as block:
                @block.vector
                def _(dve):
                    dve.memset(k.eps, EPS)
                    dve.memset(k.one, 1.0)
                    dve.memset(k.zero, 0.0)
                    dve.memset(k.small, 0.0)
            with nc.allow_non_contiguous_dma(reason="a few thousand single words, once"):
                load_tokens(nc, k, io)
            token_norms(nc, k, io)
            row_gates_even(nc, k, io)
            if stop > 1:
                with nc.Fori(0, H) as h:
                    head_A(nc, k, io, h)
            if stop > 2:
                with nc.Fori(0, H) as h:
                    head_B(nc, k, io, h)
            if stop > 3:
                output_projection(nc, k, io, 0)
                row_gates_odd(nc, k, io)
                k.foxs, k.wins = sb("foxs", [P, 3, H, TS]), sb("wins", [P, 3, H, TS])
                k.foxv, k.winv = sb("foxv", [TS, H, P]), sb("winv", [TS, H, P])
                k.snew, k.osample = sb("snew", [TS, 2, H, TS]), sb("osample", [P, 2 * H, TS])
            if stop > 4:
                with nc.Fori(0, H) as h:
                    head_attention(nc, k, io, h, "C")
            if stop > 5:
                with nc.Fori(0, H) as h:
                    head_attention(nc, k, io, h, "D")
            if stop > 6:
                k.qpad = sb("qpad", [P, 2, H, 4 * H])
                k.sc_all = sb("sc_all", [P, NPG + 1 + WT + 1, 4 * H])
                k.kring = sb("kring", [P, RING, HD])
                sample_new_scores(nc, k, io)
                first_keys(nc, k, io)
                with nc.Fori(0, B) as b:
                    sample_attention(nc, k, io, b)
                store_sample_heads(nc, k, io)
                output_projection(nc, k, io, 1)
            if stop > 3:
                write_tokens(nc, k, io)
            with nc.Block() as block:
                @block.sync
                def _(sp):
                    sp.wait_ge(windows_shifted, 16 * 2 * B)


_INS = ["x_prompt", "x_sample", "cache_fox_k", "cache_fox_v", "cache_fox_logf", "page_table", "cache_win_k", "cache_win_v",
        "state_delta", "state_delta_conv", "state_ret", "norm_even", "w_in_even", "conv_w", "a_log", "dt_bias", "a_norm",
        "b_norm", "w_out_even", "norm_odd", "w_in_odd", "c_q_norm", "c_k_norm", "f_bias", "d_q_norm", "d_k_norm", "w_out_odd"]
_OUTS = [("y_prompt", (1, T, D_MODEL)), ("y_sample", (B, L, D_MODEL)),
         ("fox_k_prompt", (1, 1, T, H, P)), ("fox_v_prompt", (1, 1, T, H, P)), ("fox_logf_prompt", (1, 1, T, H)),
         ("fox_k_sample", (B, 1, L, H, P)), ("fox_v_sample", (B, 1, L, H, P)), ("fox_logf_sample", (B, 1, L, H)),
         ("win_k_prompt", (1, 1, T, H, P)), ("win_v_prompt", (1, 1, T, H, P)),
         ("win_k_sample", (1, B, WBUF, H, P)), ("win_v_sample", (1, B, WBUF, H, P)),
         ("delta_prompt", (1, 1, H, P, P)), ("delta_conv_prompt", (1, 1, 3, 3 * HD)),
         ("delta_sample", (1, B, H, P, P)), ("delta_conv_sample", (1, B, 3, 3 * HD)),
         ("ret_prompt", (1, 1, H, P, P)), ("ret_sample", (1, B, H, P, P))]


class Dram:

    def __init__(self, t):
        self.a_log = t["a_log"]
        self.a_norm = t["a_norm"]
        self.b_norm = t["b_norm"]
        self.c_k_norm = t["c_k_norm"]
        self.c_pack = t["c_pack"]
        self.c_q_norm = t["c_q_norm"]
        self.c_reset = t["c_reset"]
        self.c_ret = t["c_ret"]
        self.c_window = t["c_window"]
        self.cache_fox_k = t["cache_fox_k"]
        self.cache_fox_logf = t["cache_fox_logf"]
        self.cache_fox_v = t["cache_fox_v"]
        self.cache_win_k = t["cache_win_k"]
        self.cache_win_v = t["cache_win_v"]
        self.conv_w = t["conv_w"]
        self.d_k_norm = t["d_k_norm"]
        self.d_q_norm = t["d_q_norm"]
        self.dt_bias = t["dt_bias"]
        self.f_bias = t["f_bias"]
        self.norm_even = t["norm_even"]
        self.norm_odd = t["norm_odd"]
        self.out_delta_conv_prompt = t["out_delta_conv_prompt"]
        self.out_delta_conv_sample = t["out_delta_conv_sample"]
        self.out_delta_prompt = t["out_delta_prompt"]
        self.out_delta_sample = t["out_delta_sample"]
        self.out_fox_k_prompt = t["out_fox_k_prompt"]
        self.out_fox_k_sample = t["out_fox_k_sample"]
        self.out_fox_logf_prompt = t["out_fox_logf_prompt"]
        self.out_fox_logf_sample = t["out_fox_logf_sample"]
        self.out_fox_v_prompt = t["out_fox_v_prompt"]
        self.out_fox_v_sample = t["out_fox_v_sample"]
        self.out_ret_prompt = t["out_ret_prompt"]
        self.out_ret_sample = t["out_ret_sample"]
        self.out_win_k_prompt = t["out_win_k_prompt"]
        self.out_win_k_sample = t["out_win_k_sample"]
        self.out_win_v_prompt = t["out_win_v_prompt"]
        self.out_win_v_sample = t["out_win_v_sample"]
        self.out_y_prompt = t["out_y_prompt"]
        self.out_y_sample = t["out_y_sample"]
        self.page_table = t["page_table"]
        self.scr_f = t["scr_f"]
        self.scr_g = t["scr_g"]
        self.scr_o = t["scr_o"]
        self.state_delta = t["state_delta"]
        self.state_delta_conv = t["state_delta_conv"]
        self.state_ret = t["state_ret"]
        self.w_in_even = t["w_in_even"]
        self.w_in_odd = t["w_in_odd"]
        self.w_out_even = t["w_out_even"]
        self.w_out_odd = t["w_out_odd"]
        self.x_prompt = t["x_prompt"]
        self.x_sample = t["x_sample"]


def declare(nc, inputs):
    tensors, arrays = {}, {}
    consts, names = shape_constants()
    given = {n: np.ascontiguousarray(inputs[n]) for n in _INS}
    given.update(consts)
    for n, a in given.items():
        arrays[f"in_{n}"] = a
        tensors[n] = nc.dram_tensor(f"in_{n}", a.shape, mybir.dt.from_np(a.dtype), kind="ExternalInput").ap()
    for n, shape in _OUTS:
        tensors[f"out_{n}"] = nc.dram_tensor(f"out_{n}", shape, F32, kind="ExternalOutput").ap()
    tensors["scr_g"] = nc.dram_tensor("scr_g", (H, NT), F32).ap()
    tensors["scr_f"] = nc.dram_tensor("scr_f", (H, T), F32).ap()
    tensors["scr_o"] = nc.dram_tensor("scr_o", (2 * H, P, NT), F32).ap()
    return Dram(tensors), arrays, names


def kernel(**inputs):
    import concourse.bacc as _bacc
    from concourse.bass_utils import run_bass_kernel_spmd as _run

    nc = _bacc.Bacc("TRN2", target_bir_lowering=False, num_devices=1)
    io, arrays, names = declare(nc, inputs)
    build(nc, io, names)
    r = _run(nc, [arrays], core_ids=[0])
    return tuple(r.results[0][f"out_{n}"] for n, _ in _OUTS)
```
